# Optimizing a Trainium2 kernel written in Bass

```python
import jax, jax.numpy as jnp
from jax import lax
import numpy as np

D_MODEL = 1024
BATCH = 1
SEQ = 256
DEPTH = 2

N_MOD = 6
CONV_CH = 512
CONV_WIDTH = 31
N_HEADS = 8
HEAD_DIM = 64
ATTN_W = N_HEADS * HEAD_DIM
IDX_HEADS = 8
IDX_DIM = 32
TOPK_MAX = 256
Q_BLOCK = 128
ROPE_THETA = 10000.0
INDEX_SCALE = (IDX_DIM ** -0.5) * (IDX_HEADS ** -0.5)
N_BRANCH = 2
N_GROUPS = 4
EXPERTS_PER_GROUP = 8
N_EXPERTS = N_GROUPS * EXPERTS_PER_GROUP
TOP_K_INNER = 2
D_EXPERT = 256
EPS = 1e-6

IN_SIZES = (CONV_CH, CONV_CH, ATTN_W, HEAD_DIM, HEAD_DIM, IDX_HEADS * IDX_DIM, IDX_DIM, IDX_HEADS, N_BRANCH * D_MODEL)
N_IN = 2 * CONV_CH + ATTN_W + 2 * HEAD_DIM + IDX_HEADS * IDX_DIM + IDX_DIM + IDX_HEADS + N_BRANCH * D_MODEL

kernel_name = "hybrid_conformer_dsa_hmoe_adaln"

def rms_norm(x, g):
    x32 = x.astype(jnp.float32)
    y = x32 * lax.rsqrt(jnp.mean(x32 * x32, axis=-1, keepdims=True) + EPS)
    return (y * g.astype(jnp.float32)).astype(x.dtype)

def layer_norm(x, g, b):
    x32 = x.astype(jnp.float32)
    mu = jnp.mean(x32, axis=-1, keepdims=True)
    xc = x32 - mu
    y = xc * lax.rsqrt(jnp.mean(xc * xc, axis=-1, keepdims=True) + EPS)
    return (y * g.astype(jnp.float32) + b.astype(jnp.float32)).astype(x.dtype)

def rope_tables(length, dim):
    pos = jnp.arange(length, dtype=jnp.float32)
    inv = ROPE_THETA ** (-jnp.arange(0, dim, 2, dtype=jnp.float32) / dim)
    ang = pos[:, None] * inv[None, :]
    return jnp.cos(ang), jnp.sin(ang)

def apply_rope(x, cos, sin):
    L = x.shape[1]
    half = x.shape[-1] // 2
    shp = (1, L) + (1,) * (x.ndim - 3) + (half,)
    cos = cos.reshape(shp)
    sin = sin.reshape(shp)
    x1 = x[..., :half].astype(jnp.float32)
    x2 = x[..., half:].astype(jnp.float32)
    out = jnp.concatenate([x1 * cos - x2 * sin, x2 * cos + x1 * sin], axis=-1)
    return out.astype(x.dtype)

def conformer_conv(a, b, conv_w, conv_b, ln_g, ln_b, w_o, b_o):
    u = a * jax.nn.sigmoid(b)
    y = lax.conv_general_dilated(
        u, conv_w[:, None, :], window_strides=(1,),
        padding=[(CONV_WIDTH - 1, 0)],
        dimension_numbers=("NWC", "WIO", "NWC"),
        feature_group_count=CONV_CH) + conv_b
    y = jax.nn.silu(layer_norm(y, ln_g, ln_b))
    return y @ w_o + b_o

def dsa_attention(q, k, v, iq, ik, iw, w_o):
    B, L = q.shape[0], q.shape[1]
    k_sel = min(TOPK_MAX, L // 4)
    qb = min(Q_BLOCK, L)
    n_blocks = L // qb
    scale = HEAD_DIM ** -0.5
    key_pos = jnp.arange(L)

    def block(i):
        start = i * qb
        q_blk = lax.dynamic_slice_in_dim(q, start, qb, axis=1)
        iq_blk = lax.dynamic_slice_in_dim(iq, start, qb, axis=1)
        iw_blk = lax.dynamic_slice_in_dim(iw, start, qb, axis=1)
        t = start + jnp.arange(qb)
        rel = jax.nn.relu(jnp.einsum("bqhd,bsd->bqhs", iq_blk, ik).astype(jnp.float32))
        score = jnp.einsum("bqhs,bqh->bqs", rel, iw_blk.astype(jnp.float32)) * INDEX_SCALE
        causal = key_pos[None, :] <= t[:, None]
        score = jnp.where(causal[None], score, -jnp.inf)
        _, idx = lax.top_k(score, k_sel)
        valid = idx <= t[None, :, None]
        k_g = jax.vmap(lambda kk, ii: kk[ii])(k, idx)
        v_g = jax.vmap(lambda vv, ii: vv[ii])(v, idx)
        s = jnp.einsum("bqhd,bqkd->bqhk", q_blk, k_g).astype(jnp.float32) * scale
        s = jnp.where(valid[:, :, None, :], s, -jnp.inf)
        p = jax.nn.softmax(s, axis=-1).astype(v.dtype)
        return jnp.einsum("bqhk,bqkd->bqhd", p, v_g)

    out = lax.map(block, jnp.arange(n_blocks))
    out = jnp.transpose(out, (1, 0, 2, 3, 4)).reshape(B, L, ATTN_W)
    return out @ w_o

def hierarchical_moe(h, w_group, b_group, w_router, b_router, w_gate, w_up, w_down):
    B, L, D = h.shape
    t = h.reshape(B * L, D)
    T = B * L
    g_logits = (t @ w_group + b_group).astype(jnp.float32)
    g_prob = jax.nn.softmax(g_logits, axis=-1)
    g_sel = jnp.argmax(g_logits, axis=-1)
    p_group = jnp.take_along_axis(g_prob, g_sel[:, None], axis=-1)
    e_logits = (t @ w_router + b_router).astype(jnp.float32).reshape(T, N_GROUPS, EXPERTS_PER_GROUP)
    e_in = jnp.take_along_axis(e_logits, g_sel[:, None, None], axis=1)[:, 0]
    top_v, top_i = lax.top_k(e_in, TOP_K_INNER)
    p_in = jax.nn.softmax(top_v, axis=-1)
    expert_id = g_sel[:, None] * EXPERTS_PER_GROUP + top_i
    combine = jnp.sum(jax.nn.one_hot(expert_id, N_EXPERTS, dtype=jnp.float32)
                      * (p_group * p_in)[..., None], axis=1).astype(h.dtype)
    y = jnp.zeros_like(t)
    for e in range(N_EXPERTS):
        hid = jax.nn.silu(t @ w_gate[e]) * (t @ w_up[e])
        y = y + combine[:, e:e + 1] * (hid @ w_down[e])
    return y.reshape(B, L, D)

def setup_inputs(seed: int = 0) -> dict:
    key = jax.random.key(seed)
    ks = jax.random.split(key, 32)
    f32 = jnp.float32

    def nrm(k, shape, scale):
        return jax.random.normal(k, shape, f32) * scale

    D = D_MODEL
    return {
        "x": nrm(ks[0], (BATCH, SEQ, D), 1.0),
        "c": nrm(ks[1], (BATCH, D), 1.0),
        "w_ada": nrm(ks[2], (DEPTH, D, N_MOD * D), 0.5 * D ** -0.5),
        "b_ada": nrm(ks[3], (DEPTH, N_MOD * D), 0.02),
        "g_norm1": 1.0 + nrm(ks[4], (DEPTH, D), 0.02),
        "w_in": nrm(ks[5], (DEPTH, D, N_IN), D ** -0.5),
        "q_norm_g": 1.0 + nrm(ks[6], (DEPTH, HEAD_DIM), 0.02),
        "k_norm_g": 1.0 + nrm(ks[7], (DEPTH, HEAD_DIM), 0.02),
        "conv_w": nrm(ks[8], (DEPTH, CONV_WIDTH, CONV_CH), CONV_WIDTH ** -0.5),
        "conv_b": nrm(ks[9], (DEPTH, CONV_CH), 0.02),
        "conv_ln_g": 1.0 + nrm(ks[10], (DEPTH, CONV_CH), 0.02),
        "conv_ln_b": nrm(ks[11], (DEPTH, CONV_CH), 0.02),
        "w_conv_out": nrm(ks[12], (DEPTH, CONV_CH, D), CONV_CH ** -0.5),
        "b_conv_out": nrm(ks[13], (DEPTH, D), 0.02),
        "w_attn_out": nrm(ks[14], (DEPTH, ATTN_W, D), ATTN_W ** -0.5),
        "w_out": nrm(ks[15], (DEPTH, D, D), D ** -0.5),
        "g_norm2": 1.0 + nrm(ks[16], (DEPTH, D), 0.02),
        "w_group": nrm(ks[17], (DEPTH, D, N_GROUPS), D ** -0.5),
        "b_group": nrm(ks[18], (DEPTH, N_GROUPS), 0.01),
        "w_router": nrm(ks[19], (DEPTH, D, N_EXPERTS), D ** -0.5),
        "b_router": nrm(ks[20], (DEPTH, N_EXPERTS), 0.01),
        "w_gate": nrm(ks[21], (DEPTH, N_EXPERTS, D, D_EXPERT), D ** -0.5),
        "w_up": nrm(ks[22], (DEPTH, N_EXPERTS, D, D_EXPERT), D ** -0.5),
        "w_down": nrm(ks[23], (DEPTH, N_EXPERTS, D_EXPERT, D), D_EXPERT ** -0.5),
    }

def reference(x, c, w_ada, b_ada, g_norm1, w_in, q_norm_g, k_norm_g, conv_w, conv_b,
              conv_ln_g, conv_ln_b, w_conv_out, b_conv_out, w_attn_out, w_out, g_norm2,
              w_group, b_group, w_router, b_router, w_gate, w_up, w_down):
    B, L, D = x.shape
    cos_h, sin_h = rope_tables(L, HEAD_DIM)
    cos_i, sin_i = rope_tables(L, IDX_DIM)
    split_at = [int(s) for s in np.cumsum(IN_SIZES)[:-1]]
    for l in range(DEPTH):
        mod = jax.nn.silu(c) @ w_ada[l] + b_ada[l]
        shift1, scale1, gate1, shift2, scale2, gate2 = jnp.split(mod, N_MOD, axis=-1)

        h = rms_norm(x, g_norm1[l]) * (1.0 + scale1[:, None]) + shift1[:, None]
        u = h @ w_in[l]
        ca, cb, uq, uk, uv, uiq, uik, uiw, ug = jnp.split(u, split_at, axis=-1)

        y_conv = conformer_conv(ca, cb, conv_w[l], conv_b[l], conv_ln_g[l], conv_ln_b[l],
                                w_conv_out[l], b_conv_out[l])

        q = apply_rope(rms_norm(uq.reshape(B, L, N_HEADS, HEAD_DIM), q_norm_g[l]), cos_h, sin_h)
        k = apply_rope(rms_norm(uk, k_norm_g[l]), cos_h, sin_h)
        iq = apply_rope(uiq.reshape(B, L, IDX_HEADS, IDX_DIM), cos_i, sin_i)
        ik = apply_rope(uik, cos_i, sin_i)
        y_attn = dsa_attention(q, k, uv, iq, ik, uiw, w_attn_out[l])

        gates = jax.nn.sigmoid(ug.reshape(B, L, N_BRANCH, D))
        merged = (gates[:, :, 0] * y_conv + gates[:, :, 1] * y_attn) @ w_out[l]
        x = x + gate1[:, None] * merged

        h2 = rms_norm(x, g_norm2[l]) * (1.0 + scale2[:, None]) + shift2[:, None]
        x = x + gate2[:, None] * hierarchical_moe(h2, w_group[l], b_group[l], w_router[l],
                                                   b_router[l], w_gate[l], w_up[l], w_down[l])
    return x


_drawn_inputs = setup_inputs


def setup_inputs(seed=0):
    import zlib

    import numpy as np

    out = dict(_drawn_inputs(seed))
    spreads = {}
    factors = {'g_norm1': 5.105,
     'q_norm_g': 8.0,
     'k_norm_g': 8.0,
     'conv_b': 6.818,
     'conv_ln_g': 5.895,
     'conv_ln_b': 8.0,
     'b_conv_out': 8.0,
     'g_norm2': 3.167,
     'b_group': 8.0,
     'b_router': 6.659}
    for name, (base, spread) in spreads.items():
        noise = np.random.default_rng([zlib.crc32(name.encode()), seed]).standard_normal(out[name].shape)
        drawn = base * np.exp(spread * noise) if base else spread * noise
        out[name] = __import__('jax').numpy.asarray(drawn.astype(out[name].dtype))
    for name, factor in factors.items():
        out[name] = (out[name] * factor).astype(out[name].dtype)
    return out
```

```python
from collections import namedtuple
from contextlib import ExitStack

import concourse.bass as bass
from concourse import mybir

F32 = mybir.dt.float32
I32 = mybir.dt.int32
ALU = mybir.AluOpType
ACT = mybir.ActivationFunctionType
AX = mybir.AxisListType

P = 128
D = 1024
DC = D // P
T = 256
TC = T // P
DEPTH = 2
N_MOD = 6
CH = 512
CC = CH // P
TAPS = 31
HEADS = 8
HD = 64
IH = 8
ID = 32
ISCALE = (ID ** -0.5) * (IH ** -0.5)
TOPK = 64
GROUPS = 4
EPG = 8
NE = GROUPS * EPG
FE = 256
FC = FE // P
EPS = 1e-6
NEG = -1e30
TAKEN = -3e38

COL_Q = 2 * CH
COL_K = COL_Q + HEADS * HD
COL_G = COL_K + 2 * HD + IH * ID + ID + IH
N_KVI = COL_G - COL_K
N_IN = COL_G + 2 * D

BLK = 64
NBLK = T // BLK
PAIRS = 2 * T
PADDED = PAIRS + BLK

ITEM = 4096
NITEM = 6
EXP = 6144
NEXP = 4
RING = NITEM * ITEM
assert RING == NEXP * EXP

CONST = {}
_at = 0
for _name, _n in (("ident", P), ("ones", P), ("before", P), ("causal", TC * T), ("iota", PAIRS),
                  ("cos_h", TC * HD // 2), ("sin_h", TC * HD // 2), ("cos_i", TC * ID // 2),
                  ("sin_i", TC * ID // 2), ("falling", NE), ("eps", 1)):
    CONST[_name] = (_at, _at + _n)
    _at += _n
N_CONST = _at

ROWS = {}
_at = 0
for _name, _n in (("b_ada", N_MOD * DC), ("g_norm1", DC), ("g_norm2", DC), ("b_conv_out", DC),
                  ("conv_b", CC), ("conv_ln_g", CC), ("conv_ln_b", CC), ("c", DC)):
    ROWS[_name] = (_at, _at + _n)
    _at += _n
N_ROWS = _at
N_TAPROWS = TAPS * CC


class Place:

    def __init__(self):
        self.item = self.block = self.n = 0


def mixer_blocks(layer):
    if layer == 0:
        return [("M", 0, 0), ("KVI",), ("Q",), ("CA",), ("CB",), ("M", 0, 1), ("G", 0), ("M", 0, 2),
                ("G", 1), ("M", 1, 0), ("G", 2), ("M", 1, 1), ("M", 1, 2), ("G", 3)]
    return [("KVI",), ("Q",), ("CA",), ("CB",), ("G", 0), ("G", 1), ("G", 2), ("G", 3)]


def mixer_items(layer):
    items = []
    for b in mixer_blocks(layer):
        if b[0] == "M":
            items += [("ada", b[1], 4 * b[2] + i) for i in range(4)]
        else:
            items.append(("in", b))
    return items + [("attn_out",), ("conv_out",), ("out", 0), ("out", 1)]


def items_at_block_end(layer):
    ends, n = [], 0
    for b in mixer_blocks(layer):
        n += 4 if b[0] == "M" else 1
        ends.append(n)
    return ends


N_SMALL = DEPTH * (len(ROWS) + 1 + 2 + 2 + 2)


def trunk_kernel(nc, w, constants, out):
    with ExitStack() as ctx:
        def sb(name, shape, dt=F32):
            return ctx.enter_context(nc.sbuf_tensor(name, shape, dt))

        const = sb("const", [P, N_CONST])
        ring = sb("ring", [P, RING])
        xT = sb("xT", [P, DC, T])
        hT = sb("hT", [P, DC, T])
        vec = sb("vec", [P, DEPTH, N_ROWS])
        taps = sb("taps", [P, DEPTH, TAPS, CC])
        silu_c = sb("silu_c", [P, DC])
        mod = sb("mod", [P, DEPTH, N_MOD * DC])
        gain = sb("gain", [P, DEPTH, 2, DC])
        qk_gain = sb("qk_gain", [P, DEPTH, HEADS + 1, HD])
        w_route = sb("w_route", [P, DEPTH, DC, GROUPS + NE])
        b_route = sb("b_route", [P, DEPTH, GROUPS + NE])
        std = sb("std", [P, T])
        rstd = sb("rstd", [P, T])

        MIX = {}
        EX = {}

        def lay(table, names, at=0):
            for name, n in names:
                table[name] = (at, at + n)
                at += n
            return at

        end_mix = lay(MIX, (("kvi", TC * N_KVI), ("qk", TC * (HEADS + 1) * HD), ("tmp", TC * (HEADS + 1) * HD),
                            ("qr", TC * (HEADS + 2) * HD), ("ir", TC * (IH + 4) * ID), ("turned", 8 * T),
                            ("scores", HEADS * T), ("probsT", HEADS * T), ("gates", 2 * DC * T),
                            ("ca", CC * T), ("cb", CC * T), ("pad", CC * (T + TAPS - 1)),
                            ("drop", TC * T), ("stat", 160)))
        end_ex = lay(EX, (("hn", TC * D), ("onehot", TC * PAIRS), ("weighted", TC * PAIRS), ("spread", 4 * T),
                          ("sorted", DC * PADDED), ("made", DC * PADDED), ("xe", 2 * DC * BLK),
                          ("act", 2 * FC * BLK), ("hid", 2 * FC * BLK), ("route", 700)))
        arena = sb("arena", [P, max(end_mix, end_ex)])
        offs = sb("offs", [1, DEPTH, NBLK, NE], I32)
        flag = sb("flag", [1, DEPTH], I32)

        def mix(name):
            return arena[:, MIX[name][0]:MIX[name][1]]

        def ex(name):
            return arena[:, EX[name][0]:EX[name][1]]

        kvi = mix("kvi").rearrange("p (t n) -> p t n", t=TC)
        qk = mix("qk").rearrange("p (t h d) -> p t h d", t=TC, d=HD)
        tmp = mix("tmp").rearrange("p (t h d) -> p t h d", t=TC, d=HD)
        qr = mix("qr").rearrange("p (t h d) -> p t h d", t=TC, d=HD)
        ir = mix("ir").rearrange("p (t h d) -> p t h d", t=TC, d=ID)
        turned = mix("turned").rearrange("p (n t) -> p n t", t=T)
        IQT, IKT, KT, QT = 0, 2, 3, 4
        scores = mix("scores").rearrange("p (h s) -> p h s", h=HEADS)
        probsT = mix("probsT").rearrange("p (h t) -> p h t", h=HEADS)
        merged = mix("scores").rearrange("p (c t) -> p c t", c=DC)
        attn = arena[:, MIX["qr"][0]:MIX["qr"][0] + TC * HEADS * HD].rearrange(
            "p (t h d) -> p t h d", t=TC, d=HD)
        attnT = arena[:, MIX["qk"][0]:MIX["qk"][0] + 4 * T].rearrange("p (c t) -> p c t", t=T)
        gates = mix("gates").rearrange("p (b c t) -> p b c t", b=2, c=DC)
        ca = mix("ca").rearrange("p (c t) -> p c t", c=CC)
        cb = mix("cb").rearrange("p (c t) -> p c t", c=CC)
        pad = mix("pad").rearrange("p (c t) -> p c t", c=CC)
        drop = mix("drop").rearrange("p (t s) -> p t s", t=TC)
        iscore = arena[:, MIX["tmp"][0]:MIX["tmp"][0] + TC * T].rearrange("p (t s) -> p t s", t=TC)
        scores0 = mix("cb").rearrange("p (h s) -> p h s", h=HEADS)
        square = mix("probsT").rearrange("p (c t) -> p c t", c=DC)
        st = mix("stat")
        sumsq, rms = st[:, 0:18], st[:, 18:36]
        top8 = st[:, 36:44]
        rowmax, rowsum, rowinv = st[:, 44:60], st[:, 60:76], st[:, 76:92]

        hn = ex("hn").rearrange("p (t d) -> p t d", t=TC)
        onehot = ex("onehot").rearrange("p (t s) -> p t s", t=TC)
        weighted = ex("weighted").rearrange("p (t s) -> p t s", t=TC)
        spread = ex("spread").rearrange("p (j t) -> p j t", t=T)
        sorted_x = ex("sorted").rearrange("p (c s) -> p c s", c=DC)
        made = ex("made").rearrange("p (c s) -> p c s", c=DC)
        made_n = arena[:, 0:4 * D].rearrange("p (j d) -> p j d", d=D)
        assert 4 * D <= EX["spread"][0]
        square2 = made[:, :, 0:T]
        xe = ex("xe").rearrange("p (b c s) -> p b c s", b=2, c=DC)
        act_g = ex("act").rearrange("p (b n) -> p b n", b=2)
        hid = ex("hid").rearrange("p (b f s) -> p b f s", b=2, f=FC)
        rt = ex("route")
        small = {}
        lay(small, (("member", TC * NE), ("logits", TC * (GROUPS + NE)), ("g_max", TC), ("g_shift", TC * GROUPS),
                    ("g_exp", TC * GROUPS), ("g_one", TC * GROUPS), ("best", TC), ("e_in", TC * NE), ("top_a", TC),
                    ("top_b", TC), ("hot_a", TC * NE), ("hot_b", TC * NE), ("gap", TC), ("gap_exp", TC),
                    ("count", NE), ("start", NE), ("place", TC * NE), ("slot_a", TC), ("slot_b", TC),
                    ("weight_a", TC), ("weight_b", TC)))

        def small_tile(name, per_token=False):
            t = rt[:, small[name][0]:small[name][1]]
            return t.rearrange("p (t e) -> p t e", t=TC) if per_token else t

        member, logits, e_in = small_tile("member", True), small_tile("logits", True), small_tile("e_in", True)
        hot_a, hot_b, place = small_tile("hot_a", True), small_tile("hot_b", True), small_tile("place", True)
        g_shift, g_exp, g_one = small_tile("g_shift"), small_tile("g_exp"), small_tile("g_one", True)
        g_shift3, g_exp3 = small_tile("g_shift", True), small_tile("g_exp", True)
        g_max, best, top_a, top_b = small_tile("g_max"), small_tile("best"), small_tile("top_a"), small_tile("top_b")
        gap, gap_exp, count_sb, start = small_tile("gap"), small_tile("gap_exp"), small_tile("count"), small_tile("start")
        slot_a, slot_b = small_tile("slot_a"), small_tile("slot_b")
        weight_a, weight_b = small_tile("weight_a"), small_tile("weight_b")
        scratch = made[:, 0:2, 0:PAIRS]
        stage = arena[0:N_ROWS, EX["sorted"][0]:EX["sorted"][0] + DEPTH * P].rearrange("r (l q) -> r l q", l=DEPTH)
        stage_taps = arena[0:N_TAPROWS, EX["sorted"][0] + 256:EX["sorted"][0] + 512].rearrange(
            "r (l q) -> r l q", l=DEPTH)
        x_nat = ex("made")[:, 0:TC * D].rearrange("p (t d) -> p t d", t=TC)
        y_nat = hT[:, :, :].rearrange("p c t -> p (c t)").rearrange("p (t d) -> p t d", t=TC)

        def k(name):
            return const[:, CONST[name][0]:CONST[name][1]]

        ident, ones, before, iota = k("ident"), k("ones"), k("before"), k("iota")
        causal = k("causal").rearrange("p (t s) -> p t s", t=TC)
        cos_h = k("cos_h").rearrange("p (t d) -> p t d", t=TC)
        sin_h = k("sin_h").rearrange("p (t d) -> p t d", t=TC)
        cos_i = k("cos_i").rearrange("p (t d) -> p t d", t=TC)
        sin_i = k("sin_i").rearrange("p (t d) -> p t d", t=TC)
        falling, eps = k("falling"), k("eps")

        def row(layer, name):
            return vec[:, layer, ROWS[name][0]:ROWS[name][1]]

        SHIFT1, SCALE1, GATE1, SHIFT2, SCALE2, GATE2 = range(6)

        def modulation(layer, which):
            return mod[:, layer, which * DC:(which + 1) * DC]

        ps = ctx.enter_context(nc.psum_tensor("ps", [P, 8, 512], F32))

        def item_slot(i):
            return ring[:, (i % NITEM) * ITEM:(i % NITEM + 1) * ITEM]

        def expert_gate(slot):
            return ring[:, slot * EXP:slot * EXP + 2048].rearrange("p (c n) -> p c n", c=DC)

        def expert_up(slot):
            return ring[:, slot * EXP + 2048:slot * EXP + 4096].rearrange("p (c n) -> p c n", c=DC)

        def expert_down(slot):
            return ring[:, slot * EXP + 4096:slot * EXP + 6144].rearrange("p (f n) -> p f n", f=FC)

        def sem(name):
            return ctx.enter_context(nc.semaphore(name))

        const_in, x_in, small_in = sem("const_in"), sem("x_in"), sem("small_in")
        x_turned, vec_turned, vec_kept, silu_c_ready = sem("x_turned"), sem("vec_turned"), sem("vec_kept"), sem("silu_c_ready")
        dve_step = sem("dve_step")
        y_turned, y_kept, y_out = sem("y_turned"), sem("y_kept"), sem("y_out")
        EACH_LAYER = dict(
            sq_ready=2, ssq_ready=2, std_ready=2, scaled=2 * DC, h_ready=2 * DC, index_rotated=1, q_rms_ready=1,
            q_std_ready=1, q_rotated=1, turn_done=4, turn_kept=4, index_done=2, index_kept=2, index_read=1,
            att_done=3, att_masked=3, att_max=3, att_exp=2 * HEADS, prob_turned=6, prob_kept=6, pv_done=2,
            attn_ready=2, attn_turned=1, attn_kept=1, conv_ready=1, mean_ready=1, centred=1, ln_sq_ready=1,
            var_ready=1, ln_std_ready=1, ln_ready=1, conv_act_ready=CC, ya_done=3, ya_used=4, yc_done=3,
            merged_ready=4, out_done=2, pad_zero=1, logits_done=1, group_shifted=1, group_exp=1, gap_ready=1,
            gap_exp=1, member_ready=1, rank_done=1, hn_turned=4, hn_kept=4, onehot_ready=TC, offs_ready=1,
            sorted_done=DC, sorted_kept=DC, weighted_ready=TC, spread_turned=1, spread_kept=1, tail_zero=1,
            expert_used=NE, experts_done=1, made_turned=8, made_kept=8, final_done=4)
        OWN = ("item_used", "x_ready", "block_kept", "xe_ready", "gu_done", "act_ready", "hid_ready", "y_stored",
               "xe_slow", "gu_slow", "act_slow", "hid_slow", "down_slow", "y_slow")

        class Signal:

            def __init__(self, semaphore, base):
                self.sem, self.base = semaphore, base

            def at(self, n):
                return self.sem, n + self.base if self.base else n

        shared = {name: sem(name) for name in EACH_LAYER}
        Signals = namedtuple("Signals", (*EACH_LAYER, *OWN))
        sig = [Signals(*(Signal(shared[n], l * each) for n, each in EACH_LAYER.items()),
                       *(Signal(sem(f"{n}_{l}"), 0) for n in OWN)) for l in range(DEPTH)]
        item_in = [[sem(f"item_in_{l}_{s}") for s in range(NITEM)] for l in range(DEPTH)]
        expert_in = [[sem(f"expert_in_{l}_{s}") for s in range(NEXP)] for l in range(DEPTH)]

        block = ctx.enter_context(nc.Block())

        @block.sync
        def _(sp):
            for l in range(DEPTH):
                s = sig[l]
                items = mixer_items(l)
                for i, item in enumerate(items):
                    if i >= NITEM:
                        sp.wait_ge(*s.item_used.at(i - NITEM + 1))
                    elif l > 0:
                        last = (i * ITEM + ITEM - 1) // EXP
                        sp.wait_ge(*sig[l - 1].expert_used.at(NE - NEXP + last + 1))
                    dst = item_slot(i)
                    if item[0] == "ada":
                        _, ml, n = item
                        src = w["w_ada"][ml, :, n * 512:(n + 1) * 512].rearrange("(c p) n -> p c n", p=P)
                        dst = dst.rearrange("p (c n) -> p c n", c=DC)
                    elif item[0] == "in":
                        b = item[1]
                        c0, n = {"KVI": (COL_K, N_KVI), "Q": (COL_Q, 512), "CA": (0, 512), "CB": (CH, 512),
                                 "G": (COL_G + 512 * b[-1] if b[0] == "G" else 0, 512)}[b[0]]
                        src = w["w_in"][l, :, c0:c0 + n].rearrange("(c p) n -> p c n", p=P)
                        dst = dst[:, 0:DC * n].rearrange("p (c n) -> p c n", c=DC)
                    elif item[0] == "out":
                        src = w["w_out"][l, :, item[1] * 512:(item[1] + 1) * 512].rearrange("(c p) n -> p c n", p=P)
                        dst = dst.rearrange("p (c n) -> p c n", c=DC)
                    else:
                        src = w["w_" + item[0]][l].rearrange("(c p) n -> p c n", p=P)
                        dst = dst.rearrange("p (c n) -> p c n", c=4)
                    sp.dma_start(dst, src).then_inc(item_in[l][i % NITEM], 16)

                def load_expert(slot, e):
                    def src(name, pattern, **kw):
                        return w[name][l, bass.ds(e, 1)].rearrange(pattern, **kw)
                    sp.dma_start(expert_gate(slot).rearrange("p c n -> p (c n)"),
                                 src("w_gate", "a (p c) n -> p (a c n)", c=DC)).then_inc(expert_in[l][slot], 16)
                    sp.dma_start(expert_up(slot).rearrange("p c n -> p (c n)"),
                                 src("w_up", "a (p c) n -> p (a c n)", c=DC)).then_inc(expert_in[l][slot], 16)
                    sp.dma_start(expert_down(slot),
                                 src("w_down", "a (f p) n -> p (a f) n", p=P)).then_inc(expert_in[l][slot], 16)

                for slot in range(NEXP):
                    under = [i for i in range(len(items) - NITEM, len(items))
                             if (i % NITEM) * ITEM < (slot + 1) * EXP and (i % NITEM + 1) * ITEM > slot * EXP]
                    sp.wait_ge(*s.item_used.at(max(under) + 1))
                    load_expert(slot, slot)
                with sp.Fori(1, NE // NEXP) as r:
                    for slot in range(NEXP):
                        sp.wait_ge(*s.expert_used.at((r - 1) * NEXP + slot + 1))
                        load_expert(slot, r * NEXP + slot)
            for t in range(TC):
                sp.wait_ge(y_kept, 2 * t + 2)
                sp.dma_start(out[0, t * P:(t + 1) * P, :], y_nat[:, t, :]).then_inc(y_out, 16)
            sp.wait_ge(y_out, 16 * TC)

        @block.tensor
        def _(pe):
            mm = nc.tensor.matmul

            def turn(dst, src, n_rows=P):
                return nc.tensor.transpose(dst, src, ident[0:n_rows, 0:n_rows])

            pe.wait_ge(const_in, 16)
            pe.wait_ge(small_in, 16 * N_SMALL)
            for l in range(DEPTH):
                turn(ps[:, 0, l * P:l * P + N_ROWS], stage[:, l, :], N_ROWS)
                last = turn(ps[:, 0, 256 + l * P:256 + l * P + N_TAPROWS], stage_taps[:, l, :], N_TAPROWS)
            last.then_inc(vec_turned, 1)
            pe.wait_ge(x_in, 16)
            for c in range(DC):
                for t in range(TC):
                    last = turn(ps[:, 4 + c // 2, (c % 2) * T + t * P:(c % 2) * T + (t + 1) * P],
                                x_nat[:, t, c * P:(c + 1) * P])
            last.then_inc(x_turned, 1)

            for l in range(DEPTH):
                s = sig[l]
                count = Place()

                def item(c):
                    i = count.item
                    pe.wait_ge(item_in[l][i % NITEM], 16 * (i // NITEM + 1))
                    count.item += 1
                    return item_slot(i).rearrange("p (c n) -> p c n", c=c)

                def run_block(b):
                    j = count.block
                    count.block += 1
                    bank = 2 * (j % 2)
                    if j >= 2:
                        pe.wait_ge(*s.block_kept.at(j - 1))
                    if b[0] == "M":
                        for i in range(4):
                            wt = item(DC)
                            for n in range(4):
                                col = 4 * i + n
                                for c in range(DC):
                                    last = mm(ps[:, bank, col:col + 1], wt[:, c, n * P:(n + 1) * P],
                                              silu_c[:, c:c + 1], start=c == 0, stop=c == DC - 1)
                            last.then_inc(s.item_used.sem, 1)
                    elif b[0] in ("KVI", "Q"):
                        n = N_KVI if b[0] == "KVI" else 512
                        pe.wait_ge(item_in[l][count.item % NITEM], 16 * (count.item // NITEM + 1))
                        wt = item_slot(count.item)[:, 0:DC * n].rearrange("p (c n) -> p c n", c=DC)
                        count.item += 1
                        for t in range(TC):
                            for c in range(DC):
                                if t == 0:
                                    pe.wait_ge(*s.h_ready.at(c + 1))
                                last = mm(ps[:, bank + t, 0:n], hT[:, c, t * P:(t + 1) * P], wt[:, c, :],
                                          start=c == 0, stop=c == DC - 1)
                        last.then_inc(s.item_used.sem, 1)
                    else:
                        wt = item(DC)
                        for n in range(4):
                            for c in range(DC):
                                last = mm(ps[:, bank + n // 2, (n % 2) * T:(n % 2 + 1) * T],
                                          wt[:, c, n * P:(n + 1) * P], hT[:, c, :], start=c == 0, stop=c == DC - 1)
                        last.then_inc(s.item_used.sem, 1)

                def sum_over_channels(dst, src, chunks):
                    for c in range(chunks):
                        last = mm(dst, ones, src[:, c, :], start=c == 0, stop=c == chunks - 1)
                    return last

                def index_unit(t):
                    n = (t + 1) * P
                    for h in range(IH):
                        q = slice(ID * (h % 4), ID * (h % 4 + 1))
                        last = mm(ps[:, 4 + h % 4, (h // 4) * n:(h // 4 + 1) * n],
                                  turned[q, IQT + h // 4, t * P:(t + 1) * P], turned[q, IKT, 0:n],
                                  start=True, stop=True)
                    last.then_inc(s.index_done.sem, 1)

                def attention_unit(t, half):
                    n = (t + 1) * P
                    for h in (range(HEADS) if t == 0 else range(4 * half, 4 * half + 4)):
                        q = slice(HD * (h % 2), HD * (h % 2 + 1))
                        at = h // 2 if t == 0 else h // 2 % 2
                        last = mm(ps[:, 4 + h % 2, at * n:(at + 1) * n],
                                  turned[q, QT + h // 2, t * P:(t + 1) * P], turned[q, KT, 0:n],
                                  start=True, stop=True)
                    last.then_inc(s.att_done.sem, 1)

                blocks = mixer_blocks(l)
                if blocks[0][0] == "M":
                    pe.wait_ge(silu_c_ready, 1)
                    run_block(blocks.pop(0))
                pe.wait_ge(*s.sq_ready.at(1))
                sum_over_channels(ps[:, 7, 0:T], square, DC).then_inc(s.ssq_ready.sem, 1)

                run_block(blocks.pop(0))
                run_block(blocks.pop(0))
                run_block(blocks.pop(0))
                pe.wait_ge(*s.index_rotated.at(1))
                pe.wait_ge(*s.q_rotated.at(1))
                groups = ((("i", 0), ("i", 1)), (("i", 2), ("q", 4)), (("q", 0), ("q", 1)), (("q", 2), ("q", 3)))
                for g, group in enumerate(groups):
                    if g == 3:
                        pe.wait_ge(*s.turn_kept.at(1))
                    for half, (kind, n) in enumerate(group):
                        for t in range(TC):
                            src = ir[:, t, 4 * n:4 * n + 4, :] if kind == "i" else qr[:, t, 2 * n:2 * n + 2, :]
                            o = half * T + t * P
                            last = turn(ps[:, 4 + g % 3, o:o + P], src.rearrange("p h d -> p (h d)"))
                    last.then_inc(s.turn_done.sem, 1)
                pe.wait_ge(*s.turn_kept.at(4))
                index_unit(0)
                run_block(blocks.pop(0))
                pe.wait_ge(*s.index_kept.at(1))
                index_unit(1)
                run_block(blocks.pop(0))
                run_block(blocks.pop(0))
                pe.wait_ge(*s.index_kept.at(2))
                attention_unit(0, 0)
                if l == 0:
                    run_block(blocks.pop(0))
                pe.wait_ge(*s.att_masked.at(1))
                attention_unit(1, 0)
                run_block(blocks.pop(0))
                pe.wait_ge(*s.att_masked.at(2))
                attention_unit(1, 1)
                if l == 0:
                    run_block(blocks.pop(0))

                pe.wait_ge(*s.att_exp.at(8))
                for g in range(2):
                    for i in range(4):
                        last = turn(ps[:, 6 + g, i * P:(i + 1) * P], scores0[:, 4 * g + i, :])
                    last.then_inc(s.prob_turned.sem, 1)
                pe.wait_ge(*s.prob_kept.at(2))
                pe.wait_ge(*s.att_masked.at(3))
                for h in range(HEADS):
                    last = mm(ps[:, 4, h * HD:(h + 1) * HD], probsT[:, h, 0:P], kvi[:, 0, HD:2 * HD],
                              start=True, stop=True)
                last.then_inc(s.pv_done.sem, 1)
                pe.wait_ge(*s.att_exp.at(16))
                for g in range(4):
                    if g >= 2:
                        pe.wait_ge(*s.prob_kept.at(2 + g - 1))
                    for i in range(2):
                        for sc in range(TC):
                            last = turn(ps[:, 6 + g % 2, (2 * i + sc) * P:(2 * i + sc + 1) * P],
                                        scores[:, 2 * g + i, sc * P:(sc + 1) * P])
                    last.then_inc(s.prob_turned.sem, 1)
                pe.wait_ge(*s.prob_kept.at(6))
                for h in range(HEADS):
                    for sc in range(TC):
                        last = mm(ps[:, 5, h * HD:(h + 1) * HD], probsT[:, h, sc * P:(sc + 1) * P],
                                  kvi[:, sc, HD:2 * HD], start=sc == 0, stop=sc == TC - 1)
                last.then_inc(s.pv_done.sem, 1)
                while blocks:
                    run_block(blocks.pop(0))

                pe.wait_ge(*s.attn_ready.at(2))
                for c in range(4):
                    for t in range(TC):
                        last = turn(ps[:, 6 + c // 2, (c % 2) * T + t * P:(c % 2) * T + (t + 1) * P],
                                    attn[:, t, 2 * c:2 * c + 2, :].rearrange("p h d -> p (h d)"))
                last.then_inc(s.attn_turned.sem, 1)
                pe.wait_ge(*s.attn_kept.at(1))
                pe.wait_ge(*s.block_kept.at(count.block))
                wt = item(4)
                for n in range(DC):
                    for c in range(4):
                        last = mm(ps[:, n // 2, (n % 2) * T:(n % 2 + 1) * T], wt[:, c, n * P:(n + 1) * P],
                                  attnT[:, c, :], start=c == 0, stop=c == 3)
                    if n % 2 and n < DC - 1:
                        last.then_inc(s.ya_done.sem, 1)
                last.then_inc(s.item_used.sem, 1)

                pe.wait_ge(*s.conv_ready.at(1))
                sum_over_channels(ps[:, 7, 0:T], ca, CC).then_inc(s.mean_ready.sem, 1)
                pe.wait_ge(*s.ln_sq_ready.at(1))
                sum_over_channels(ps[:, 7, T:2 * T], ca, CC).then_inc(s.var_ready.sem, 1)
                pe.wait_ge(*s.conv_act_ready.at(CC))
                wt = item(4)
                for n in range(DC):
                    for c in range(4):
                        last = mm(ps[:, 4 + n // 2, (n % 2) * T:(n % 2 + 1) * T], wt[:, c, n * P:(n + 1) * P],
                                  ca[:, c, :], start=c == 0, stop=c == 3)
                    if n % 2 and n < DC - 1:
                        last.then_inc(s.yc_done.sem, 1)
                last.then_inc(s.item_used.sem, 1)

                pe.wait_ge(*s.ya_used.at(4))
                for n in range(DC):
                    if n % 4 == 0:
                        wt = item(DC)
                    for c in range(DC):
                        if n == 0:
                            pe.wait_ge(*s.merged_ready.at(c // 2 + 1))
                        last = mm(ps[:, n // 2, (n % 2) * T:(n % 2 + 1) * T],
                                  wt[:, c, (n % 4) * P:(n % 4 + 1) * P], merged[:, c, :],
                                  start=c == 0, stop=c == DC - 1)
                    if n % 4 == 3:
                        last.then_inc(s.item_used.sem, 1)
                    elif n % 2:
                        last.then_inc(s.out_done.sem, 1)

                pe.wait_ge(*s.sq_ready.at(2))
                sum_over_channels(ps[:, 7, 0:T], square2, DC).then_inc(s.ssq_ready.sem, 1)
                pe.wait_ge(*s.h_ready.at(2 * DC))
                for t in range(TC):
                    for c in range(DC):
                        last = mm(ps[:, 4, t * (GROUPS + NE):(t + 1) * (GROUPS + NE)], hT[:, c, t * P:(t + 1) * P],
                                  w_route[:, l, c, :], start=c == 0, stop=c == DC - 1)
                last.then_inc(s.logits_done.sem, 1)
                for g in range(4):
                    t, half = g // 2, g % 2
                    for i in range(4):
                        last = turn(ps[:, g, i * P:(i + 1) * P], hT[:, 4 * half + i, t * P:(t + 1) * P])
                    last.then_inc(s.hn_turned.sem, 1)
                pe.wait_ge(*s.member_ready.at(1))
                mm(ps[:, 5, 0:NE], before, member[:, 0, :], start=True, stop=True)
                mm(ps[:, 5, NE:2 * NE], ones, member[:, 0, :], start=True, stop=False)
                mm(ps[:, 5, NE:2 * NE], before, member[:, 1, :], start=False, stop=True)
                mm(ps[:, 5, 2 * NE:3 * NE], ones, member[:, 0, :], start=True, stop=False)
                mm(ps[:, 5, 2 * NE:3 * NE], ones, member[:, 1, :], start=False, stop=True).then_inc(s.rank_done.sem, 1)
                pe.wait_ge(*s.hn_kept.at(4))
                pe.wait_ge(*s.onehot_ready.at(TC))
                for c in range(DC):
                    if c >= 4:
                        pe.wait_ge(*s.sorted_kept.at(c - 3))
                    for t in range(TC):
                        last = mm(ps[:, c % 4, :], hn[:, t, c:D:DC], onehot[:, t, :], start=t == 0, stop=t == TC - 1)
                    last.then_inc(s.sorted_done.sem, 1)
                pe.wait_ge(*s.weighted_ready.at(TC))
                for j in range(4):
                    for t in range(TC):
                        last = turn(ps[:, 6 + j // 2, (j % 2) * T + t * P:(j % 2) * T + (t + 1) * P],
                                    weighted[:, t, j * P:(j + 1) * P])
                last.then_inc(s.spread_turned.sem, 1)

                def gate_up(slot, x_block, bank):
                    for half, wt in enumerate((expert_gate(slot), expert_up(slot))):
                        for f in range(FC):
                            o = (half * FC + f) * BLK
                            for c in range(DC):
                                last = mm(ps[:, bank, o:o + BLK], wt[:, c, f * P:(f + 1) * P], x_block[:, c, :],
                                          start=c == 0, stop=c == DC - 1)
                    return last

                def down(slot, h_block, bank):
                    wt = expert_down(slot)
                    for c in range(DC):
                        for f in range(FC):
                            last = mm(ps[:, bank, c * BLK:(c + 1) * BLK], wt[:, f, c * P:(c + 1) * P],
                                      h_block[:, f, :], start=f == 0, stop=f == FC - 1)
                    return last

                pe.wait_ge(*s.sorted_kept.at(DC))
                pe.wait_ge(*s.offs_ready.at(1))
                big = pe.value_load(flag[0:1, l:l + 1], min_val=0, max_val=1)
                with pe.If(big == 0):
                    def step_up(e, r, j):
                        pe.wait_ge(expert_in[l][j % NEXP], (r + j // NEXP) * 48 + 48)
                        pe.wait_ge(*s.xe_ready.at(e + 1))
                        if not isinstance(e, int) or e >= 2:
                            pe.wait_ge(*s.hid_ready.at(e - 1))
                        gate_up(j % NEXP, xe[:, j % 2], j % 2).then_inc(s.gu_done.sem, 1)

                    def step_down(e, j):
                        pe.wait_ge(*s.hid_ready.at(e + 1))
                        if not isinstance(e, int) or e >= 2:
                            pe.wait_ge(*s.y_stored.at(e - 1))
                        down(j, hid[:, j % 2], 2 + j % 2).then_inc(s.expert_used.sem, 1)

                    step_up(0, 0, 0)
                    for j in range(NEXP):
                        step_up(j + 1, 0, j + 1)
                        step_down(j, j)
                    with pe.Fori(1, NE // NEXP - 1) as r:
                        for j in range(NEXP):
                            step_up(r * NEXP + j + 1, r, j + 1)
                            step_down(r * NEXP + j, j)
                    for j in range(NEXP):
                        if j < NEXP - 1:
                            step_up(NE - NEXP + j + 1, NE // NEXP - 1, j + 1)
                        step_down(NE - NEXP + j, j)
                with pe.Else():
                    pe.sem_inc(s.gu_slow.sem, 1)
                    with pe.Fori(0, NE // NEXP) as r:
                        for j in range(NEXP):
                            def run_slow(n, used):
                                pe.wait_ge(expert_in[l][j], r * 48 + 48)
                                pe.wait_ge(*s.xe_slow.at(n + 1))
                                gate_up(j, xe[:, 0], 0).then_inc(s.gu_slow.sem, 1)
                                pe.wait_ge(*s.hid_slow.at(n + 1))
                                pe.wait_ge(*s.y_slow.at(n + 1))
                                down(j, hid[:, 0], 2).then_inc(used.sem, 1)

                            with pe.Fori(0, NBLK - 1) as b:
                                run_slow((r * NEXP + j) * NBLK + b, s.down_slow)
                            run_slow((r * NEXP + j) * NBLK + NBLK - 1, s.expert_used)

                pe.wait_ge(*s.experts_done.at(1))
                pe.wait_ge(*s.spread_kept.at(1))
                for g in range(8):
                    j, half = g // 2, g % 2
                    if g >= 4:
                        pe.wait_ge(*s.made_kept.at(g - 3))
                    for i in range(4):
                        last = turn(ps[:, 4 + g % 4, i * P:(i + 1) * P], made[:, 4 * half + i, j * P:(j + 1) * P])
                    last.then_inc(s.made_turned.sem, 1)
                for c in range(DC):
                    for j in range(4):
                        if c == 0:
                            pe.wait_ge(*s.made_kept.at(2 * j + 2))
                        last = mm(ps[:, c // 2, (c % 2) * T:(c % 2 + 1) * T], made_n[:, j, c * P:(c + 1) * P],
                                  spread[:, j, :], start=j == 0, stop=j == 3)
                    if c % 2:
                        last.then_inc(s.final_done.sem, 1)

            pe.wait_ge(*sig[DEPTH - 1].x_ready.at(3))
            for g in range(4):
                t, half = g // 2, g % 2
                for i in range(4):
                    last = turn(ps[:, 4 + g, i * P:(i + 1) * P], xT[:, 4 * half + i, t * P:(t + 1) * P])
                last.then_inc(y_turned, 1)

        @block.gpsimd
        def _(pool):
            for l in range(DEPTH):
                for name, (r0, r1) in ROWS.items():
                    src = w[name][0] if name == "c" else w[name][l]
                    pool.dma_start(stage[r0:r1, l, :], src.rearrange("(r q) -> r q", q=P)).then_inc(small_in, 16)
                pool.dma_start(stage_taps[:, l, :],
                               w["conv_w"][l].rearrange("k (c q) -> (k c) q", q=P)).then_inc(small_in, 16)
                pool.dma_start(qk_gain[:, l, 0:HEADS, :],
                               w["q_norm_g"][l:l + 1, :].unsqueeze(1).to_broadcast([P, HEADS, HD])).then_inc(small_in, 16)
                pool.dma_start(qk_gain[:, l, HEADS, :], w["k_norm_g"][l:l + 1, :].to_broadcast([P, HD])).then_inc(small_in, 16)
                pool.dma_start(w_route[:, l, :, 0:GROUPS],
                               w["w_group"][l].rearrange("(c p) n -> p c n", p=P)).then_inc(small_in, 16)
                pool.dma_start(w_route[:, l, :, GROUPS:],
                               w["w_router"][l].rearrange("(c p) n -> p c n", p=P)).then_inc(small_in, 16)
                pool.dma_start(b_route[:, l, 0:GROUPS], w["b_group"][l:l + 1, :].to_broadcast([P, GROUPS])).then_inc(small_in, 16)
                pool.dma_start(b_route[:, l, GROUPS:], w["b_router"][l:l + 1, :].to_broadcast([P, NE])).then_inc(small_in, 16)
            for l in range(DEPTH):
                s = sig[l]
                pool.wait_ge(*s.x_ready.at(1))
                pool.memset(pad[:, :, 0:TAPS - 1], 0.0).then_inc(s.pad_zero.sem, 1)
                pool.wait_ge(*s.x_ready.at(2))
                pool.memset(sorted_x[:, :, PAIRS:PADDED], 0.0).then_inc(s.tail_zero.sem, 1)
                pool.wait_ge(*s.tail_zero.at(1))
                pool.wait_ge(*s.offs_ready.at(1))
                pool.wait_ge(*s.sorted_kept.at(DC))
                big = pool.value_load(flag[0:1, l:l + 1], min_val=0, max_val=1)
                starts = offs[0:1, l].rearrange("q b e -> q (b e)")

                def gather(n, buffer, ready):
                    at = pool.value_load(starts[0:1, bass.ds(n, 1)], min_val=0, max_val=PAIRS)
                    pool.tensor_copy(xe[:, buffer], sorted_x[:, :, bass.ds(at, BLK)]).then_inc(ready.sem, 1)

                with pool.If(big == 0):
                    for e in range(2):
                        gather(e, e, s.xe_ready)
                    with pool.Fori(1, NE // 2) as r:
                        for j in range(2):
                            pool.wait_ge(*s.gu_done.at(r * 2 + j - 1))
                            gather(r * 2 + j, j, s.xe_ready)
                with pool.Else():
                    with pool.Fori(0, NE) as e:
                        for b in range(NBLK):
                            pool.wait_ge(*s.gu_slow.at(e * NBLK + b + 1))
                            gather(e + b * NE, 0, s.xe_slow)

        @block.scalar
        def _(act):
            activate = nc.scalar.activation
            act.dma_start(const[:, :], constants).then_inc(const_in, 16)
            act.dma_start(x_nat, w["x"][0].rearrange("(t p) d -> p t d", p=P)).then_inc(x_in, 16)
            act.wait_ge(vec_kept, 2)
            activate(silu_c[:, :], row(0, "c"), ACT.Silu).then_inc(silu_c_ready, 1)

            for l in range(DEPTH):
                s = sig[l]
                blocks = mixer_blocks(l)
                ends = items_at_block_end(l)
                count = Place()

                def keep_block():
                    j = count.block
                    count.block += 1
                    b, bank = blocks[j], 2 * (j % 2)
                    act.wait_ge(*s.item_used.at(ends[j]))
                    pair = ps[:, bank:bank + 2, :].rearrange("p b (n t) -> p (b n) t", t=T)
                    if b[0] == "M":
                        last = nc.scalar.copy(mod[:, b[1], 16 * b[2]:16 * b[2] + 16], ps[:, bank, 0:16])
                    elif b[0] == "KVI":
                        nc.scalar.copy(qk[:, :, HEADS, :], ps[:, bank:bank + 2, 0:HD])
                        last = nc.scalar.copy(kvi, ps[:, bank:bank + 2, 0:N_KVI])
                    elif b[0] == "Q":
                        last = nc.scalar.copy(qk[:, :, 0:HEADS, :].rearrange("p t h d -> p t (h d)"),
                                              ps[:, bank:bank + 2, :])
                    elif b[0] == "CA":
                        last = nc.scalar.copy(ca, pair)
                    elif b[0] == "CB":
                        last = activate(cb, pair, ACT.Sigmoid)
                    else:
                        last = activate(gates[:, b[1] // 2, 4 * (b[1] % 2):4 * (b[1] % 2) + 4, :], pair, ACT.Sigmoid)
                    last.then_inc(s.block_kept.sem, 1)

                def norm(n, sq, shift):
                    act.wait_ge(*s.x_ready.at(n))
                    activate(sq, xT[:, :, :], ACT.Square).then_inc(s.sq_ready.sem, 1)
                    act.wait_ge(*s.ssq_ready.at(n))
                    activate(std[:, :], ps[:, 7, 0:T], ACT.Sqrt, bias=eps, scale=1.0 / D).then_inc(s.std_ready.sem, 1)
                    for c in range(DC):
                        act.wait_ge(*s.scaled.at(DC * (n - 1) + c + 1))
                        activate(hT[:, c, :], hT[:, c, :], ACT.Identity,
                                 bias=modulation(l, shift)[:, c:c + 1]).then_inc(s.h_ready.sem, 1)

                act.wait_ge(const_in, 16)
                if l == 0:
                    keep_block()
                norm(1, square, SHIFT1)
                keep_block()
                keep_block()
                act.wait_ge(*s.q_rms_ready.at(1))
                activate(rms, sumsq, ACT.Sqrt, bias=eps, scale=1.0 / HD).then_inc(s.q_std_ready.sem, 1)
                keep_block()
                for g in range(4):
                    act.wait_ge(*s.turn_done.at(g + 1))
                    nc.scalar.copy(turned[:, 2 * (0, 1, 2, 3)[g]:2 * (0, 1, 2, 3)[g] + 2, :],
                                   ps[:, 4 + g % 3, :].rearrange("p (n t) -> p n t", t=T)).then_inc(s.turn_kept.sem, 1)

                def keep_index(u):
                    act.wait_ge(*s.index_done.at(u + 1))
                    n = (u + 1) * P
                    if u == 1:
                        act.wait_ge(*s.index_read.at(1))
                    activate(scores[:, :, 0:n].rearrange("p (b g) s -> p b g s", g=2),
                             ps[:, 4:8, 0:2 * n].rearrange("p b (g s) -> p b g s", s=n),
                             ACT.Relu).then_inc(s.index_kept.sem, 1)

                def exponentials(u):
                    act.wait_ge(*s.att_max.at(u + 1))
                    for h in (range(HEADS) if u == 0 else range(4 * (u - 1), 4 * u)):
                        tile = scores0[:, h, :] if u == 0 else scores[:, h, :]
                        i = (HEADS if u else 0) + h
                        activate(tile, tile, ACT.Exp, bias=rowmax[:, i:i + 1],
                                 accum_out=rowsum[:, i:i + 1]).then_inc(s.att_exp.sem, 1)

                keep_index(0)
                keep_block()
                keep_index(1)
                keep_block()
                keep_block()
                if l == 0:
                    keep_block()
                exponentials(0)
                keep_block()
                exponentials(1)
                if l == 0:
                    keep_block()
                exponentials(2)
                for g in range(2):
                    act.wait_ge(*s.prob_turned.at(g + 1))
                    nc.scalar.copy(probsT[:, 4 * g:4 * g + 4, 0:P],
                                   ps[:, 6 + g, :].rearrange("p (h t) -> p h t", t=P)).then_inc(s.prob_kept.sem, 1)
                act.wait_ge(*s.pv_done.at(1))
                for g in range(4):
                    act.wait_ge(*s.prob_turned.at(2 + g + 1))
                    nc.scalar.copy(probsT[:, 2 * g:2 * g + 2, :],
                                   ps[:, 6 + g % 2, :].rearrange("p (h t) -> p h t", t=T)).then_inc(s.prob_kept.sem, 1)
                while count.block < len(blocks):
                    keep_block()
                act.wait_ge(*s.attn_turned.at(1))
                nc.scalar.copy(attnT, ps[:, 6:8, :].rearrange("p b (n t) -> p (b n) t", t=T)).then_inc(s.attn_kept.sem, 1)

                act.wait_ge(*s.centred.at(1))
                activate(ca, cb, ACT.Square).then_inc(s.ln_sq_ready.sem, 1)
                act.wait_ge(*s.var_ready.at(1))
                activate(std[:, :], ps[:, 7, T:2 * T], ACT.Sqrt, bias=eps, scale=1.0 / CH).then_inc(s.ln_std_ready.sem, 1)
                act.wait_ge(*s.ln_ready.at(1))
                for c in range(CC):
                    activate(ca[:, c, :], cb[:, c, :], ACT.Silu, bias=row(l, "conv_ln_b")[:, c:c + 1],
                             scale=row(l, "conv_ln_g")[:, c:c + 1]).then_inc(s.conv_act_ready.sem, 1)

                norm(2, square2, SHIFT2)
                for g in range(4):
                    act.wait_ge(*s.hn_turned.at(g + 1))
                    nc.scalar.copy(hn[:, g // 2, (g % 2) * 512:(g % 2 + 1) * 512], ps[:, g, :]).then_inc(s.hn_kept.sem, 1)
                act.wait_ge(*s.group_shifted.at(1))
                activate(g_exp, g_shift, ACT.Exp).then_inc(s.group_exp.sem, 1)
                act.wait_ge(*s.gap_ready.at(1))
                activate(gap_exp, gap, ACT.Exp).then_inc(s.gap_exp.sem, 1)
                for c in range(DC):
                    act.wait_ge(*s.sorted_done.at(c + 1))
                    nc.scalar.copy(sorted_x[:, c, 0:PAIRS], ps[:, c % 4, :]).then_inc(s.sorted_kept.sem, 1)
                act.wait_ge(*s.offs_ready.at(1))
                act.wait_ge(*s.weighted_ready.at(TC))
                big = act.value_load(flag[0:1, l:l + 1], min_val=0, max_val=1)
                starts = offs[0:1, l].rearrange("q b e -> q (b e)")

                def store(n, bank):
                    at = act.value_load(starts[0:1, bass.ds(n, 1)], min_val=0, max_val=PAIRS)
                    return nc.scalar.copy(made[:, :, bass.ds(at, BLK)],
                                          ps[:, bank, :].rearrange("p (c s) -> p c s", c=DC))

                with act.If(big == 0):
                    act.preload_act_table(ACT.Silu)

                    def step(e, j):
                        act.wait_ge(*s.gu_done.at(e + 1))
                        if not isinstance(e, int) or e >= 2:
                            act.wait_ge(*s.hid_ready.at(e - 1))
                        activate(act_g[:, j % 2, :], ps[:, j % 2, 0:FC * BLK], ACT.Silu).then_inc(s.act_ready.sem, 1)

                    def step_store(e, j):
                        act.wait_ge(*s.expert_used.at(e + 1))
                        if not isinstance(e, int) or e >= 1:
                            act.wait_ge(*s.y_stored.at(e))
                        store(e, 2 + j % 2).then_inc(s.y_stored.sem, 1)

                    step(0, 0)
                    step(1, 1)
                    step_store(0, 0)
                    with act.Fori(1, NE // 2) as r:
                        step(r * 2, 0)
                        step_store(r * 2 - 1, 1)
                        step(r * 2 + 1, 1)
                        step_store(r * 2, 0)
                    act.wait_ge(*s.expert_used.at(NE))
                    act.wait_ge(*s.y_stored.at(NE - 1))
                    store(NE - 1, 3).then_inc(s.experts_done.sem, 1)
                with act.Else():
                    act.preload_act_table(ACT.Silu)
                    act.sem_inc(s.y_slow.sem, 1)

                    def step_slow(e, b):
                        n = e * NBLK + b
                        act.wait_ge(*s.gu_slow.at(n + 2))
                        activate(act_g[:, 0, :], ps[:, 0, 0:FC * BLK], ACT.Silu).then_inc(s.act_slow.sem, 1)
                        if b < NBLK - 1:
                            act.wait_ge(*s.down_slow.at(e * (NBLK - 1) + b + 1))
                        else:
                            act.wait_ge(*s.expert_used.at(e + 1))
                        act.wait_ge(*s.y_slow.at(n + 1))
                        return store(e + b * NE, 2)

                    with act.Fori(0, NE - 1) as e:
                        for b in range(NBLK):
                            step_slow(e, b).then_inc(s.y_slow.sem, 1)
                    for b in range(NBLK):
                        step_slow(NE - 1, b).then_inc((s.y_slow if b < NBLK - 1 else s.experts_done).sem, 1)

                for g in range(8):
                    act.wait_ge(*s.made_turned.at(g + 1))
                    nc.scalar.copy(made_n[:, g // 2, (g % 2) * 512:(g % 2 + 1) * 512],
                                   ps[:, 4 + g % 4, :]).then_inc(s.made_kept.sem, 1)

            for g in range(4):
                act.wait_ge(y_turned, g + 1)
                nc.scalar.copy(y_nat[:, g // 2, (g % 2) * 512:(g % 2 + 1) * 512], ps[:, 4 + g, :]).then_inc(y_kept, 1)

        @block.vector
        def _(dve):
            v = nc.vector
            n_step = Place()

            def mark(ins):
                n_step.n += 1
                ins.then_inc(dve_step, 1)
                return n_step.n

            def sync():
                dve.wait_ge(dve_step, n_step.n)

            def do(ins):
                mark(ins)
                sync()

            tt, ts, stt, red = v.tensor_tensor, v.tensor_scalar, v.scalar_tensor_tensor, v.tensor_reduce

            dve.wait_ge(const_in, 16)
            dve.wait_ge(small_in, 16 * N_SMALL)
            dve.wait_ge(vec_turned, 1)
            v.tensor_copy(vec[:, :, :], ps[:, 0, 0:256].rearrange("p (l r) -> p l r", l=DEPTH)[:, :, 0:N_ROWS]).then_inc(vec_kept, 1)
            v.tensor_copy(taps[:, :, :, :].rearrange("p l k c -> p l (k c)"),
                          ps[:, 0, 256:512].rearrange("p (l r) -> p l r", l=DEPTH)[:, :, 0:N_TAPROWS]).then_inc(vec_kept, 1)
            dve.wait_ge(x_turned, 1)
            v.tensor_copy(xT[:, :, :].rearrange("p c t -> p (c t)"),
                          ps[:, 4:8, :].rearrange("p b n -> p (b n)")).then_inc(sig[0].x_ready.sem, 1)
            dve.wait_ge(vec_kept, 2)

            def bias_modulation(ml, a, b):
                m = mod[:, ml, a:b]
                return tt(m, m, row(ml, "b_ada")[:, a:b], ALU.add)

            for l in range(DEPTH):
                s = sig[l]
                blocks = mixer_blocks(l)
                ends = items_at_block_end(l)
                n_items = len(mixer_items(l))

                def gains(n, scale, g):
                    return stt(out=gain[:, l, n, :], in0=modulation(l, scale), scalar=1.0, in1=row(l, g),
                               op0=ALU.add, op1=ALU.mult)

                def norm(n):
                    dve.wait_ge(*s.std_ready.at(n))
                    do(v.reciprocal(rstd[:, :], std[:, :]))
                    for c in range(DC):
                        stt(out=hT[:, c, :], in0=xT[:, c, :], scalar=gain[:, l, n - 1, c:c + 1], in1=rstd[:, :],
                            op0=ALU.mult, op1=ALU.mult).then_inc(s.scaled.sem, 1)

                if l == 0:
                    dve.wait_ge(*s.block_kept.at(1))
                    do(bias_modulation(0, 0, 16))
                do(gains(0, SCALE1, "g_norm1"))
                norm(1)

                def rotate(dst, src, cos, sin, heads, half):
                    shape = [P, TC, heads, half]
                    cs, sn = cos.unsqueeze(2).to_broadcast(shape), sin.unsqueeze(2).to_broadcast(shape)
                    x1, x2 = src[:, :, :, 0:half], src[:, :, :, half:2 * half]
                    o1, o2 = dst[:, :, 0:heads, 0:half], dst[:, :, 0:heads, half:2 * half]
                    t1, t2 = tmp[:, :, 0:heads, 0:half], tmp[:, :, 0:heads, half:2 * half]
                    mark(tt(o1, x1, cs, ALU.mult))
                    mark(tt(o2, x2, cs, ALU.mult))
                    mark(tt(t1, x2, sn, ALU.mult))
                    mark(tt(t2, x1, sn, ALU.mult))
                    sync()
                    mark(tt(o1, o1, t1, ALU.subtract))
                    mark(tt(o2, o2, t2, ALU.add))
                    sync()

                first = 1 if l == 0 else 0
                dve.wait_ge(*s.block_kept.at(first + 1))
                index = kvi[:, :, 2 * HD:2 * HD + (IH + 1) * ID].rearrange("p t (h d) -> p t h d", d=ID)
                iweight = kvi[:, :, N_KVI - IH:N_KVI]
                rotate(ir, index, cos_i, sin_i, IH + 1, ID // 2)
                v.tensor_copy(ir[:, :, IH + 1:IH + 4, :],
                              ir[:, :, IH:IH + 1, :].to_broadcast([P, TC, 3, ID])).then_inc(s.index_rotated.sem, 1)
                dve.wait_ge(*s.block_kept.at(first + 2))
                do(tt(tmp, qk, qk, ALU.mult))
                red(sumsq.rearrange("p (t h) -> p t h", t=TC), tmp, AX.X, ALU.add).then_inc(s.q_rms_ready.sem, 1)
                dve.wait_ge(*s.q_std_ready.at(1))
                do(v.reciprocal(rms, rms))
                do(tt(qk, qk, rms.rearrange("p (t h) -> p t h", t=TC).unsqueeze(3).to_broadcast(
                    [P, TC, HEADS + 1, HD]), ALU.mult))
                do(tt(qk, qk, qk_gain[:, l].unsqueeze(1).to_broadcast([P, TC, HEADS + 1, HD]), ALU.mult))
                rotate(qr, qk, cos_h, sin_h, HEADS + 1, HD // 2)
                v.tensor_copy(qr[:, :, HEADS + 1, :], qr[:, :, HEADS, :]).then_inc(s.q_rotated.sem, 1)

                def add_index(t, heads):
                    n = (t + 1) * P
                    acc = iscore[:, t, 0:n]
                    for h in heads:
                        at = (h % 4) * 2 + h // 4
                        if h == 0:
                            ins = ts(acc, scores[:, at, 0:n], iweight[:, t, h:h + 1], None, ALU.mult)
                        else:
                            ins = stt(out=acc, in0=scores[:, at, 0:n], scalar=iweight[:, t, h:h + 1], in1=acc,
                                      op0=ALU.mult, op1=ALU.add)
                        if h < IH - 1 or t > 0:
                            do(ins)
                        else:
                            ins.then_inc(s.index_read.sem, 1)
                            dve.wait_ge(*s.index_read.at(1))

                def select(t):
                    n = (t + 1) * P
                    work = iscore[:, t, 0:n]
                    do(stt(out=work, in0=work, scalar=ISCALE, in1=causal[:, t, 0:n], op0=ALU.mult, op1=ALU.add))
                    for _ in range(TOPK // 8):
                        do(v.max(out=top8, in_=work))
                        do(v.match_replace(out=work, in_to_replace=top8, in_values=work, imm_value=TAKEN))
                    do(ts(drop[:, t, 0:n], work, 0.5 * TAKEN, NEG, ALU.is_gt, ALU.mult))
                    do(tt(drop[:, t, 0:n], drop[:, t, 0:n], causal[:, t, 0:n], ALU.add))

                def mask(u):
                    t = 0 if u == 0 else 1
                    dve.wait_ge(*s.att_done.at(u + 1))
                    if u == 0:
                        dst, heads, n, i = scores0, HEADS, P, 0
                    else:
                        dst, heads, n, i = scores[:, 4 * (u - 1):4 * u, :], 4, T, HEADS + 4 * (u - 1)
                    stt(out=dst, in0=ps[:, 4:6, :].rearrange("p b (h s) -> p (b h) s", s=n), scalar=HD ** -0.5,
                        in1=drop[:, t, 0:n].unsqueeze(1).to_broadcast([P, heads, n]),
                        op0=ALU.mult, op1=ALU.add).then_inc(s.att_masked.sem, 1)
                    dve.wait_ge(*s.att_masked.at(u + 1))
                    red(rowmax[:, i:i + heads], dst, AX.X, ALU.max, negate=True).then_inc(s.att_max.sem, 1)

                at_tap = {}

                def convolve(a, b):
                    for tap in range(a, b):
                        for c in range(CC):
                            src, wt = pad[:, c, tap:tap + T], taps[:, l, tap, c:c + 1]
                            if tap == 0:
                                ins = ts(ca[:, c, :], src, wt, row(l, "conv_b")[:, c:c + 1], ALU.mult, ALU.add)
                            else:
                                dve.wait_ge(dve_step, at_tap[c])
                                ins = stt(out=ca[:, c, :], in0=src, scalar=wt, in1=ca[:, c, :],
                                          op0=ALU.mult, op1=ALU.add)
                            at_tap[c] = mark(ins)

                def normalise(t):
                    dve.wait_ge(*s.pv_done.at(t + 1))
                    do(v.reciprocal(rowinv[:, 8 * t:8 * t + 8], rowsum[:, 8 * t:8 * t + 8]))
                    units = 1 if t == 0 else 2
                    n = HEADS // units
                    for u in range(units):
                        last = tt(attn[:, t, u * n:(u + 1) * n, :].rearrange("p (c q) d -> p q c d", q=2),
                                  ps[:, 4 + t, u * n * HD:(u + 1) * n * HD].rearrange("p (q c d) -> p q c d", q=2, d=HD),
                                  rowinv[:, 8 * t + u * n:8 * t + (u + 1) * n].rearrange("p (q c) -> p q c", q=2)
                                  .unsqueeze(3).to_broadcast([P, 2, n // 2, HD]), ALU.mult)
                        if u < units - 1:
                            mark(last)
                    last.then_inc(s.attn_ready.sem, 1)

                dve.wait_ge(*s.index_kept.at(1))
                add_index(0, range(IH))
                select(0)
                dve.wait_ge(*s.block_kept.at(first + 4))
                dve.wait_ge(*s.pad_zero.at(1))
                mark(tt(pad[:, :, TAPS - 1:], ca, cb, ALU.mult))
                dve.wait_ge(*s.index_kept.at(2))
                add_index(1, range(IH))
                select(1)
                mask(0)
                mask(1)
                convolve(0, 12)
                mask(2)
                convolve(12, 22)
                normalise(0)
                normalise(1)
                convolve(22, TAPS - 1)
                for c in range(CC):
                    dve.wait_ge(dve_step, at_tap[c])
                    src, wt = pad[:, c, TAPS - 1:], taps[:, l, TAPS - 1, c:c + 1]
                    ins = stt(out=ca[:, c, :], in0=src, scalar=wt, in1=ca[:, c, :], op0=ALU.mult, op1=ALU.add)
                    if c < CC - 1:
                        mark(ins)
                    else:
                        ins.then_inc(s.conv_ready.sem, 1)
                sync()

                dve.wait_ge(*s.mean_ready.at(1))
                dve.wait_ge(*s.conv_ready.at(1))
                stt(out=cb, in0=ps[:, 7, 0:T].unsqueeze(1).to_broadcast([P, CC, T]), scalar=-1.0 / CH, in1=ca,
                    op0=ALU.mult, op1=ALU.add).then_inc(s.centred.sem, 1)
                dve.wait_ge(*s.ln_std_ready.at(1))
                do(v.reciprocal(rstd[:, :], std[:, :]))
                tt(cb, cb, rstd[:, :].unsqueeze(1).to_broadcast([P, CC, T]), ALU.mult).then_inc(s.ln_ready.sem, 1)

                dve.wait_ge(*s.block_kept.at(len(blocks)))
                if l == 0:
                    mark(bias_modulation(0, 16, 48))
                    mark(bias_modulation(1, 0, 48))
                    sync()
                for p in range(4):
                    if p < 3:
                        dve.wait_ge(*s.ya_done.at(p + 1))
                    else:
                        dve.wait_ge(*s.item_used.at(n_items - 3))
                    g = gates[:, 1, 2 * p:2 * p + 2, :]
                    tt(g, ps[:, p, :].rearrange("p (n t) -> p n t", t=T), g, ALU.mult).then_inc(s.ya_used.sem, 1)
                for p in range(4):
                    if p < 3:
                        dve.wait_ge(*s.yc_done.at(p + 1))
                    else:
                        dve.wait_ge(*s.item_used.at(n_items - 2))
                    for n in range(2):
                        c = 2 * p + n
                        mark(stt(out=gates[:, 0, c, :], in0=ps[:, 4 + p, n * T:(n + 1) * T],
                                 scalar=row(l, "b_conv_out")[:, c:c + 1], in1=gates[:, 0, c, :],
                                 op0=ALU.add, op1=ALU.mult))
                    sync()
                    dve.wait_ge(*s.ya_used.at(p + 1))
                    tt(merged[:, 2 * p:2 * p + 2, :], gates[:, 0, 2 * p:2 * p + 2, :],
                       gates[:, 1, 2 * p:2 * p + 2, :], ALU.add).then_inc(s.merged_ready.sem, 1)
                for c in range(DC):
                    if c % 4 == 1 or c % 4 == 0:
                        dve.wait_ge(*s.out_done.at(c // 4 + 1))
                    else:
                        dve.wait_ge(*s.item_used.at(n_items - 1 + c // 4))
                    ins = stt(out=xT[:, c, :], in0=ps[:, c // 2, (c % 2) * T:(c % 2 + 1) * T],
                              scalar=modulation(l, GATE1)[:, c:c + 1], in1=xT[:, c, :], op0=ALU.mult, op1=ALU.add)
                    if c < DC - 1:
                        mark(ins)
                    else:
                        sync()
                        ins.then_inc(s.x_ready.sem, 1)

                dve.wait_ge(*s.x_ready.at(2))
                do(gains(1, SCALE2, "g_norm2"))
                norm(2)
                dve.wait_ge(*s.logits_done.at(1))
                W = GROUPS + NE
                do(tt(logits, ps[:, 4, 0:TC * W].rearrange("p (t n) -> p t n", n=W),
                      b_route[:, l].unsqueeze(1).to_broadcast([P, TC, W]), ALU.add))
                g_log = logits[:, :, 0:GROUPS]

                def over(x, n):
                    return x.unsqueeze(2).to_broadcast([P, TC, n])

                def first_of(dst, eq, n, best):
                    do(tt(eq, eq, falling[:, 0:n].unsqueeze(1).to_broadcast([P, TC, n]), ALU.mult))
                    do(red(best, eq, AX.X, ALU.max))
                    return tt(dst, eq, over(best, n), ALU.is_equal)

                do(red(g_max, g_log, AX.X, ALU.max))
                tt(g_shift3, g_log, over(g_max, GROUPS), ALU.subtract).then_inc(s.group_shifted.sem, 1)
                do(tt(g_one, g_log, over(g_max, GROUPS), ALU.is_equal))
                do(first_of(g_one, g_one, GROUPS, best))
                do(ts(g_one, g_one, -1.0, -NEG, ALU.add, ALU.mult))
                do(tt(e_in.rearrange("p t (g e) -> p t g e", g=GROUPS),
                      logits[:, :, GROUPS:].rearrange("p t (g e) -> p t g e", g=GROUPS),
                      g_one.unsqueeze(3).to_broadcast([P, TC, GROUPS, EPG]), ALU.add))
                do(red(top_a, e_in, AX.X, ALU.max))
                do(tt(hot_a, e_in, over(top_a, NE), ALU.is_equal))
                do(first_of(hot_a, hot_a, NE, best))
                do(stt(out=e_in, in0=hot_a, scalar=2 * NEG, in1=e_in, op0=ALU.mult, op1=ALU.add))
                do(red(top_b, e_in, AX.X, ALU.max))
                do(tt(hot_b, e_in, over(top_b, NE), ALU.is_equal))
                do(first_of(hot_b, hot_b, NE, best))
                tt(member, hot_a, hot_b, ALU.add).then_inc(s.member_ready.sem, 1)
                tt(gap, top_b, top_a, ALU.subtract).then_inc(s.gap_ready.sem, 1)
                dve.wait_ge(*s.rank_done.at(1))
                counts = ps[:, 5, 2 * NE:3 * NE]
                do(v.tensor_copy(count_sb, counts))
                do(v.tensor_tensor_scan(start, ones[:, 0:NE], count_sb, 0.0, ALU.mult, ALU.add))
                do(tt(start, start, count_sb, ALU.subtract))
                for b in range(NBLK):
                    mark(ts(offs[0:1, l, b, :], start[0:1, :], float(b * BLK), float(PAIRS), ALU.add, ALU.min))
                do(red(best[0:1, 0:1], count_sb[0:1, :], AX.X, ALU.max))
                ts(flag[0:1, l:l + 1], best[0:1, 0:1], float(BLK), None, ALU.is_gt).then_inc(s.offs_ready.sem, 1)
                do(tt(place, ps[:, 5, 0:2 * NE].rearrange("p (t e) -> p t e", t=TC),
                      start.unsqueeze(1).to_broadcast([P, TC, NE]), ALU.add))
                mark(tt(hot_a, hot_a, place, ALU.mult))
                mark(tt(hot_b, hot_b, place, ALU.mult))
                sync()
                mark(red(slot_a, hot_a, AX.X, ALU.add))
                mark(red(slot_b, hot_b, AX.X, ALU.add))
                sync()
                for t in range(TC):
                    do(ts(onehot[:, t, :], iota, slot_a[:, t:t + 1], None, ALU.is_equal))
                    stt(out=onehot[:, t, :], in0=iota, scalar=slot_b[:, t:t + 1], in1=onehot[:, t, :],
                        op0=ALU.is_equal, op1=ALU.add).then_inc(s.onehot_ready.sem, 1)
                dve.wait_ge(*s.group_exp.at(1))
                do(red(best, g_exp3, AX.X, ALU.add))
                do(v.reciprocal(best, best))
                dve.wait_ge(*s.gap_exp.at(1))
                do(ts(weight_b, gap_exp, 1.0, None, ALU.add))
                do(v.reciprocal(weight_b, weight_b))
                do(tt(weight_a, best, weight_b, ALU.mult))
                do(tt(weight_b, weight_a, gap_exp, ALU.mult))
                for t in range(TC):
                    mark(ts(weighted[:, t, :], iota, slot_a[:, t:t + 1], weight_a[:, t:t + 1], ALU.is_equal, ALU.mult))
                    mark(ts(scratch[:, t, :], iota, slot_b[:, t:t + 1], weight_b[:, t:t + 1], ALU.is_equal, ALU.mult))
                    sync()
                    tt(weighted[:, t, :], weighted[:, t, :], scratch[:, t, :], ALU.add).then_inc(s.weighted_ready.sem, 1)
                dve.wait_ge(*s.spread_turned.at(1))
                v.tensor_copy(spread.rearrange("p j t -> p (j t)"),
                              ps[:, 6:8, :].rearrange("p b n -> p (b n)")).then_inc(s.spread_kept.sem, 1)

                dve.wait_ge(*s.offs_ready.at(1))
                big = dve.value_load(flag[0:1, l:l + 1], min_val=0, max_val=1)

                def product(j, bank):
                    return tt(hid[:, j].rearrange("p f s -> p (f s)"), ps[:, bank, FC * BLK:2 * FC * BLK],
                              act_g[:, j, :], ALU.mult)

                with dve.If(big == 0):
                    for e in range(2):
                        dve.wait_ge(*s.act_ready.at(e + 1))
                        product(e, e).then_inc(s.hid_ready.sem, 1)
                    with dve.Fori(1, NE // 2) as r:
                        for j in range(2):
                            dve.wait_ge(*s.act_ready.at(r * 2 + j + 1))
                            dve.wait_ge(*s.expert_used.at(r * 2 + j - 1))
                            product(j, j).then_inc(s.hid_ready.sem, 1)
                with dve.Else():
                    with dve.Fori(0, NE * NBLK) as n:
                        dve.wait_ge(*s.act_slow.at(n + 1))
                        dve.wait_ge(*s.y_slow.at(n + 1))
                        product(0, 0).then_inc(s.hid_slow.sem, 1)

                done = sig[l + 1].x_ready if l + 1 < DEPTH else s.x_ready
                for c in range(DC):
                    dve.wait_ge(*s.final_done.at(c // 2 + 1))
                    ins = stt(out=xT[:, c, :], in0=ps[:, c // 2, (c % 2) * T:(c % 2 + 1) * T],
                              scalar=modulation(l, GATE2)[:, c:c + 1], in1=xT[:, c, :], op0=ALU.mult, op1=ALU.add)
                    if c < DC - 1:
                        mark(ins)
                    else:
                        sync()
                        ins.then_inc(done.sem, 1)
                dve.wait_ge(*done.at(1 if l + 1 < DEPTH else 3))


NAMES = ["x", "c", "w_ada", "b_ada", "g_norm1", "w_in", "q_norm_g", "k_norm_g", "conv_w", "conv_b", "conv_ln_g",
         "conv_ln_b", "w_conv_out", "b_conv_out", "w_attn_out", "w_out", "g_norm2", "w_group", "b_group",
         "w_router", "b_router", "w_gate", "w_up", "w_down"]


def shape_constants():
    import numpy as np

    f = np.float32
    table = np.zeros((P, N_CONST), f)
    i = np.arange(P)

    def put(name, value):
        table[:, CONST[name][0]:CONST[name][1]] = value

    put("ident", np.eye(P))
    put("ones", 1.0)
    put("before", i[:, None] < i[None, :])
    token = np.arange(T).reshape(TC, P)
    later = np.arange(T)[None, None, :] > token.T[:, :, None]
    put("causal", np.where(later, f(NEG), f(0)).reshape(P, TC * T))
    put("iota", np.arange(PAIRS)[None, :])
    for tag, dim in (("h", HD), ("i", ID)):
        inv = f(10000.0) ** (-np.arange(0, dim, 2, dtype=f) / f(dim))
        ang = np.arange(T, dtype=f)[:, None] * inv.astype(f)[None, :]
        for name, fn in (("cos_", np.cos), ("sin_", np.sin)):
            put(name + tag, fn(ang).astype(f).reshape(TC, P, dim // 2).transpose(1, 0, 2).reshape(P, -1))
    put("falling", np.arange(NE, 0, -1)[None, :])
    put("eps", EPS)
    return table


def kernel(**inputs):
    import numpy as np
    import concourse.bacc as bacc
    from concourse.bass_utils import run_bass_kernel_spmd as run

    nc = bacc.Bacc("TRN2", target_bir_lowering=False, num_devices=1)
    arrays, w = {}, {}
    for name in NAMES:
        a = np.ascontiguousarray(inputs[name])
        arrays[f"in_{name}"] = a
        w[name] = nc.dram_tensor(f"in_{name}", a.shape, mybir.dt.from_np(a.dtype), kind="ExternalInput").ap()
    arrays["constants"] = shape_constants()
    constants = nc.dram_tensor("constants", (P, N_CONST), F32, kind="ExternalInput").ap()
    out = nc.dram_tensor("out", (1, T, D), F32, kind="ExternalOutput").ap()
    trunk_kernel(nc, w, constants, out)
    r = run(nc, [arrays], core_ids=[0])
    return r.results[0]["out"]
```

```python
from collections import namedtuple
from contextlib import ExitStack

import concourse.bass as bass
from concourse import mybir

F32 = mybir.dt.float32
I32 = mybir.dt.int32
ALU = mybir.AluOpType
ACT = mybir.ActivationFunctionType
AX = mybir.AxisListType

P = 128
D = 1024
DC = D // P
T = 256
TC = T // P
DEPTH = 2
N_MOD = 6
CH = 512
CC = CH // P
TAPS = 31
HEADS = 8
HD = 64
IH = 8
ID = 32
ISCALE = (ID ** -0.5) * (IH ** -0.5)
TOPK = 64
GROUPS = 4
EPG = 8
NE = GROUPS * EPG
FE = 256
FC = FE // P
EPS = 1e-6
NEG = -1e30
TAKEN = -3e38

COL_Q = 2 * CH
COL_K = COL_Q + HEADS * HD
COL_G = COL_K + 2 * HD + IH * ID + ID + IH
N_KVI = COL_G - COL_K
N_IN = COL_G + 2 * D

BLK = 128
NBLK = T // BLK
PAIRS = 2 * T
PADDED = PAIRS + BLK

ITEM = 4096
NITEM = 6
EXP = 6144
NEXP = 4
RING = NITEM * ITEM
assert RING == NEXP * EXP

CONST = {}
_at = 0
for _name, _n in (("ident", P), ("ones", P), ("before", P), ("causal", TC * T), ("iota", PAIRS),
                  ("cos_h", TC * HD // 2), ("sin_h", TC * HD // 2), ("cos_i", TC * ID // 2),
                  ("sin_i", TC * ID // 2), ("falling", NE), ("eps", 1)):
    CONST[_name] = (_at, _at + _n)
    _at += _n
N_CONST = _at

ROWS = {}
_at = 0
for _name, _n in (("b_ada", N_MOD * DC), ("g_norm1", DC), ("g_norm2", DC), ("b_conv_out", DC),
                  ("conv_b", CC), ("conv_ln_g", CC), ("conv_ln_b", CC), ("c", DC)):
    ROWS[_name] = (_at, _at + _n)
    _at += _n
N_ROWS = _at
N_TAPROWS = TAPS * CC


class Place:

    def __init__(self):
        self.item = self.block = self.n = 0


BLOCKS = ("KVI", "Q", "CA", "CB", "G0", "G1", "G2", "G3")


def mixer_items(layer):
    def ada(third, l=layer):
        return [("ada", l, third, i) for i in range(4)]

    early = ada(1)
    late = ada(2) + (ada(0, layer + 1) if layer + 1 < DEPTH else [])
    items = ada(0) if layer == 0 else []
    items += [("in", "KVI"), early[0], early[1], ("in", "Q"), early[2], ("in", "CA"), early[3]]
    items += [("in", b) for b in BLOCKS[3:]]
    items += [("attn_out",), ("conv_out",)] + late[:3] + [("out", 0), ("out", 1)] + late[3:]
    return items


def used_by(items):
    n = {"PE": 0, "DVE": 0}
    found = []
    for item in items:
        who = "DVE" if item[0] == "ada" else "PE"
        n[who] += 1
        found.append((who, n[who]))
    return found


N_OUT = len(BLOCKS) + 2
N_STAGE = DEPTH * (len(ROWS) + 1)
N_SMALL = DEPTH * 6


def trunk_kernel(nc, w, constants, out):
    with ExitStack() as ctx:
        def sb(name, shape, dt=F32):
            return ctx.enter_context(nc.sbuf_tensor(name, shape, dt))

        const = sb("const", [P, N_CONST])
        ring = sb("ring", [P, RING])
        xT = sb("xT", [P, DC, T])
        hT = sb("hT", [P, DC, T])
        vec = sb("vec", [P, DEPTH, N_ROWS])
        taps = sb("taps", [P, DEPTH, TAPS, CC])
        silu_c = sb("silu_c", [P, DC])
        mod = sb("mod", [P, DEPTH, N_MOD * DC])
        gain = sb("gain", [P, DEPTH, 2, DC])
        qk_gain = sb("qk_gain", [P, DEPTH, HEADS + 1, HD])
        w_route = sb("w_route", [P, DEPTH, DC, GROUPS + NE])
        b_route = sb("b_route", [P, DEPTH, GROUPS + NE])
        std = sb("std", [P, T])
        rstd = sb("rstd", [P, T])

        MIX = {}
        EX = {}

        def lay(table, names, at=0):
            for name, n in names:
                table[name] = (at, at + n)
                at += n
            return at

        end_mix = lay(MIX, (("kvi", TC * N_KVI), ("qk", TC * (HEADS + 1) * HD), ("tmp", TC * (HEADS + 1) * HD),
                            ("qr", TC * (HEADS + 2) * HD), ("ir", TC * (IH + 4) * ID), ("turned", 8 * T),
                            ("scores", HEADS * T), ("probsT", HEADS * T), ("gates", 2 * DC * T),
                            ("ca", CC * T), ("cb", CC * T), ("pad", CC * (T + TAPS - 1)),
                            ("drop", TC * T), ("stat", 160)))
        end_ex = lay(EX, (("hn", TC * D), ("onehot", TC * PAIRS), ("weighted", TC * PAIRS), ("spread", 4 * T),
                          ("sorted", DC * PADDED), ("made", DC * PADDED), ("xe", 2 * DC * BLK),
                          ("act", 2 * FC * BLK), ("hid", 2 * FC * BLK), ("route", 700)))
        arena = sb("arena", [P, max(end_mix, end_ex)])
        offs = sb("offs", [1, DEPTH, NBLK, NE], I32)
        flag = sb("flag", [1, DEPTH], I32)

        def mix(name):
            return arena[:, MIX[name][0]:MIX[name][1]]

        def ex(name):
            return arena[:, EX[name][0]:EX[name][1]]

        kvi = mix("kvi").rearrange("p (t n) -> p t n", t=TC)
        qk = mix("qk").rearrange("p (t h d) -> p t h d", t=TC, d=HD)
        tmp = mix("tmp").rearrange("p (t h d) -> p t h d", t=TC, d=HD)
        qr = mix("qr").rearrange("p (t h d) -> p t h d", t=TC, d=HD)
        ir = mix("ir").rearrange("p (t h d) -> p t h d", t=TC, d=ID)
        turned = mix("turned").rearrange("p (n t) -> p n t", t=T)
        IQT, IKT, KT, QT = 0, 2, 3, 4
        scores = mix("scores").rearrange("p (h s) -> p h s", h=HEADS)
        probsT = mix("probsT").rearrange("p (h t) -> p h t", h=HEADS)
        merged = mix("scores").rearrange("p (c t) -> p c t", c=DC)
        attn = arena[:, MIX["qr"][0]:MIX["qr"][0] + TC * HEADS * HD].rearrange(
            "p (t h d) -> p t h d", t=TC, d=HD)
        attnT = arena[:, MIX["qk"][0]:MIX["qk"][0] + 4 * T].rearrange("p (c t) -> p c t", t=T)
        gates = mix("gates").rearrange("p (b c t) -> p b c t", b=2, c=DC)
        ca = mix("ca").rearrange("p (c t) -> p c t", c=CC)
        cb = mix("cb").rearrange("p (c t) -> p c t", c=CC)
        pad = mix("pad").rearrange("p (c t) -> p c t", c=CC)
        drop = mix("drop").rearrange("p (t s) -> p t s", t=TC)
        iscore = arena[:, MIX["tmp"][0]:MIX["tmp"][0] + TC * T].rearrange("p (t s) -> p t s", t=TC)
        scores0 = mix("cb").rearrange("p (h s) -> p h s", h=HEADS)
        square = mix("probsT").rearrange("p (c t) -> p c t", c=DC)
        st = mix("stat")
        sumsq, rms = st[:, 0:18], st[:, 18:36]
        top8 = st[:, 36:44]
        rowmax, rowsum, rowinv = st[:, 44:60], st[:, 60:76], st[:, 76:92]

        hn = ex("hn").rearrange("p (t d) -> p t d", t=TC)
        onehot = ex("onehot").rearrange("p (t s) -> p t s", t=TC)
        weighted = ex("weighted").rearrange("p (t s) -> p t s", t=TC)
        spread = ex("spread").rearrange("p (j t) -> p j t", t=T)
        sorted_x = ex("sorted").rearrange("p (c s) -> p c s", c=DC)
        made = ex("made").rearrange("p (c s) -> p c s", c=DC)
        made_n = arena[:, 0:4 * D].rearrange("p (j d) -> p j d", d=D)
        assert 4 * D <= EX["spread"][0]
        square2 = mix("gates")[:, 0:DC * T].rearrange("p (c t) -> p c t", c=DC)
        partial_first = hT[:, :, :].rearrange("p c t -> p (c t)").rearrange("p (i n) -> p i n", i=4)
        partial_early = mix("gates")[:, DC * T:].rearrange("p (i n) -> p i n", i=4)
        partial_late = mix("turned").rearrange("p (i n) -> p i n", i=4)
        partial_next = mix("probsT").rearrange("p (i n) -> p i n", i=4)
        xe = ex("xe").rearrange("p (b c s) -> p b c s", b=2, c=DC)
        act_g = ex("act").rearrange("p (b n) -> p b n", b=2)
        hid = ex("hid").rearrange("p (b f s) -> p b f s", b=2, f=FC)
        rt = ex("route")
        small = {}
        lay(small, (("member", TC * NE), ("logits", TC * (GROUPS + NE)), ("g_max", TC), ("g_shift", TC * GROUPS),
                    ("g_exp", TC * GROUPS), ("g_one", TC * GROUPS), ("best", TC), ("e_in", TC * NE), ("top_a", TC),
                    ("top_b", TC), ("hot_a", TC * NE), ("hot_b", TC * NE), ("gap", TC), ("gap_exp", TC),
                    ("count", NE), ("start", NE), ("place", TC * NE), ("slot_a", TC), ("slot_b", TC),
                    ("weight_a", TC), ("weight_b", TC)))

        def small_tile(name, per_token=False):
            t = rt[:, small[name][0]:small[name][1]]
            return t.rearrange("p (t e) -> p t e", t=TC) if per_token else t

        member, logits, e_in = small_tile("member", True), small_tile("logits", True), small_tile("e_in", True)
        hot_a, hot_b, place = small_tile("hot_a", True), small_tile("hot_b", True), small_tile("place", True)
        g_shift, g_exp, g_one = small_tile("g_shift"), small_tile("g_exp"), small_tile("g_one", True)
        g_shift3, g_exp3 = small_tile("g_shift", True), small_tile("g_exp", True)
        g_max, best, top_a, top_b = small_tile("g_max"), small_tile("best"), small_tile("top_a"), small_tile("top_b")
        gap, gap_exp, count_sb, start = small_tile("gap"), small_tile("gap_exp"), small_tile("count"), small_tile("start")
        slot_a, slot_b = small_tile("slot_a"), small_tile("slot_b")
        weight_a, weight_b = small_tile("weight_a"), small_tile("weight_b")
        scratch = made[:, 0:2, 0:PAIRS]
        stage = arena[0:N_ROWS, EX["sorted"][0]:EX["sorted"][0] + DEPTH * P].rearrange("r (l q) -> r l q", l=DEPTH)
        stage_taps = arena[0:N_TAPROWS, EX["sorted"][0] + 256:EX["sorted"][0] + 512].rearrange(
            "r (l q) -> r l q", l=DEPTH)
        x_nat = ex("made")[:, 0:TC * D].rearrange("p (t d) -> p t d", t=TC)
        y_nat = hT[:, :, :].rearrange("p c t -> p (c t)").rearrange("p (t d) -> p t d", t=TC)

        def k(name):
            return const[:, CONST[name][0]:CONST[name][1]]

        ident, ones, before, iota = k("ident"), k("ones"), k("before"), k("iota")
        causal = k("causal").rearrange("p (t s) -> p t s", t=TC)
        cos_h = k("cos_h").rearrange("p (t d) -> p t d", t=TC)
        sin_h = k("sin_h").rearrange("p (t d) -> p t d", t=TC)
        cos_i = k("cos_i").rearrange("p (t d) -> p t d", t=TC)
        sin_i = k("sin_i").rearrange("p (t d) -> p t d", t=TC)
        falling, eps = k("falling"), k("eps")

        def row(layer, name):
            return vec[:, layer, ROWS[name][0]:ROWS[name][1]]

        SHIFT1, SCALE1, GATE1, SHIFT2, SCALE2, GATE2 = range(6)

        def modulation(layer, which):
            return mod[:, layer, which * DC:(which + 1) * DC]

        ps = ctx.enter_context(nc.psum_tensor("ps", [P, 8, 512], F32))

        def item_slot(i):
            return ring[:, (i % NITEM) * ITEM:(i % NITEM + 1) * ITEM]

        def expert_gate(slot):
            return ring[:, slot * EXP:slot * EXP + 2048].rearrange("p (c n) -> p c n", c=DC)

        def expert_up(slot):
            return ring[:, slot * EXP + 2048:slot * EXP + 4096].rearrange("p (c n) -> p c n", c=DC)

        def expert_down(slot):
            return ring[:, slot * EXP + 4096:slot * EXP + 6144].rearrange("p (f n) -> p f n", f=FC)

        def sem(name):
            return ctx.enter_context(nc.semaphore(name))

        const_in, x_in, stage_in, small_in = sem("const_in"), sem("x_in"), sem("stage_in"), sem("small_in")
        x_turned, vec_turned, vec_kept, silu_c_ready = sem("x_turned"), sem("vec_turned"), sem("vec_kept"), sem("silu_c_ready")
        dve_step = sem("dve_step")
        y_turned, y_kept, y_out = sem("y_turned"), sem("y_kept"), sem("y_out")
        EACH_LAYER = dict(
            sq_ready=2, ssq_ready=2, std_ready=2, scaled=2 * DC, h_ready=2 * DC, index_rotated=1, q_rms_ready=1,
            q_std_ready=1, q_rotated=1, turn_done=4, turn_kept=4, index_done=2, index_kept=2, index_read=1,
            att_done=3, att_masked=3, att_max=3, att_exp=2 * HEADS, prob_turned=6, prob_kept=6, pv_done=2,
            attn_ready=2, attn_turned=1, attn_kept=1, conv_ready=1, mean_ready=1, centred=1, ln_sq_ready=1,
            var_ready=1, ln_std_ready=1, ln_ready=1, conv_act_ready=CC, ya_done=3, ya_used=4, yc_done=3,
            merged_ready=4, out_done=2, pad_zero=1, logits_done=1, group_shifted=1, group_exp=1, gap_ready=1,
            gap_exp=1, member_ready=1, rank_done=1, hn_turned=4, hn_kept=4, onehot_ready=TC, offs_ready=1,
            sorted_done=DC, sorted_kept=DC, weighted_ready=TC, spread_turned=1, spread_kept=1, tail_zero=1,
            expert_used=NE, experts_done=1, made_turned=8, made_kept=8, final_done=4)
        OWN = ("item_used", "ada_used", "mod_summed", "x_ready", "block_kept", "xe_ready", "gu_done", "act_ready", "hid_ready", "y_stored",
               "xe_slow", "gu_slow", "act_slow", "hid_slow", "down_slow", "y_slow")

        class Signal:

            def __init__(self, semaphore, base):
                self.sem, self.base = semaphore, base

            def at(self, n):
                return self.sem, n + self.base if self.base else n

        shared = {name: sem(name) for name in EACH_LAYER}
        Signals = namedtuple("Signals", (*EACH_LAYER, *OWN))
        sig = [Signals(*(Signal(shared[n], l * each) for n, each in EACH_LAYER.items()),
                       *(Signal(sem(f"{n}_{l}"), 0) for n in OWN)) for l in range(DEPTH)]
        item_in = [[sem(f"item_in_{l}_{s}") for s in range(NITEM)] for l in range(DEPTH)]
        expert_in = [[sem(f"expert_in_{l}_{s}") for s in range(NEXP)] for l in range(DEPTH)]

        block = ctx.enter_context(nc.Block())

        @block.sync
        def _(sp):
            for l in range(DEPTH):
                s = sig[l]
                items = mixer_items(l)
                users = used_by(items)

                def wait_used(chosen):
                    for who, signal in (("PE", s.item_used), ("DVE", s.ada_used)):
                        counts = [users[i][1] for i in chosen if users[i][0] == who]
                        if counts:
                            sp.wait_ge(*signal.at(max(counts)))

                for i, item in enumerate(items):
                    if i >= NITEM:
                        wait_used([i - NITEM])
                    elif l > 0:
                        last = (i * ITEM + ITEM - 1) // EXP
                        sp.wait_ge(*sig[l - 1].expert_used.at(NE - NEXP + last + 1))
                    dst = item_slot(i)
                    if item[0] == "ada":
                        _, ml, third, quarter = item
                        n = 4 * third + quarter
                        src = w["w_ada"][ml, :, n * 512:(n + 1) * 512].rearrange("(c p) n -> p c n", p=P)
                        dst = dst.rearrange("p (c n) -> p c n", c=DC)
                    elif item[0] == "in":
                        b = item[1]
                        c0, n = {"KVI": (COL_K, N_KVI), "Q": (COL_Q, 512), "CA": (0, 512), "CB": (CH, 512)}.get(
                            b, (COL_G + 512 * (BLOCKS.index(b) - 4), 512))
                        src = w["w_in"][l, :, c0:c0 + n].rearrange("(c p) n -> p c n", p=P)
                        dst = dst[:, 0:DC * n].rearrange("p (c n) -> p c n", c=DC)
                    elif item[0] == "out":
                        src = w["w_out"][l, :, item[1] * 512:(item[1] + 1) * 512].rearrange("(c p) n -> p c n", p=P)
                        dst = dst.rearrange("p (c n) -> p c n", c=DC)
                    else:
                        src = w["w_" + item[0]][l].rearrange("(c p) n -> p c n", p=P)
                        dst = dst.rearrange("p (c n) -> p c n", c=4)
                    sp.dma_start(dst, src).then_inc(item_in[l][i % NITEM], 16)

                def load_expert(slot, e):
                    def src(name, pattern, **kw):
                        return w[name][l, bass.ds(e, 1)].rearrange(pattern, **kw)
                    sp.dma_start(expert_gate(slot).rearrange("p c n -> p (c n)"),
                                 src("w_gate", "a (p c) n -> p (a c n)", c=DC)).then_inc(expert_in[l][slot], 16)
                    sp.dma_start(expert_up(slot).rearrange("p c n -> p (c n)"),
                                 src("w_up", "a (p c) n -> p (a c n)", c=DC)).then_inc(expert_in[l][slot], 16)
                    sp.dma_start(expert_down(slot),
                                 src("w_down", "a (f p) n -> p (a f) n", p=P)).then_inc(expert_in[l][slot], 16)

                for slot in range(NEXP):
                    wait_used([i for i in range(len(items) - NITEM, len(items))
                               if (i % NITEM) * ITEM < (slot + 1) * EXP and (i % NITEM + 1) * ITEM > slot * EXP])
                    load_expert(slot, slot)
                with sp.Fori(1, NE // NEXP) as r:
                    for slot in range(NEXP):
                        sp.wait_ge(*s.expert_used.at((r - 1) * NEXP + slot + 1))
                        load_expert(slot, r * NEXP + slot)
            for t in range(TC):
                sp.wait_ge(y_kept, 2 * t + 2)
                sp.dma_start(out[0, t * P:(t + 1) * P, :], y_nat[:, t, :]).then_inc(y_out, 16)
            sp.wait_ge(y_out, 16 * TC)

        @block.tensor
        def _(pe):
            mm = nc.tensor.matmul

            def turn(dst, src, n_rows=P):
                return nc.tensor.transpose(dst, src, ident[0:n_rows, 0:n_rows])

            pe.wait_ge(const_in, 16)
            pe.wait_ge(stage_in, 16 * N_STAGE)
            for l in range(DEPTH):
                turn(ps[:, 0, l * P:l * P + N_ROWS], stage[:, l, :], N_ROWS)
                last = turn(ps[:, 0, 256 + l * P:256 + l * P + N_TAPROWS], stage_taps[:, l, :], N_TAPROWS)
            last.then_inc(vec_turned, 1)
            pe.wait_ge(x_in, 16)
            for c in range(DC):
                for t in range(TC):
                    last = turn(ps[:, 4 + c // 2, (c % 2) * T + t * P:(c % 2) * T + (t + 1) * P],
                                x_nat[:, t, c * P:(c + 1) * P])
            last.then_inc(x_turned, 1)

            for l in range(DEPTH):
                s = sig[l]
                at = Place()
                own = [i for i, (who, _) in enumerate(used_by(mixer_items(l))) if who == "PE"]

                n_ada = 4 if l == 0 else 0

                def item(c, n=ITEM):
                    i = own[at.item]
                    at.item += 1
                    pe.wait_ge(item_in[l][i % NITEM], 16 * (i // NITEM + 1))
                    return item_slot(i)[:, 0:n].rearrange("p (c n) -> p c n", c=c)

                def run_block():
                    j = at.block
                    at.block += 1
                    bank = 2 * (j % 2)
                    if j >= 2:
                        pe.wait_ge(*s.block_kept.at(j - 1))
                    if BLOCKS[j] in ("KVI", "Q"):
                        n = N_KVI if BLOCKS[j] == "KVI" else 512
                        wt = item(DC, DC * n)
                        for t in range(TC):
                            for c in range(DC):
                                if t == 0:
                                    pe.wait_ge(*s.h_ready.at(c + 1))
                                last = mm(ps[:, bank + t, 0:n], hT[:, c, t * P:(t + 1) * P], wt[:, c, :],
                                          start=c == 0, stop=c == DC - 1)
                    else:
                        wt = item(DC)
                        for n in range(4):
                            for c in range(DC):
                                last = mm(ps[:, bank + n // 2, (n % 2) * T:(n % 2 + 1) * T],
                                          wt[:, c, n * P:(n + 1) * P], hT[:, c, :], start=c == 0, stop=c == DC - 1)
                    last.then_inc(s.item_used.sem, 1)

                def sum_modulation(bank, partial, used):
                    for n in range(4 * 4):
                        if n % 4 == 0:
                            pe.wait_ge(*s.ada_used.at(used - 3 + n // 4))
                        for half in (0, P // 2):
                            c0 = (n % 4) * P + half
                            last = mm(ps[half:half + P // 2, bank, n:n + 1], partial[:, n // 4, c0:c0 + P // 2],
                                      ones[:, 0:1], start=True, stop=True)
                    last.then_inc(s.mod_summed.sem, 1)

                def sum_over_channels(dst, src, chunks):
                    for c in range(chunks):
                        last = mm(dst, ones, src[:, c, :], start=c == 0, stop=c == chunks - 1)
                    return last

                def index_unit(t):
                    n = (t + 1) * P
                    for h in range(IH):
                        q = slice(ID * (h % 4), ID * (h % 4 + 1))
                        last = mm(ps[:, 4 + h % 4, (h // 4) * n:(h // 4 + 1) * n],
                                  turned[q, IQT + h // 4, t * P:(t + 1) * P], turned[q, IKT, 0:n],
                                  start=True, stop=True)
                    last.then_inc(s.index_done.sem, 1)

                def attention_unit(t, half):
                    n = (t + 1) * P
                    for h in (range(HEADS) if t == 0 else range(4 * half, 4 * half + 4)):
                        q = slice(HD * (h % 2), HD * (h % 2 + 1))
                        at = h // 2 if t == 0 else h // 2 % 2
                        last = mm(ps[:, 4 + h % 2, at * n:(at + 1) * n],
                                  turned[q, QT + h // 2, t * P:(t + 1) * P], turned[q, KT, 0:n],
                                  start=True, stop=True)
                    last.then_inc(s.att_done.sem, 1)

                if l == 0:
                    sum_modulation(2, partial_first, 4)
                pe.wait_ge(*s.sq_ready.at(1))
                sum_over_channels(ps[:, 7, 0:T], square, DC).then_inc(s.ssq_ready.sem, 1)

                run_block()
                run_block()
                run_block()
                pe.wait_ge(*s.index_rotated.at(1))
                pe.wait_ge(*s.q_rotated.at(1))
                groups = ((("i", 0), ("i", 1)), (("i", 2), ("q", 4)), (("q", 0), ("q", 1)), (("q", 2), ("q", 3)))
                for g, group in enumerate(groups):
                    if g == 3:
                        pe.wait_ge(*s.turn_kept.at(1))
                    for half, (kind, n) in enumerate(group):
                        for t in range(TC):
                            src = ir[:, t, 4 * n:4 * n + 4, :] if kind == "i" else qr[:, t, 2 * n:2 * n + 2, :]
                            o = half * T + t * P
                            last = turn(ps[:, 4 + g % 3, o:o + P], src.rearrange("p h d -> p (h d)"))
                    last.then_inc(s.turn_done.sem, 1)
                pe.wait_ge(*s.turn_kept.at(4))
                index_unit(0)
                run_block()
                pe.wait_ge(*s.index_kept.at(1))
                index_unit(1)
                run_block()
                pe.wait_ge(*s.index_kept.at(2))
                sum_modulation(6, partial_early, n_ada + 4)
                attention_unit(0, 0)
                pe.wait_ge(*s.att_masked.at(1))
                attention_unit(1, 0)
                run_block()
                pe.wait_ge(*s.att_masked.at(2))
                attention_unit(1, 1)
                run_block()

                pe.wait_ge(*s.att_exp.at(8))
                for g in range(2):
                    for i in range(4):
                        last = turn(ps[:, 6 + g, i * P:(i + 1) * P], scores0[:, 4 * g + i, :])
                    last.then_inc(s.prob_turned.sem, 1)
                pe.wait_ge(*s.prob_kept.at(2))
                pe.wait_ge(*s.att_masked.at(3))
                for h in range(HEADS):
                    last = mm(ps[:, 4, h * HD:(h + 1) * HD], probsT[:, h, 0:P], kvi[:, 0, HD:2 * HD],
                              start=True, stop=True)
                last.then_inc(s.pv_done.sem, 1)
                pe.wait_ge(*s.att_exp.at(16))
                for g in range(4):
                    if g >= 2:
                        pe.wait_ge(*s.prob_kept.at(2 + g - 1))
                    for i in range(2):
                        for sc in range(TC):
                            last = turn(ps[:, 6 + g % 2, (2 * i + sc) * P:(2 * i + sc + 1) * P],
                                        scores[:, 2 * g + i, sc * P:(sc + 1) * P])
                    last.then_inc(s.prob_turned.sem, 1)
                pe.wait_ge(*s.prob_kept.at(6))
                for h in range(HEADS):
                    for sc in range(TC):
                        last = mm(ps[:, 5, h * HD:(h + 1) * HD], probsT[:, h, sc * P:(sc + 1) * P],
                                  kvi[:, sc, HD:2 * HD], start=sc == 0, stop=sc == TC - 1)
                last.then_inc(s.pv_done.sem, 1)
                run_block()

                pe.wait_ge(*s.attn_ready.at(2))
                for c in range(4):
                    for t in range(TC):
                        last = turn(ps[:, 6 + c // 2, (c % 2) * T + t * P:(c % 2) * T + (t + 1) * P],
                                    attn[:, t, 2 * c:2 * c + 2, :].rearrange("p h d -> p (h d)"))
                last.then_inc(s.attn_turned.sem, 1)
                pe.wait_ge(*s.attn_kept.at(1))
                pe.wait_ge(*s.block_kept.at(len(BLOCKS)))
                wt = item(4)
                for n in range(DC):
                    for c in range(4):
                        last = mm(ps[:, n // 2, (n % 2) * T:(n % 2 + 1) * T], wt[:, c, n * P:(n + 1) * P],
                                  attnT[:, c, :], start=c == 0, stop=c == 3)
                    if n % 2 and n < DC - 1:
                        last.then_inc(s.ya_done.sem, 1)
                last.then_inc(s.item_used.sem, 1)

                pe.wait_ge(*s.conv_ready.at(1))
                sum_over_channels(ps[:, 7, 0:T], ca, CC).then_inc(s.mean_ready.sem, 1)
                pe.wait_ge(*s.ln_sq_ready.at(1))
                sum_over_channels(ps[:, 7, T:2 * T], ca, CC).then_inc(s.var_ready.sem, 1)
                pe.wait_ge(*s.conv_act_ready.at(CC))
                wt = item(4)
                for n in range(DC):
                    for c in range(4):
                        last = mm(ps[:, 4 + n // 2, (n % 2) * T:(n % 2 + 1) * T], wt[:, c, n * P:(n + 1) * P],
                                  ca[:, c, :], start=c == 0, stop=c == 3)
                    if n % 2 and n < DC - 1:
                        last.then_inc(s.yc_done.sem, 1)
                last.then_inc(s.item_used.sem, 1)

                pe.wait_ge(*s.ya_used.at(4))
                for n in range(DC):
                    if n % 4 == 0:
                        wt = item(DC)
                    for c in range(DC):
                        if n == 0:
                            pe.wait_ge(*s.merged_ready.at(c // 2 + 1))
                        last = mm(ps[:, n // 2, (n % 2) * T:(n % 2 + 1) * T],
                                  wt[:, c, (n % 4) * P:(n % 4 + 1) * P], merged[:, c, :],
                                  start=c == 0, stop=c == DC - 1)
                    if n % 4 == 3:
                        last.then_inc(s.item_used.sem, 1)
                    elif n % 2:
                        last.then_inc(s.out_done.sem, 1)

                sum_modulation(4, partial_late, n_ada + 8)

                pe.wait_ge(*s.sq_ready.at(2))
                sum_over_channels(ps[:, 7, 0:T], square2, DC).then_inc(s.ssq_ready.sem, 1)
                if l + 1 < DEPTH:
                    sum_modulation(5, partial_next, n_ada + 12)
                pe.wait_ge(*s.h_ready.at(2 * DC))
                for t in range(TC):
                    for c in range(DC):
                        last = mm(ps[:, 4, t * (GROUPS + NE):(t + 1) * (GROUPS + NE)], hT[:, c, t * P:(t + 1) * P],
                                  w_route[:, l, c, :], start=c == 0, stop=c == DC - 1)
                last.then_inc(s.logits_done.sem, 1)
                for g in range(4):
                    t, half = g // 2, g % 2
                    for i in range(4):
                        last = turn(ps[:, g, i * P:(i + 1) * P], hT[:, 4 * half + i, t * P:(t + 1) * P])
                    last.then_inc(s.hn_turned.sem, 1)
                pe.wait_ge(*s.member_ready.at(1))
                mm(ps[:, 5, 0:NE], before, member[:, 0, :], start=True, stop=True)
                mm(ps[:, 5, NE:2 * NE], ones, member[:, 0, :], start=True, stop=False)
                mm(ps[:, 5, NE:2 * NE], before, member[:, 1, :], start=False, stop=True)
                mm(ps[:, 5, 2 * NE:3 * NE], ones, member[:, 0, :], start=True, stop=False)
                mm(ps[:, 5, 2 * NE:3 * NE], ones, member[:, 1, :], start=False, stop=True).then_inc(s.rank_done.sem, 1)
                pe.wait_ge(*s.hn_kept.at(4))
                pe.wait_ge(*s.onehot_ready.at(TC))
                for c in range(DC):
                    if c >= 4:
                        pe.wait_ge(*s.sorted_kept.at(c - 3))
                    for t in range(TC):
                        last = mm(ps[:, c % 4, :], hn[:, t, c:D:DC], onehot[:, t, :], start=t == 0, stop=t == TC - 1)
                    last.then_inc(s.sorted_done.sem, 1)
                pe.wait_ge(*s.weighted_ready.at(TC))
                for j in range(4):
                    for t in range(TC):
                        last = turn(ps[:, 6 + j // 2, (j % 2) * T + t * P:(j % 2) * T + (t + 1) * P],
                                    weighted[:, t, j * P:(j + 1) * P])
                last.then_inc(s.spread_turned.sem, 1)

                def gate_up(slot, x_block, bank):
                    for half, wt in enumerate((expert_gate(slot), expert_up(slot))):
                        for f in range(FC):
                            o = (half * FC + f) * BLK
                            for c in range(DC):
                                last = mm(ps[:, bank, o:o + BLK], wt[:, c, f * P:(f + 1) * P], x_block[:, c, :],
                                          start=c == 0, stop=c == DC - 1)
                    return last

                def down(slot, h_block, bank):
                    wt = expert_down(slot)
                    for c in range(DC):
                        for f in range(FC):
                            last = mm(ps[:, bank + c // 4, c % 4 * BLK:(c % 4 + 1) * BLK], wt[:, f, c * P:(c + 1) * P],
                                      h_block[:, f, :], start=f == 0, stop=f == FC - 1)
                    return last

                pe.wait_ge(*s.sorted_kept.at(DC))
                pe.wait_ge(*s.offs_ready.at(1))
                big = pe.value_load(flag[0:1, l:l + 1], min_val=0, max_val=1)
                with pe.If(big == 0):
                    def step_up(e, r, j):
                        pe.wait_ge(expert_in[l][j % NEXP], (r + j // NEXP) * 48 + 48)
                        pe.wait_ge(*s.xe_ready.at(e + 1))
                        if not isinstance(e, int) or e >= 2:
                            pe.wait_ge(*s.hid_ready.at(e - 1))
                        gate_up(j % NEXP, xe[:, j % 2], j % 2).then_inc(s.gu_done.sem, 1)

                    def step_down(e, j):
                        pe.wait_ge(*s.hid_ready.at(e + 1))
                        if not isinstance(e, int) or e >= 2:
                            pe.wait_ge(*s.y_stored.at(e - 1))
                        down(j, hid[:, j % 2], 2 + 2 * (j % 2)).then_inc(s.expert_used.sem, 1)

                    step_up(0, 0, 0)
                    for j in range(NEXP):
                        step_up(j + 1, 0, j + 1)
                        step_down(j, j)
                    with pe.Fori(1, NE // NEXP - 1) as r:
                        for j in range(NEXP):
                            step_up(r * NEXP + j + 1, r, j + 1)
                            step_down(r * NEXP + j, j)
                    for j in range(NEXP):
                        if j < NEXP - 1:
                            step_up(NE - NEXP + j + 1, NE // NEXP - 1, j + 1)
                        step_down(NE - NEXP + j, j)
                with pe.Else():
                    pe.sem_inc(s.gu_slow.sem, 1)
                    with pe.Fori(0, NE // NEXP) as r:
                        for j in range(NEXP):
                            def run_slow(n, used):
                                pe.wait_ge(expert_in[l][j], r * 48 + 48)
                                pe.wait_ge(*s.xe_slow.at(n + 1))
                                gate_up(j, xe[:, 0], 0).then_inc(s.gu_slow.sem, 1)
                                pe.wait_ge(*s.hid_slow.at(n + 1))
                                pe.wait_ge(*s.y_slow.at(n + 1))
                                down(j, hid[:, 0], 2).then_inc(used.sem, 1)

                            with pe.Fori(0, NBLK - 1) as b:
                                run_slow((r * NEXP + j) * NBLK + b, s.down_slow)
                            run_slow((r * NEXP + j) * NBLK + NBLK - 1, s.expert_used)

                pe.wait_ge(*s.experts_done.at(1))
                pe.wait_ge(*s.spread_kept.at(1))
                for g in range(8):
                    j, half = g // 2, g % 2
                    if g >= 4:
                        pe.wait_ge(*s.made_kept.at(g - 3))
                    for i in range(4):
                        last = turn(ps[:, 4 + g % 4, i * P:(i + 1) * P], made[:, 4 * half + i, j * P:(j + 1) * P])
                    last.then_inc(s.made_turned.sem, 1)
                for c in range(DC):
                    for j in range(4):
                        if c == 0:
                            pe.wait_ge(*s.made_kept.at(2 * j + 2))
                        last = mm(ps[:, c // 2, (c % 2) * T:(c % 2 + 1) * T], made_n[:, j, c * P:(c + 1) * P],
                                  spread[:, j, :], start=j == 0, stop=j == 3)
                    if c % 2:
                        last.then_inc(s.final_done.sem, 1)

            pe.wait_ge(*sig[DEPTH - 1].x_ready.at(3))
            for g in range(4):
                t, half = g // 2, g % 2
                for i in range(4):
                    last = turn(ps[:, 4 + g, i * P:(i + 1) * P], xT[:, 4 * half + i, t * P:(t + 1) * P])
                last.then_inc(y_turned, 1)

        @block.gpsimd
        def _(pool):
            for l in range(DEPTH):
                pool.dma_start(qk_gain[:, l, 0:HEADS, :],
                               w["q_norm_g"][l:l + 1, :].unsqueeze(1).to_broadcast([P, HEADS, HD])).then_inc(small_in, 16)
                pool.dma_start(qk_gain[:, l, HEADS, :], w["k_norm_g"][l:l + 1, :].to_broadcast([P, HD])).then_inc(small_in, 16)
                pool.dma_start(w_route[:, l, :, 0:GROUPS],
                               w["w_group"][l].rearrange("(c p) n -> p c n", p=P)).then_inc(small_in, 16)
                pool.dma_start(w_route[:, l, :, GROUPS:],
                               w["w_router"][l].rearrange("(c p) n -> p c n", p=P)).then_inc(small_in, 16)
                pool.dma_start(b_route[:, l, 0:GROUPS], w["b_group"][l:l + 1, :].to_broadcast([P, GROUPS])).then_inc(small_in, 16)
                pool.dma_start(b_route[:, l, GROUPS:], w["b_router"][l:l + 1, :].to_broadcast([P, NE])).then_inc(small_in, 16)
            for l in range(DEPTH):
                s = sig[l]
                pool.wait_ge(*s.x_ready.at(1))
                pool.memset(pad[:, :, 0:TAPS - 1], 0.0).then_inc(s.pad_zero.sem, 1)
                pool.wait_ge(*s.ssq_ready.at(2))
                pool.wait_ge(*s.mod_summed.at(2 + (l == 0) + (l + 1 < DEPTH)))
                pool.memset(sorted_x[:, :, PAIRS:PADDED], 0.0).then_inc(s.tail_zero.sem, 1)
                pool.wait_ge(*s.tail_zero.at(1))
                pool.wait_ge(*s.offs_ready.at(1))
                pool.wait_ge(*s.sorted_kept.at(DC))
                big = pool.value_load(flag[0:1, l:l + 1], min_val=0, max_val=1)
                starts = offs[0:1, l].rearrange("q b e -> q (b e)")

                def gather(n, buffer, ready):
                    at = pool.value_load(starts[0:1, bass.ds(n, 1)], min_val=0, max_val=PAIRS)
                    pool.tensor_copy(xe[:, buffer], sorted_x[:, :, bass.ds(at, BLK)]).then_inc(ready.sem, 1)

                with pool.If(big == 0):
                    for e in range(2):
                        gather(e, e, s.xe_ready)
                    with pool.Fori(1, NE // 2) as r:
                        for j in range(2):
                            pool.wait_ge(*s.gu_done.at(r * 2 + j - 1))
                            gather(r * 2 + j, j, s.xe_ready)
                with pool.Else():
                    with pool.Fori(0, NE) as e:
                        for b in range(NBLK):
                            pool.wait_ge(*s.gu_slow.at(e * NBLK + b + 1))
                            gather(e + b * NE, 0, s.xe_slow)

        @block.scalar
        def _(act):
            activate = nc.scalar.activation
            act.dma_start(const[:, :], constants).then_inc(const_in, 16)
            for l in range(DEPTH):
                for name, (r0, r1) in ROWS.items():
                    src = w[name][0] if name == "c" else w[name][l]
                    act.dma_start(stage[r0:r1, l, :], src.rearrange("(r q) -> r q", q=P)).then_inc(stage_in, 16)
                act.dma_start(stage_taps[:, l, :],
                              w["conv_w"][l].rearrange("k (c q) -> (k c) q", q=P)).then_inc(stage_in, 16)
            act.dma_start(x_nat, w["x"][0].rearrange("(t p) d -> p t d", p=P)).then_inc(x_in, 16)
            act.wait_ge(vec_kept, 2)
            activate(silu_c[:, :], row(0, "c"), ACT.Silu).then_inc(silu_c_ready, 1)

            for l in range(DEPTH):
                s = sig[l]
                at = Place()

                def keep_block():
                    j = at.block
                    at.block += 1
                    b, bank = BLOCKS[j], 2 * (j % 2)
                    act.wait_ge(*s.item_used.at(j + 1))
                    pair = ps[:, bank:bank + 2, :].rearrange("p b (n t) -> p (b n) t", t=T)
                    if b == "KVI":
                        nc.scalar.copy(qk[:, :, HEADS, :], ps[:, bank:bank + 2, 0:HD])
                        last = nc.scalar.copy(kvi, ps[:, bank:bank + 2, 0:N_KVI])
                    elif b == "Q":
                        last = nc.scalar.copy(qk[:, :, 0:HEADS, :].rearrange("p t h d -> p t (h d)"),
                                              ps[:, bank:bank + 2, :])
                    elif b == "CA":
                        last = nc.scalar.copy(ca, pair)
                    elif b == "CB":
                        last = activate(cb, pair, ACT.Sigmoid)
                    else:
                        g = j - 4
                        last = activate(gates[:, g // 2, 4 * (g % 2):4 * (g % 2) + 4, :], pair, ACT.Sigmoid)
                    last.then_inc(s.block_kept.sem, 1)

                def norm(n, sq, shift):
                    act.wait_ge(*s.x_ready.at(n))
                    activate(sq, xT[:, :, :], ACT.Square).then_inc(s.sq_ready.sem, 1)
                    act.wait_ge(*s.ssq_ready.at(n))
                    activate(std[:, :], ps[:, 7, 0:T], ACT.Sqrt, bias=eps, scale=1.0 / D).then_inc(s.std_ready.sem, 1)
                    for c in range(DC):
                        act.wait_ge(*s.scaled.at(DC * (n - 1) + c + 1))
                        activate(hT[:, c, :], hT[:, c, :], ACT.Identity,
                                 bias=modulation(l, shift)[:, c:c + 1]).then_inc(s.h_ready.sem, 1)

                act.wait_ge(const_in, 16)
                norm(1, square, SHIFT1)
                keep_block()
                keep_block()
                act.wait_ge(*s.q_rms_ready.at(1))
                activate(rms, sumsq, ACT.Sqrt, bias=eps, scale=1.0 / HD).then_inc(s.q_std_ready.sem, 1)
                keep_block()
                for g in range(4):
                    act.wait_ge(*s.turn_done.at(g + 1))
                    nc.scalar.copy(turned[:, 2 * (0, 1, 2, 3)[g]:2 * (0, 1, 2, 3)[g] + 2, :],
                                   ps[:, 4 + g % 3, :].rearrange("p (n t) -> p n t", t=T)).then_inc(s.turn_kept.sem, 1)

                def keep_index(u):
                    act.wait_ge(*s.index_done.at(u + 1))
                    n = (u + 1) * P
                    if u == 1:
                        act.wait_ge(*s.index_read.at(1))
                    activate(scores[:, :, 0:n].rearrange("p (b g) s -> p b g s", g=2),
                             ps[:, 4:8, 0:2 * n].rearrange("p b (g s) -> p b g s", s=n),
                             ACT.Relu).then_inc(s.index_kept.sem, 1)

                def exponentials(u):
                    act.wait_ge(*s.att_max.at(u + 1))
                    for h in (range(HEADS) if u == 0 else range(4 * (u - 1), 4 * u)):
                        tile = scores0[:, h, :] if u == 0 else scores[:, h, :]
                        i = (HEADS if u else 0) + h
                        activate(tile, tile, ACT.Exp, bias=rowmax[:, i:i + 1],
                                 accum_out=rowsum[:, i:i + 1]).then_inc(s.att_exp.sem, 1)

                keep_index(0)
                keep_block()
                keep_index(1)
                keep_block()
                exponentials(0)
                keep_block()
                exponentials(1)
                exponentials(2)
                keep_block()
                for g in range(2):
                    act.wait_ge(*s.prob_turned.at(g + 1))
                    nc.scalar.copy(probsT[:, 4 * g:4 * g + 4, 0:P],
                                   ps[:, 6 + g, :].rearrange("p (h t) -> p h t", t=P)).then_inc(s.prob_kept.sem, 1)
                act.wait_ge(*s.pv_done.at(1))
                for g in range(4):
                    act.wait_ge(*s.prob_turned.at(2 + g + 1))
                    nc.scalar.copy(probsT[:, 2 * g:2 * g + 2, :],
                                   ps[:, 6 + g % 2, :].rearrange("p (h t) -> p h t", t=T)).then_inc(s.prob_kept.sem, 1)
                keep_block()
                act.wait_ge(*s.attn_turned.at(1))
                nc.scalar.copy(attnT, ps[:, 6:8, :].rearrange("p b (n t) -> p (b n) t", t=T)).then_inc(s.attn_kept.sem, 1)

                act.wait_ge(*s.centred.at(1))
                activate(ca, cb, ACT.Square).then_inc(s.ln_sq_ready.sem, 1)
                act.wait_ge(*s.var_ready.at(1))
                activate(std[:, :], ps[:, 7, T:2 * T], ACT.Sqrt, bias=eps, scale=1.0 / CH).then_inc(s.ln_std_ready.sem, 1)
                act.wait_ge(*s.ln_ready.at(1))
                for c in range(CC):
                    activate(ca[:, c, :], cb[:, c, :], ACT.Silu, bias=row(l, "conv_ln_b")[:, c:c + 1],
                             scale=row(l, "conv_ln_g")[:, c:c + 1]).then_inc(s.conv_act_ready.sem, 1)

                norm(2, square2, SHIFT2)
                for g in range(4):
                    act.wait_ge(*s.hn_turned.at(g + 1))
                    nc.scalar.copy(hn[:, g // 2, (g % 2) * 512:(g % 2 + 1) * 512], ps[:, g, :]).then_inc(s.hn_kept.sem, 1)
                act.wait_ge(*s.group_shifted.at(1))
                activate(g_exp, g_shift, ACT.Exp).then_inc(s.group_exp.sem, 1)
                act.wait_ge(*s.gap_ready.at(1))
                activate(gap_exp, gap, ACT.Exp).then_inc(s.gap_exp.sem, 1)
                for c in range(DC):
                    act.wait_ge(*s.sorted_done.at(c + 1))
                    nc.scalar.copy(sorted_x[:, c, 0:PAIRS], ps[:, c % 4, :]).then_inc(s.sorted_kept.sem, 1)
                act.wait_ge(*s.offs_ready.at(1))
                act.wait_ge(*s.weighted_ready.at(TC))
                big = act.value_load(flag[0:1, l:l + 1], min_val=0, max_val=1)
                starts = offs[0:1, l].rearrange("q b e -> q (b e)")

                def store(n, bank):
                    at = act.value_load(starts[0:1, bass.ds(n, 1)], min_val=0, max_val=PAIRS)
                    return nc.scalar.copy(made[:, :, bass.ds(at, BLK)],
                                          ps[:, bank:bank + 2, :].rearrange("p b (c s) -> p (b c) s", s=BLK))

                with act.If(big == 0):
                    act.preload_act_table(ACT.Silu)

                    def step(e, j):
                        act.wait_ge(*s.gu_done.at(e + 1))
                        if not isinstance(e, int) or e >= 2:
                            act.wait_ge(*s.hid_ready.at(e - 1))
                        activate(act_g[:, j % 2, :], ps[:, j % 2, 0:FC * BLK], ACT.Silu).then_inc(s.act_ready.sem, 1)

                    def step_store(e, j):
                        act.wait_ge(*s.expert_used.at(e + 1))
                        if not isinstance(e, int) or e >= 1:
                            act.wait_ge(*s.y_stored.at(e))
                        store(e, 2 + 2 * (j % 2)).then_inc(s.y_stored.sem, 1)

                    step(0, 0)
                    step(1, 1)
                    step_store(0, 0)
                    with act.Fori(1, NE // 2) as r:
                        step(r * 2, 0)
                        step_store(r * 2 - 1, 1)
                        step(r * 2 + 1, 1)
                        step_store(r * 2, 0)
                    act.wait_ge(*s.expert_used.at(NE))
                    act.wait_ge(*s.y_stored.at(NE - 1))
                    store(NE - 1, 4).then_inc(s.experts_done.sem, 1)
                with act.Else():
                    act.preload_act_table(ACT.Silu)
                    act.sem_inc(s.y_slow.sem, 1)

                    def step_slow(e, b):
                        n = e * NBLK + b
                        act.wait_ge(*s.gu_slow.at(n + 2))
                        activate(act_g[:, 0, :], ps[:, 0, 0:FC * BLK], ACT.Silu).then_inc(s.act_slow.sem, 1)
                        if b < NBLK - 1:
                            act.wait_ge(*s.down_slow.at(e * (NBLK - 1) + b + 1))
                        else:
                            act.wait_ge(*s.expert_used.at(e + 1))
                        act.wait_ge(*s.y_slow.at(n + 1))
                        return store(e + b * NE, 2)

                    with act.Fori(0, NE - 1) as e:
                        for b in range(NBLK):
                            step_slow(e, b).then_inc(s.y_slow.sem, 1)
                    for b in range(NBLK):
                        step_slow(NE - 1, b).then_inc((s.y_slow if b < NBLK - 1 else s.experts_done).sem, 1)

                for g in range(8):
                    act.wait_ge(*s.made_turned.at(g + 1))
                    nc.scalar.copy(made_n[:, g // 2, (g % 2) * 512:(g % 2 + 1) * 512],
                                   ps[:, 4 + g % 4, :]).then_inc(s.made_kept.sem, 1)

            for g in range(4):
                act.wait_ge(y_turned, g + 1)
                nc.scalar.copy(y_nat[:, g // 2, (g % 2) * 512:(g % 2 + 1) * 512], ps[:, 4 + g, :]).then_inc(y_kept, 1)

        @block.vector
        def _(dve):
            v = nc.vector
            n_step = Place()

            def mark(ins):
                n_step.n += 1
                ins.then_inc(dve_step, 1)
                return n_step.n

            def sync():
                dve.wait_ge(dve_step, n_step.n)

            def do(ins):
                mark(ins)
                sync()

            tt, ts, stt, red = v.tensor_tensor, v.tensor_scalar, v.scalar_tensor_tensor, v.tensor_reduce

            dve.wait_ge(const_in, 16)
            dve.wait_ge(vec_turned, 1)
            v.tensor_copy(vec[:, :, :], ps[:, 0, 0:256].rearrange("p (l r) -> p l r", l=DEPTH)[:, :, 0:N_ROWS]).then_inc(vec_kept, 1)
            v.tensor_copy(taps[:, :, :, :].rearrange("p l k c -> p l (k c)"),
                          ps[:, 0, 256:512].rearrange("p (l r) -> p l r", l=DEPTH)[:, :, 0:N_TAPROWS]).then_inc(vec_kept, 1)
            dve.wait_ge(vec_kept, 2)

            for l in range(DEPTH):
                s = sig[l]
                users = used_by(mixer_items(l))
                own = [i for i, (who, _) in enumerate(users) if who == "DVE"]
                at = Place()

                def ada_item(partial):
                    i, n = own[at.item], at.item
                    at.item += 1
                    dve.wait_ge(item_in[l][i % NITEM], 16 * (i // NITEM + 1))
                    wt = item_slot(i).rearrange("p (c n) -> p c n", c=DC)
                    acc = partial[:, n % 4, :]
                    do(ts(acc, wt[:, 0, :], silu_c[:, 0:1], None, ALU.mult))
                    for c in range(1, DC - 1):
                        do(stt(out=acc, in0=wt[:, c, :], scalar=silu_c[:, c:c + 1], in1=acc,
                               op0=ALU.mult, op1=ALU.add))
                    stt(out=acc, in0=wt[:, DC - 1, :], scalar=silu_c[:, DC - 1:DC], in1=acc,
                        op0=ALU.mult, op1=ALU.add).then_inc(s.ada_used.sem, 1)

                def keep_modulation(ml, third, bank, nth):
                    dve.wait_ge(*s.mod_summed.at(nth))
                    a, b = 16 * third, 16 * third + 16
                    do(tt(mod[:, ml, a:b], ps[:, bank, 0:16], row(ml, "b_ada")[:, a:b], ALU.add))

                def gains(n, scale, g):
                    return stt(out=gain[:, l, n, :], in0=modulation(l, scale), scalar=1.0, in1=row(l, g),
                               op0=ALU.add, op1=ALU.mult)

                def norm(n):
                    dve.wait_ge(*s.std_ready.at(n))
                    do(v.reciprocal(rstd[:, :], std[:, :]))
                    for c in range(DC):
                        stt(out=hT[:, c, :], in0=xT[:, c, :], scalar=gain[:, l, n - 1, c:c + 1], in1=rstd[:, :],
                            op0=ALU.mult, op1=ALU.mult).then_inc(s.scaled.sem, 1)

                summed = 0
                if l == 0:
                    dve.wait_ge(silu_c_ready, 1)
                    ada_item(partial_first)
                    ada_item(partial_first)
                    dve.wait_ge(x_turned, 1)
                    v.tensor_copy(xT[:, :, :].rearrange("p c t -> p (c t)"),
                                  ps[:, 4:8, :].rearrange("p b n -> p (b n)")).then_inc(s.x_ready.sem, 1)
                    ada_item(partial_first)
                    ada_item(partial_first)
                    dve.wait_ge(*s.x_ready.at(1))
                    summed = 1
                    keep_modulation(0, 0, 2, summed)
                do(gains(0, SCALE1, "g_norm1"))
                norm(1)
                ada_item(partial_early)
                ada_item(partial_early)

                def rotate(dst, src, cos, sin, heads, half):
                    shape = [P, TC, heads, half]
                    cs, sn = cos.unsqueeze(2).to_broadcast(shape), sin.unsqueeze(2).to_broadcast(shape)
                    x1, x2 = src[:, :, :, 0:half], src[:, :, :, half:2 * half]
                    o1, o2 = dst[:, :, 0:heads, 0:half], dst[:, :, 0:heads, half:2 * half]
                    t1, t2 = tmp[:, :, 0:heads, 0:half], tmp[:, :, 0:heads, half:2 * half]
                    mark(tt(o1, x1, cs, ALU.mult))
                    mark(tt(o2, x2, cs, ALU.mult))
                    mark(tt(t1, x2, sn, ALU.mult))
                    mark(tt(t2, x1, sn, ALU.mult))
                    sync()
                    mark(tt(o1, o1, t1, ALU.subtract))
                    mark(tt(o2, o2, t2, ALU.add))
                    sync()

                dve.wait_ge(*s.block_kept.at(1))
                index = kvi[:, :, 2 * HD:2 * HD + (IH + 1) * ID].rearrange("p t (h d) -> p t h d", d=ID)
                iweight = kvi[:, :, N_KVI - IH:N_KVI]
                rotate(ir, index, cos_i, sin_i, IH + 1, ID // 2)
                v.tensor_copy(ir[:, :, IH + 1:IH + 4, :],
                              ir[:, :, IH:IH + 1, :].to_broadcast([P, TC, 3, ID])).then_inc(s.index_rotated.sem, 1)
                ada_item(partial_early)
                if l == 0:
                    dve.wait_ge(small_in, 16 * N_SMALL)
                dve.wait_ge(*s.block_kept.at(2))
                do(tt(tmp, qk, qk, ALU.mult))
                red(sumsq.rearrange("p (t h) -> p t h", t=TC), tmp, AX.X, ALU.add).then_inc(s.q_rms_ready.sem, 1)
                dve.wait_ge(*s.q_std_ready.at(1))
                do(v.reciprocal(rms, rms))
                do(tt(qk, qk, rms.rearrange("p (t h) -> p t h", t=TC).unsqueeze(3).to_broadcast(
                    [P, TC, HEADS + 1, HD]), ALU.mult))
                do(tt(qk, qk, qk_gain[:, l].unsqueeze(1).to_broadcast([P, TC, HEADS + 1, HD]), ALU.mult))
                rotate(qr, qk, cos_h, sin_h, HEADS + 1, HD // 2)
                v.tensor_copy(qr[:, :, HEADS + 1, :], qr[:, :, HEADS, :]).then_inc(s.q_rotated.sem, 1)
                ada_item(partial_early)

                def add_index(t, heads):
                    n = (t + 1) * P
                    acc = iscore[:, t, 0:n]
                    for h in heads:
                        at = (h % 4) * 2 + h // 4
                        if h == 0:
                            ins = ts(acc, scores[:, at, 0:n], iweight[:, t, h:h + 1], None, ALU.mult)
                        else:
                            ins = stt(out=acc, in0=scores[:, at, 0:n], scalar=iweight[:, t, h:h + 1], in1=acc,
                                      op0=ALU.mult, op1=ALU.add)
                        if h < IH - 1 or t > 0:
                            do(ins)
                        else:
                            ins.then_inc(s.index_read.sem, 1)
                            dve.wait_ge(*s.index_read.at(1))

                def select(t):
                    n = (t + 1) * P
                    work = iscore[:, t, 0:n]
                    do(stt(out=work, in0=work, scalar=ISCALE, in1=causal[:, t, 0:n], op0=ALU.mult, op1=ALU.add))
                    for _ in range(TOPK // 8):
                        do(v.max(out=top8, in_=work))
                        do(v.match_replace(out=work, in_to_replace=top8, in_values=work, imm_value=TAKEN))
                    do(ts(drop[:, t, 0:n], work, 0.5 * TAKEN, NEG, ALU.is_gt, ALU.mult))
                    do(tt(drop[:, t, 0:n], drop[:, t, 0:n], causal[:, t, 0:n], ALU.add))

                def mask(u):
                    t = 0 if u == 0 else 1
                    dve.wait_ge(*s.att_done.at(u + 1))
                    if u == 0:
                        dst, heads, n, i = scores0, HEADS, P, 0
                    else:
                        dst, heads, n, i = scores[:, 4 * (u - 1):4 * u, :], 4, T, HEADS + 4 * (u - 1)
                    stt(out=dst, in0=ps[:, 4:6, :].rearrange("p b (h s) -> p (b h) s", s=n), scalar=HD ** -0.5,
                        in1=drop[:, t, 0:n].unsqueeze(1).to_broadcast([P, heads, n]),
                        op0=ALU.mult, op1=ALU.add).then_inc(s.att_masked.sem, 1)
                    dve.wait_ge(*s.att_masked.at(u + 1))
                    red(rowmax[:, i:i + heads], dst, AX.X, ALU.max, negate=True).then_inc(s.att_max.sem, 1)

                at_tap = {}

                def convolve(a, b):
                    for tap in range(a, b):
                        for c in range(CC):
                            src, wt = pad[:, c, tap:tap + T], taps[:, l, tap, c:c + 1]
                            if tap == 0:
                                ins = ts(ca[:, c, :], src, wt, row(l, "conv_b")[:, c:c + 1], ALU.mult, ALU.add)
                            else:
                                dve.wait_ge(dve_step, at_tap[c])
                                ins = stt(out=ca[:, c, :], in0=src, scalar=wt, in1=ca[:, c, :],
                                          op0=ALU.mult, op1=ALU.add)
                            at_tap[c] = mark(ins)

                def normalise(t):
                    dve.wait_ge(*s.pv_done.at(t + 1))
                    do(v.reciprocal(rowinv[:, 8 * t:8 * t + 8], rowsum[:, 8 * t:8 * t + 8]))
                    units = 1 if t == 0 else 2
                    n = HEADS // units
                    for u in range(units):
                        last = tt(attn[:, t, u * n:(u + 1) * n, :].rearrange("p (c q) d -> p q c d", q=2),
                                  ps[:, 4 + t, u * n * HD:(u + 1) * n * HD].rearrange("p (q c d) -> p q c d", q=2, d=HD),
                                  rowinv[:, 8 * t + u * n:8 * t + (u + 1) * n].rearrange("p (q c) -> p q c", q=2)
                                  .unsqueeze(3).to_broadcast([P, 2, n // 2, HD]), ALU.mult)
                        if u < units - 1:
                            mark(last)
                    last.then_inc(s.attn_ready.sem, 1)

                dve.wait_ge(*s.index_kept.at(1))
                add_index(0, range(IH))
                select(0)
                dve.wait_ge(*s.block_kept.at(4))
                dve.wait_ge(*s.pad_zero.at(1))
                mark(tt(pad[:, :, TAPS - 1:], ca, cb, ALU.mult))
                dve.wait_ge(*s.index_kept.at(2))
                add_index(1, range(IH))
                select(1)
                keep_modulation(l, 1, 6, summed + 1)
                mask(0)
                mask(1)
                convolve(0, 12)
                mask(2)
                convolve(12, 22)
                normalise(0)
                normalise(1)
                convolve(22, TAPS - 1)
                for c in range(CC):
                    dve.wait_ge(dve_step, at_tap[c])
                    src, wt = pad[:, c, TAPS - 1:], taps[:, l, TAPS - 1, c:c + 1]
                    ins = stt(out=ca[:, c, :], in0=src, scalar=wt, in1=ca[:, c, :], op0=ALU.mult, op1=ALU.add)
                    if c < CC - 1:
                        mark(ins)
                    else:
                        ins.then_inc(s.conv_ready.sem, 1)
                sync()

                dve.wait_ge(*s.mean_ready.at(1))
                dve.wait_ge(*s.conv_ready.at(1))
                stt(out=cb, in0=ps[:, 7, 0:T].unsqueeze(1).to_broadcast([P, CC, T]), scalar=-1.0 / CH, in1=ca,
                    op0=ALU.mult, op1=ALU.add).then_inc(s.centred.sem, 1)
                dve.wait_ge(*s.ln_std_ready.at(1))
                do(v.reciprocal(rstd[:, :], std[:, :]))
                tt(cb, cb, rstd[:, :].unsqueeze(1).to_broadcast([P, CC, T]), ALU.mult).then_inc(s.ln_ready.sem, 1)

                dve.wait_ge(*s.block_kept.at(len(BLOCKS)))
                for p in range(4):
                    if p < 3:
                        dve.wait_ge(*s.ya_done.at(p + 1))
                    else:
                        dve.wait_ge(*s.item_used.at(N_OUT - 1))
                    g = gates[:, 1, 2 * p:2 * p + 2, :]
                    tt(g, ps[:, p, :].rearrange("p (n t) -> p n t", t=T), g, ALU.mult).then_inc(s.ya_used.sem, 1)
                for p in range(4):
                    if p < 3:
                        ada_item(partial_late)
                    if p < 3:
                        dve.wait_ge(*s.yc_done.at(p + 1))
                    else:
                        dve.wait_ge(*s.item_used.at(N_OUT))
                    for n in range(2):
                        c = 2 * p + n
                        mark(stt(out=gates[:, 0, c, :], in0=ps[:, 4 + p, n * T:(n + 1) * T],
                                 scalar=row(l, "b_conv_out")[:, c:c + 1], in1=gates[:, 0, c, :],
                                 op0=ALU.add, op1=ALU.mult))
                    sync()
                    dve.wait_ge(*s.ya_used.at(p + 1))
                    tt(merged[:, 2 * p:2 * p + 2, :], gates[:, 0, 2 * p:2 * p + 2, :],
                       gates[:, 1, 2 * p:2 * p + 2, :], ALU.add).then_inc(s.merged_ready.sem, 1)
                ada_item(partial_late)
                if l + 1 < DEPTH:
                    for _ in range(4):
                        ada_item(partial_next)
                for c in range(DC):
                    if c % 4 == 1 or c % 4 == 0:
                        dve.wait_ge(*s.out_done.at(c // 4 + 1))
                    else:
                        dve.wait_ge(*s.item_used.at(N_OUT + 1 + c // 4))
                    ins = stt(out=xT[:, c, :], in0=ps[:, c // 2, (c % 2) * T:(c % 2 + 1) * T],
                              scalar=modulation(l, GATE1)[:, c:c + 1], in1=xT[:, c, :], op0=ALU.mult, op1=ALU.add)
                    if c < DC - 1:
                        mark(ins)
                    else:
                        sync()
                        ins.then_inc(s.x_ready.sem, 1)

                dve.wait_ge(*s.x_ready.at(2))
                keep_modulation(l, 2, 4, summed + 2)
                do(gains(1, SCALE2, "g_norm2"))
                norm(2)
                if l + 1 < DEPTH:
                    keep_modulation(l + 1, 0, 5, summed + 3)
                dve.wait_ge(*s.logits_done.at(1))
                W = GROUPS + NE
                do(tt(logits, ps[:, 4, 0:TC * W].rearrange("p (t n) -> p t n", n=W),
                      b_route[:, l].unsqueeze(1).to_broadcast([P, TC, W]), ALU.add))
                g_log = logits[:, :, 0:GROUPS]

                def over(x, n):
                    return x.unsqueeze(2).to_broadcast([P, TC, n])

                def first_of(dst, eq, n, best):
                    do(tt(eq, eq, falling[:, 0:n].unsqueeze(1).to_broadcast([P, TC, n]), ALU.mult))
                    do(red(best, eq, AX.X, ALU.max))
                    return tt(dst, eq, over(best, n), ALU.is_equal)

                do(red(g_max, g_log, AX.X, ALU.max))
                tt(g_shift3, g_log, over(g_max, GROUPS), ALU.subtract).then_inc(s.group_shifted.sem, 1)
                do(tt(g_one, g_log, over(g_max, GROUPS), ALU.is_equal))
                do(first_of(g_one, g_one, GROUPS, best))
                do(ts(g_one, g_one, -1.0, -NEG, ALU.add, ALU.mult))
                do(tt(e_in.rearrange("p t (g e) -> p t g e", g=GROUPS),
                      logits[:, :, GROUPS:].rearrange("p t (g e) -> p t g e", g=GROUPS),
                      g_one.unsqueeze(3).to_broadcast([P, TC, GROUPS, EPG]), ALU.add))
                do(red(top_a, e_in, AX.X, ALU.max))
                do(tt(hot_a, e_in, over(top_a, NE), ALU.is_equal))
                do(first_of(hot_a, hot_a, NE, best))
                do(stt(out=e_in, in0=hot_a, scalar=2 * NEG, in1=e_in, op0=ALU.mult, op1=ALU.add))
                do(red(top_b, e_in, AX.X, ALU.max))
                do(tt(hot_b, e_in, over(top_b, NE), ALU.is_equal))
                do(first_of(hot_b, hot_b, NE, best))
                tt(member, hot_a, hot_b, ALU.add).then_inc(s.member_ready.sem, 1)
                tt(gap, top_b, top_a, ALU.subtract).then_inc(s.gap_ready.sem, 1)
                dve.wait_ge(*s.rank_done.at(1))
                counts = ps[:, 5, 2 * NE:3 * NE]
                do(v.tensor_copy(count_sb, counts))
                do(v.tensor_tensor_scan(start, ones[:, 0:NE], count_sb, 0.0, ALU.mult, ALU.add))
                do(tt(start, start, count_sb, ALU.subtract))
                for b in range(NBLK):
                    mark(ts(offs[0:1, l, b, :], start[0:1, :], float(b * BLK), float(PAIRS), ALU.add, ALU.min))
                do(red(best[0:1, 0:1], count_sb[0:1, :], AX.X, ALU.max))
                ts(flag[0:1, l:l + 1], best[0:1, 0:1], float(BLK), None, ALU.is_gt).then_inc(s.offs_ready.sem, 1)
                do(tt(place, ps[:, 5, 0:2 * NE].rearrange("p (t e) -> p t e", t=TC),
                      start.unsqueeze(1).to_broadcast([P, TC, NE]), ALU.add))
                mark(tt(hot_a, hot_a, place, ALU.mult))
                mark(tt(hot_b, hot_b, place, ALU.mult))
                sync()
                mark(red(slot_a, hot_a, AX.X, ALU.add))
                mark(red(slot_b, hot_b, AX.X, ALU.add))
                sync()
                for t in range(TC):
                    do(ts(onehot[:, t, :], iota, slot_a[:, t:t + 1], None, ALU.is_equal))
                    stt(out=onehot[:, t, :], in0=iota, scalar=slot_b[:, t:t + 1], in1=onehot[:, t, :],
                        op0=ALU.is_equal, op1=ALU.add).then_inc(s.onehot_ready.sem, 1)
                dve.wait_ge(*s.group_exp.at(1))
                do(red(best, g_exp3, AX.X, ALU.add))
                do(v.reciprocal(best, best))
                dve.wait_ge(*s.gap_exp.at(1))
                do(ts(weight_b, gap_exp, 1.0, None, ALU.add))
                do(v.reciprocal(weight_b, weight_b))
                do(tt(weight_a, best, weight_b, ALU.mult))
                do(tt(weight_b, weight_a, gap_exp, ALU.mult))
                for t in range(TC):
                    mark(ts(weighted[:, t, :], iota, slot_a[:, t:t + 1], weight_a[:, t:t + 1], ALU.is_equal, ALU.mult))
                    mark(ts(scratch[:, t, :], iota, slot_b[:, t:t + 1], weight_b[:, t:t + 1], ALU.is_equal, ALU.mult))
                    sync()
                    tt(weighted[:, t, :], weighted[:, t, :], scratch[:, t, :], ALU.add).then_inc(s.weighted_ready.sem, 1)
                dve.wait_ge(*s.spread_turned.at(1))
                v.tensor_copy(spread.rearrange("p j t -> p (j t)"),
                              ps[:, 6:8, :].rearrange("p b n -> p (b n)")).then_inc(s.spread_kept.sem, 1)

                dve.wait_ge(*s.offs_ready.at(1))
                big = dve.value_load(flag[0:1, l:l + 1], min_val=0, max_val=1)

                def product(j, bank):
                    return tt(hid[:, j].rearrange("p f s -> p (f s)"), ps[:, bank, FC * BLK:2 * FC * BLK],
                              act_g[:, j, :], ALU.mult)

                with dve.If(big == 0):
                    for e in range(2):
                        dve.wait_ge(*s.act_ready.at(e + 1))
                        product(e, e).then_inc(s.hid_ready.sem, 1)
                    with dve.Fori(1, NE // 2) as r:
                        for j in range(2):
                            dve.wait_ge(*s.act_ready.at(r * 2 + j + 1))
                            dve.wait_ge(*s.expert_used.at(r * 2 + j - 1))
                            product(j, j).then_inc(s.hid_ready.sem, 1)
                with dve.Else():
                    with dve.Fori(0, NE * NBLK) as n:
                        dve.wait_ge(*s.act_slow.at(n + 1))
                        dve.wait_ge(*s.y_slow.at(n + 1))
                        product(0, 0).then_inc(s.hid_slow.sem, 1)

                done = sig[l + 1].x_ready if l + 1 < DEPTH else s.x_ready
                for c in range(DC):
                    dve.wait_ge(*s.final_done.at(c // 2 + 1))
                    ins = stt(out=xT[:, c, :], in0=ps[:, c // 2, (c % 2) * T:(c % 2 + 1) * T],
                              scalar=modulation(l, GATE2)[:, c:c + 1], in1=xT[:, c, :], op0=ALU.mult, op1=ALU.add)
                    if c < DC - 1:
                        mark(ins)
                    else:
                        sync()
                        ins.then_inc(done.sem, 1)
                dve.wait_ge(*done.at(1 if l + 1 < DEPTH else 3))


NAMES = ["x", "c", "w_ada", "b_ada", "g_norm1", "w_in", "q_norm_g", "k_norm_g", "conv_w", "conv_b", "conv_ln_g",
         "conv_ln_b", "w_conv_out", "b_conv_out", "w_attn_out", "w_out", "g_norm2", "w_group", "b_group",
         "w_router", "b_router", "w_gate", "w_up", "w_down"]


def shape_constants():
    import numpy as np

    f = np.float32
    table = np.zeros((P, N_CONST), f)
    i = np.arange(P)

    def put(name, value):
        table[:, CONST[name][0]:CONST[name][1]] = value

    put("ident", np.eye(P))
    put("ones", 1.0)
    put("before", i[:, None] < i[None, :])
    token = np.arange(T).reshape(TC, P)
    later = np.arange(T)[None, None, :] > token.T[:, :, None]
    put("causal", np.where(later, f(NEG), f(0)).reshape(P, TC * T))
    put("iota", np.arange(PAIRS)[None, :])
    for tag, dim in (("h", HD), ("i", ID)):
        inv = f(10000.0) ** (-np.arange(0, dim, 2, dtype=f) / f(dim))
        ang = np.arange(T, dtype=f)[:, None] * inv.astype(f)[None, :]
        for name, fn in (("cos_", np.cos), ("sin_", np.sin)):
            put(name + tag, fn(ang).astype(f).reshape(TC, P, dim // 2).transpose(1, 0, 2).reshape(P, -1))
    put("falling", np.arange(NE, 0, -1)[None, :])
    put("eps", EPS)
    return table


def kernel(**inputs):
    import numpy as np
    import concourse.bacc as bacc
    from concourse.bass_utils import run_bass_kernel_spmd as run

    nc = bacc.Bacc("TRN2", target_bir_lowering=False, num_devices=1)
    arrays, w = {}, {}
    for name in NAMES:
        a = np.ascontiguousarray(inputs[name])
        arrays[f"in_{name}"] = a
        w[name] = nc.dram_tensor(f"in_{name}", a.shape, mybir.dt.from_np(a.dtype), kind="ExternalInput").ap()
    arrays["constants"] = shape_constants()
    constants = nc.dram_tensor("constants", (P, N_CONST), F32, kind="ExternalInput").ap()
    out = nc.dram_tensor("out", (1, T, D), F32, kind="ExternalOutput").ap()
    trunk_kernel(nc, w, constants, out)
    r = run(nc, [arrays], core_ids=[0])
    return r.results[0]["out"]
```

```python
from collections import namedtuple
from contextlib import ExitStack

import concourse.bass as bass
from concourse import mybir

F32 = mybir.dt.float32
F32R = mybir.dt.float32r
I32 = mybir.dt.int32
ALU = mybir.AluOpType
ACT = mybir.ActivationFunctionType
AX = mybir.AxisListType

P = 128
D = 1024
DC = D // P
T = 256
TC = T // P
DEPTH = 2
N_MOD = 6
CH = 512
CC = CH // P
TAPS = 31
HEADS = 8
HD = 64
IH = 8
ID = 32
ISCALE = (ID ** -0.5) * (IH ** -0.5)
TOPK = 64
GROUPS = 4
EPG = 8
NE = GROUPS * EPG
FE = 256
FC = FE // P
EPS = 1e-6
NEG = -1e30
TAKEN = -3e38

COL_Q = 2 * CH
COL_K = COL_Q + HEADS * HD
COL_G = COL_K + 2 * HD + IH * ID + ID + IH
N_KVI = COL_G - COL_K
N_IN = COL_G + 2 * D

BLK = 64
NBLK = T // BLK
PAIRS = 2 * T
PADDED = PAIRS + BLK

ITEM = 4096
NITEM = 6
EXP = 6144
NEXP = 4
RING = NITEM * ITEM
assert RING == NEXP * EXP

CONST = {}
_at = 0
for _name, _n in (("ident", P), ("ones", P), ("before", P), ("fold", P), ("causal", TC * T), ("iota", PAIRS),
                  ("cos_h", TC * HD // 2), ("sin_h", TC * HD // 2), ("cos_i", TC * ID // 2),
                  ("sin_i", TC * ID // 2), ("falling", NE), ("eps", 1)):
    CONST[_name] = (_at, _at + _n)
    _at += _n
N_CONST = _at

ROWS = {}
_at = 0
for _name, _n in (("b_ada", N_MOD * DC), ("g_norm1", DC), ("g_norm2", DC), ("b_conv_out", DC),
                  ("conv_b", CC), ("conv_ln_g", CC), ("conv_ln_b", CC), ("c", DC)):
    ROWS[_name] = (_at, _at + _n)
    _at += _n
N_ROWS = _at
N_TAPROWS = TAPS * CC


class Place:

    def __init__(self):
        self.item = self.block = self.n = 0


BLOCKS = ("KVI", "Q", "CA", "CB", "G0", "G1", "G2", "G3")


def mixer_items(layer):
    def ada(third, l=layer):
        return [("ada", l, third, i) for i in range(4)]

    early = ada(1)
    late = ada(2) + (ada(0, layer + 1) if layer + 1 < DEPTH else [])
    items = ada(0) if layer == 0 else []
    items += [("in", "KVI"), early[0], ("in", "Q"), early[1], early[2], ("in", "CA"), early[3]]
    items += [("in", b) for b in BLOCKS[3:]]
    items += [late[0], ("attn_out",), ("conv_out",)] + late[1:4] + [("out", 0), ("out", 1)] + late[4:]
    return items


PE_ADA = ("ada", 0, 0, 2)


def used_by(items):
    n = {"PE": 0, "DVE": 0, "PE alone": 0}
    found = []
    for item in items:
        who = "PE alone" if item == PE_ADA else "DVE" if item[0] == "ada" else "PE"
        n[who] += 1
        found.append((who, n[who]))
    return found


N_OUT = len(BLOCKS) + 2
N_STAGE = len(ROWS) + 1
N_SMALL = DEPTH * 6


def trunk_kernel(nc, w, constants, out):
    with ExitStack() as ctx:
        def sb(name, shape, dt=F32):
            return ctx.enter_context(nc.sbuf_tensor(name, shape, dt))

        def same_memory(name, at, floats):
            return nc.alloc_sbuf_tensor_at(name, [P, floats], F32R, offset=at)[:, :]

        def next_address():
            return (nc.sbuf_base + 31) // 32 * 32

        const = sb("const", [P, N_CONST])
        ring_at = next_address()
        ring = sb("ring", [P, RING])
        xT = sb("xT", [P, DC, T])
        hT_at = next_address()
        hT = sb("hT", [P, DC, T])
        vec = sb("vec", [P, DEPTH, N_ROWS])
        taps = sb("taps", [P, DEPTH, TAPS, CC])
        silu_c = sb("silu_c", [P, DC])
        mod = sb("mod", [P, DEPTH, N_MOD * DC])
        gain = sb("gain", [P, DEPTH, 2, DC])
        qk_gain = sb("qk_gain", [P, DEPTH, HEADS + 1, HD])
        w_route = sb("w_route", [P, DEPTH, DC, GROUPS + NE])
        b_route = sb("b_route", [P, DEPTH, GROUPS + NE])
        std = sb("std", [P, T])
        rstd = sb("rstd", [P, T])

        MIX = {}
        EX = {}

        def lay(table, names, at=0):
            for name, n in names:
                table[name] = (at, at + n)
                at += n
            return at

        end_mix = lay(MIX, (("kvi", TC * N_KVI), ("qk", TC * (HEADS + 1) * HD), ("tmp", TC * (HEADS + 1) * HD),
                            ("qr", TC * (HEADS + 2) * HD), ("ir", TC * (IH + 4) * ID), ("turned", 9 * T),
                            ("scores", HEADS * T), ("probsT", HEADS * T), ("gates", 2 * DC * T),
                            ("ca", CC * T), ("cb", CC * T), ("pad", CC * (T + TAPS - 1)),
                            ("drop", TC * T), ("stat", 160)))
        end_ex = lay(EX, (("hn", TC * D), ("onehot", TC * PAIRS), ("weighted", TC * PAIRS), ("spread", 4 * T),
                          ("sorted", DC * PADDED), ("made", DC * PADDED), ("xe", 2 * DC * 2 * BLK),
                          ("rounded", 4 * 2 * FE), ("products", 2 * FE),
                          ("route", 520)))
        arena_at = next_address()
        arena = sb("arena", [P, max(end_mix, end_ex)])
        offs = sb("offs", [1, DEPTH, NBLK, NE], I32)
        flag = sb("flag", [1, DEPTH], I32)

        def mix(name):
            return arena[:, MIX[name][0]:MIX[name][1]]

        def ex(name):
            return arena[:, EX[name][0]:EX[name][1]]

        kvi = mix("kvi").rearrange("p (t n) -> p t n", t=TC)
        qk = mix("qk").rearrange("p (t h d) -> p t h d", t=TC, d=HD)
        tmp = mix("tmp").rearrange("p (t h d) -> p t h d", t=TC, d=HD)
        qr = mix("qr").rearrange("p (t h d) -> p t h d", t=TC, d=HD)
        ir = mix("ir").rearrange("p (t h d) -> p t h d", t=TC, d=ID)
        turned = mix("turned").rearrange("p (n t) -> p n t", t=T)
        IQT, QT, KT = 0, 4, (3, 8)
        scores = mix("scores").rearrange("p (h s) -> p h s", h=HEADS)
        probsT = mix("probsT").rearrange("p (h t) -> p h t", h=HEADS)
        index_kt = probsT[:, 0:4, :]
        merged = mix("scores").rearrange("p (c t) -> p c t", c=DC)
        attn = arena[:, MIX["qr"][0]:MIX["qr"][0] + TC * HEADS * HD].rearrange(
            "p (t h d) -> p t h d", t=TC, d=HD)
        attnT = arena[:, MIX["qk"][0]:MIX["qk"][0] + 4 * T].rearrange("p (c t) -> p c t", t=T)
        gates = mix("gates").rearrange("p (b c t) -> p b c t", b=2, c=DC)
        ca = mix("ca").rearrange("p (c t) -> p c t", c=CC)
        cb = mix("cb").rearrange("p (c t) -> p c t", c=CC)
        pad = mix("pad").rearrange("p (c t) -> p c t", c=CC)
        drop = mix("drop").rearrange("p (t s) -> p t s", t=TC)
        iscore = arena[:, MIX["tmp"][0]:MIX["tmp"][0] + TC * T].rearrange("p (t s) -> p t s", t=TC)
        scores0 = mix("cb").rearrange("p (h s) -> p h s", h=HEADS)
        square = hT
        st = mix("stat")
        sumsq, rms = st[:, 0:18], st[:, 18:36]
        top8 = st[:, 36:44]
        rowmax, rowsum, rowinv = st[:, 44:60], st[:, 60:76], st[:, 76:92]

        hn = ex("hn").rearrange("p (t d) -> p t d", t=TC)
        onehot = ex("onehot").rearrange("p (t s) -> p t s", t=TC)
        weighted = ex("weighted").rearrange("p (t s) -> p t s", t=TC)
        spread = ex("spread").rearrange("p (j t) -> p j t", t=T)
        sorted_x = ex("sorted").rearrange("p (c s) -> p c s", c=DC)
        made = ex("made").rearrange("p (c s) -> p c s", c=DC)
        made_n = arena[:, 0:4 * D].rearrange("p (j d) -> p j d", d=D)
        assert 4 * D <= EX["spread"][0]
        partial_first = mix("gates")[:, DC * T:].rearrange("p (i n) -> p i n", i=4)
        partial_early = mix("gates")[:, DC * T:].rearrange("p (i n) -> p i n", i=4)
        partial_late = mix("turned")[:, 0:8 * T].rearrange("p (i n) -> p i n", i=4)
        partial_next = mix("probsT").rearrange("p (i n) -> p i n", i=4)
        xe = same_memory("xe", arena_at + 4 * EX["xe"][0], 2 * DC * 2 * BLK).rearrange(
            "p (b c h s) -> p b c h s", b=2, c=DC, h=2)
        half_size = 4 * 2 * FE
        rounded = [[same_memory("rounded_0_0", arena_at + 4 * EX["rounded"][0], half_size),
                    same_memory("rounded_0_1", hT_at, half_size)],
                   [same_memory("rounded_1_0", arena_at, half_size),
                    same_memory("rounded_1_1", arena_at + 4 * half_size, half_size)]]
        hn_rounded = same_memory("hn_rounded", arena_at + 4 * (EX["made"][0] + 2 * PADDED), TC * D).rearrange(
            "p (t d) -> p t d", t=TC)
        hn_rest = same_memory("hn_rest", arena_at + 4 * EX["hn"][0], TC * D).rearrange("p (t d) -> p t d", t=TC)
        sorter = same_memory("sorter", arena_at + 4 * EX["onehot"][0], TC * PAIRS).rearrange(
            "p (t s) -> p t s", t=TC)
        rounded = [[half.rearrange("p (g c n) -> p g c n", g=2, c=4) for half in pair] for pair in rounded]
        ring_rest = same_memory("ring_rest", ring_at, RING)
        products = ex("products")
        act_g = std[:, :]
        hid = rstd[:, :].rearrange("p (f s) -> p f s", f=FC)
        rt = ex("route")
        small = {}
        end_small = lay(small, (("member", TC * NE), ("logits", TC * (GROUPS + NE)), ("g_max", TC), ("g_shift", TC * GROUPS),
                    ("g_exp", TC * GROUPS), ("g_one", TC * GROUPS), ("best", TC), ("e_in", TC * NE), ("top_a", TC),
                    ("top_b", TC), ("hot_a", TC * NE), ("hot_b", TC * NE), ("gap", TC), ("gap_exp", TC),
                    ("count", NE), ("start", NE), ("place", TC * NE), ("slot_a", TC), ("slot_b", TC),
                    ("weight_a", TC), ("weight_b", TC)))
        assert end_small <= 520

        def small_tile(name, per_token=False):
            t = rt[:, small[name][0]:small[name][1]]
            return t.rearrange("p (t e) -> p t e", t=TC) if per_token else t

        member, logits, e_in = small_tile("member", True), small_tile("logits", True), small_tile("e_in", True)
        hot_a, hot_b, place = small_tile("hot_a", True), small_tile("hot_b", True), small_tile("place", True)
        g_shift, g_exp, g_one = small_tile("g_shift"), small_tile("g_exp"), small_tile("g_one", True)
        g_shift3, g_exp3 = small_tile("g_shift", True), small_tile("g_exp", True)
        g_max, best, top_a, top_b = small_tile("g_max"), small_tile("best"), small_tile("top_a"), small_tile("top_b")
        gap, gap_exp, count_sb, start = small_tile("gap"), small_tile("gap_exp"), small_tile("count"), small_tile("start")
        slot_a, slot_b = small_tile("slot_a"), small_tile("slot_b")
        weight_a, weight_b = small_tile("weight_a"), small_tile("weight_b")
        scratch = made[:, 0:2, 0:PAIRS]
        stage = arena[0:N_ROWS, EX["sorted"][0]:EX["sorted"][0] + DEPTH * P].rearrange("r (l q) -> r l q", l=DEPTH)
        stage_taps = arena[0:N_TAPROWS, EX["sorted"][0] + 256:EX["sorted"][0] + 512].rearrange(
            "r (l q) -> r l q", l=DEPTH)
        x_nat = ex("made")[:, 0:TC * D].rearrange("p (t d) -> p t d", t=TC)
        y_nat = hT[:, :, :].rearrange("p c t -> p (c t)").rearrange("p (t d) -> p t d", t=TC)

        def k(name):
            return const[:, CONST[name][0]:CONST[name][1]]

        ident, ones, before, fold, iota = k("ident"), k("ones"), k("before"), k("fold"), k("iota")
        causal = k("causal").rearrange("p (t s) -> p t s", t=TC)
        cos_h = k("cos_h").rearrange("p (t d) -> p t d", t=TC)
        sin_h = k("sin_h").rearrange("p (t d) -> p t d", t=TC)
        cos_i = k("cos_i").rearrange("p (t d) -> p t d", t=TC)
        sin_i = k("sin_i").rearrange("p (t d) -> p t d", t=TC)
        falling, eps = k("falling"), k("eps")

        def row(layer, name):
            return vec[:, layer, ROWS[name][0]:ROWS[name][1]]

        SHIFT1, SCALE1, GATE1, SHIFT2, SCALE2, GATE2 = range(6)

        def modulation(layer, which):
            return mod[:, layer, which * DC:(which + 1) * DC]

        ps = ctx.enter_context(nc.psum_tensor("ps", [P, 8, 512], F32))

        def item_slot(i):
            return ring[:, (i % NITEM) * ITEM:(i % NITEM + 1) * ITEM]

        def gate_up_of(slot):
            return ring[:, slot * EXP:slot * EXP + 4096].rearrange("p (g c n) -> p g c n", g=2, c=DC)

        def gate_up_rest(slot):
            return ring_rest[:, slot * EXP:slot * EXP + 4096].rearrange("p (g c n) -> p g c n", g=2, c=DC)

        def expert_down(slot):
            return ring[:, slot * EXP + 4096:slot * EXP + 6144].rearrange("p (f n) -> p f n", f=FC)

        def sem(name):
            return ctx.enter_context(nc.semaphore(name))

        const_in, x_in, stage_in, small_in = sem("const_in"), sem("x_in"), sem("stage_in"), sem("small_in")
        x_turned, vec_turned, vec_kept, silu_c_ready = sem("x_turned"), sem("vec_turned"), sem("vec_kept"), sem("silu_c_ready")
        dve_step = sem("dve_step")
        y_turned, y_kept, y_out = sem("y_turned"), sem("y_kept"), sem("y_out")
        EACH_LAYER = dict(
            sq_ready=2 * 4, ssq_ready=2, std_ready=2, scaled=2 * 2, gain_ready=2, h_ready=DC, h_late_ready=DC, index_rotated=1, q_rms_ready=1,
            q_std_ready=1, q_rotated=1, turn_done=4, turn_kept=4, index_done=2, index_kept=2, index_read=1,
            att_done=3, att_masked=3, att_max=3, att_exp=2 * HEADS, prob_turned=6, prob_kept=6, pv_done=2,
            attn_ready=2, attn_turned=1, attn_kept=1, conv_ready=1, mean_ready=1, centred=1, ln_sq_ready=1,
            var_ready=1, ln_std_ready=1, ln_ready=1, conv_act_ready=CC, ya_done=3, ya_used=4, yc_done=3,
            merged_ready=4, out_done=2, pad_zero=1, logits_done=1, group_shifted=1, group_exp=1, gap_ready=1,
            gap_exp=1, member_ready=1, rank_done=1, hn_turned=4, hn_kept=4, hn_rest_ready=4, onehot_ready=TC, offs_ready=1,
            sorted_done=DC, sorted_kept=DC, weighted_ready=TC, spread_turned=1, spread_kept=1, tail_zero=1,
            gate_up_used=NE, expert_used=NE, experts_done=1, made_turned=8, made_kept=4, made_kept_too=4, final_done=4)
        OWN = ("item_used", "ada_used", "pe_ada_used", "mod_summed", "x_ready", "block_kept", "xe_ready", "gu_done", "act_ready", "hid_ready", "y_stored",
               "rounded_ready", "rest_ready", "xe_rounded", "products_kept", "folded", "down_slow")

        class Signal:

            def __init__(self, semaphore, base):
                self.sem, self.base = semaphore, base

            def at(self, n):
                return self.sem, n + self.base if self.base else n

        shared = {name: sem(name) for name in EACH_LAYER}
        Signals = namedtuple("Signals", (*EACH_LAYER, *OWN))
        sig = [Signals(*(Signal(shared[n], l * each) for n, each in EACH_LAYER.items()),
                       *(Signal(sem(f"{n}_{l}"), 0) for n in OWN)) for l in range(DEPTH)]
        item_in = [[sem(f"item_in_{l}_{s}") for s in range(NITEM)] for l in range(DEPTH)]
        gate_up_in = [[sem(f"gate_up_in_{l}_{s}") for s in range(NEXP)] for l in range(DEPTH)]
        down_in = [[sem(f"down_in_{l}_{s}") for s in range(NEXP)] for l in range(DEPTH)]

        block = ctx.enter_context(nc.Block())

        @block.sync
        def _(sp):
            sp.dma_start(const[:, :], constants).then_inc(const_in, 16)
            for name in ("c", *(n for n in ROWS if n != "c")):
                r0, r1 = ROWS[name]
                if name == "c":
                    src = w[name].rearrange("a (r q) -> r a q", q=P).to_broadcast([r1 - r0, DEPTH, P])
                else:
                    src = w[name].rearrange("l (r q) -> r l q", q=P)
                sp.dma_start(stage[r0:r1], src).then_inc(stage_in, 16)
            sp.dma_start(stage_taps, w["conv_w"].rearrange("l k (c q) -> (k c) l q", q=P)).then_inc(stage_in, 16)
            for l in range(DEPTH):
                s = sig[l]
                items = mixer_items(l)
                users = used_by(items)

                def wait_used(chosen):
                    for who, signal in (("PE", s.item_used), ("DVE", s.ada_used), ("PE alone", s.pe_ada_used)):
                        counts = [users[i][1] for i in chosen if users[i][0] == who]
                        if counts:
                            sp.wait_ge(*signal.at(max(counts)))

                for i, item in enumerate(items):
                    if i >= NITEM:
                        wait_used([i - NITEM])
                    elif l > 0:
                        last = (i * ITEM + ITEM - 1) // EXP
                        sp.wait_ge(*sig[l - 1].expert_used.at(NE - NEXP + last + 1))
                    dst = item_slot(i)
                    if item[0] == "ada":
                        _, ml, third, quarter = item
                        n = 4 * third + quarter
                        src = w["w_ada"][ml, :, n * 512:(n + 1) * 512].rearrange("(c p) n -> p c n", p=P)
                        dst = dst.rearrange("p (c n) -> p c n", c=DC)
                    elif item[0] == "in":
                        b = item[1]
                        c0, n = {"KVI": (COL_K, N_KVI), "Q": (COL_Q, 512), "CA": (0, 512), "CB": (CH, 512)}.get(
                            b, (COL_G + 512 * (BLOCKS.index(b) - 4), 512))
                        src = w["w_in"][l, :, c0:c0 + n].rearrange("(c p) n -> p c n", p=P)
                        dst = dst[:, 0:DC * n].rearrange("p (c n) -> p c n", c=DC)
                    elif item[0] == "out":
                        src = w["w_out"][l, :, item[1] * 512:(item[1] + 1) * 512].rearrange("(c p) n -> p c n", p=P)
                        dst = dst.rearrange("p (c n) -> p c n", c=DC)
                    else:
                        src = w["w_" + item[0]][l].rearrange("(c p) n -> p c n", p=P)
                        dst = dst.rearrange("p (c n) -> p c n", c=4)
                    sp.dma_start(dst, src).then_inc(item_in[l][i % NITEM], 16)
                    if l == 0 and i == 0:
                        sp.dma_start(x_nat, w["x"][0].rearrange("(t p) d -> p t d", p=P)).then_inc(x_in, 16)

                def load_expert(slot, e, nth=None):
                    def src(name, pattern, **kw):
                        return w[name][l, bass.ds(e, 1)].rearrange(pattern, **kw)
                    if nth is not None:
                        sp.wait_ge(*s.gate_up_used.at(nth))
                    sp.dma_start(gate_up_of(slot)[:, 0].rearrange("p c n -> p (c n)"),
                                 src("w_gate", "a (p c) n -> p (a c n)", c=DC)).then_inc(gate_up_in[l][slot], 16)
                    sp.dma_start(gate_up_of(slot)[:, 1].rearrange("p c n -> p (c n)"),
                                 src("w_up", "a (p c) n -> p (a c n)", c=DC)).then_inc(gate_up_in[l][slot], 16)
                    if nth is not None:
                        sp.wait_ge(*s.expert_used.at(nth))
                    sp.dma_start(expert_down(slot),
                                 src("w_down", "a (f p) n -> p (a f) n", p=P)).then_inc(down_in[l][slot], 16)

                for slot in range(NEXP):
                    wait_used([i for i in range(len(items) - NITEM, len(items))
                               if (i % NITEM) * ITEM < (slot + 1) * EXP and (i % NITEM + 1) * ITEM > slot * EXP])
                    load_expert(slot, slot)
                with sp.Fori(1, NE // NEXP) as r:
                    for slot in range(NEXP):
                        load_expert(slot, r * NEXP + slot, (r - 1) * NEXP + slot + 1)
            for g in range(4):
                half, t = g // 2, g % 2
                part = slice(half * 512, (half + 1) * 512)
                sp.wait_ge(y_kept, g + 1)
                sp.dma_start(out[0, t * P:(t + 1) * P, part], y_nat[:, t, part]).then_inc(y_out, 16)
            sp.wait_ge(y_out, 16 * 4)

        @block.tensor
        def _(pe):
            mm = nc.tensor.matmul

            def mm_halves(dst, lhsT, rhs, **kw):
                for half in (0, P // 2):
                    last = mm(dst[half:half + P // 2], lhsT[:, half:half + P // 2], rhs, **kw)
                return last

            def keep_warm(n):
                for _ in range(n):
                    mm(ps[:, 6, 0:P], ident, ident, start=True, stop=True)

            def turn(dst, src, n_rows=P):
                return nc.tensor.transpose(dst, src, ident[0:n_rows, 0:n_rows])

            pe.wait_ge(const_in, 16)
            pe.wait_ge(stage_in, 16 * N_STAGE)
            for l in range(DEPTH):
                turn(ps[:, 0, l * P:l * P + N_ROWS], stage[:, l, :], N_ROWS)
                last = turn(ps[:, 0, 256 + l * P:256 + l * P + N_TAPROWS], stage_taps[:, l, :], N_TAPROWS)
            last.then_inc(vec_turned, 1)
            pe.wait_ge(x_in, 16)
            for c in range(DC):
                for t in range(TC):
                    last = turn(ps[:, 3 + c // 2, (c % 2) * T + t * P:(c % 2) * T + (t + 1) * P],
                                x_nat[:, t, c * P:(c + 1) * P])
                if c % 2:
                    last.then_inc(x_turned, 1)

            for l in range(DEPTH):
                s = sig[l]
                at = Place()
                own = [i for i, (who, _) in enumerate(used_by(mixer_items(l))) if who == "PE"]

                n_ada = 3 if l == 0 else 0

                def item(c, n=ITEM):
                    i = own[at.item]
                    at.item += 1
                    pe.wait_ge(item_in[l][i % NITEM], 16 * (i // NITEM + 1))
                    return item_slot(i)[:, 0:n].rearrange("p (c n) -> p c n", c=c)

                def wait_h(n, c):
                    ready, nth = (s.h_ready, c) if c < DC // 2 else (s.h_late_ready, c - DC // 2)
                    pe.wait_ge(*ready.at(DC // 2 * (n - 1) + nth + 1))

                def run_block():
                    j = at.block
                    at.block += 1
                    bank = 2 * (j % 2)
                    if j >= 2:
                        pe.wait_ge(*s.block_kept.at(j - 1))
                    if BLOCKS[j] in ("KVI", "Q"):
                        n = N_KVI if BLOCKS[j] == "KVI" else 512
                        wt = item(DC, DC * n)
                        for t in range(TC):
                            for c in range(DC):
                                if t == 0:
                                    wait_h(1, c)
                                last = mm(ps[:, bank + t, 0:n], hT[:, c, t * P:(t + 1) * P], wt[:, c, :],
                                          start=c == 0, stop=c == DC - 1)
                    else:
                        wt = item(DC)
                        for n in range(4):
                            for c in range(DC):
                                last = mm(ps[:, bank + n // 2, (n % 2) * T:(n % 2 + 1) * T],
                                          wt[:, c, n * P:(n + 1) * P], hT[:, c, :], start=c == 0, stop=c == DC - 1)
                    last.then_inc(s.item_used.sem, 1)

                def sum_modulation(bank, partial, used, nth=range(4)):
                    for at, quarter in enumerate(nth):
                        pe.wait_ge(*s.ada_used.at(used - len(nth) + 1 + at))
                        for i in range(4):
                            n = 4 * quarter + i
                            last = mm_halves(ps[:, bank, n:n + 1], partial[:, quarter, i * P:(i + 1) * P], ones[:, 0:1],
                                             start=True, stop=True)
                    last.then_inc(s.mod_summed.sem, 1)

                def whole_ada_item(bank):
                    i = mixer_items(l).index(PE_ADA)
                    pe.wait_ge(silu_c_ready, 1)
                    pe.wait_ge(item_in[l][i % NITEM], 16 * (i // NITEM + 1))
                    wt = item_slot(i).rearrange("p (c n) -> p c n", c=DC)
                    for i in range(4):
                        n = 4 * PE_ADA[3] + i
                        for c in range(DC):
                            last = mm_halves(ps[:, bank, n:n + 1], wt[:, c, i * P:(i + 1) * P], silu_c[:, c:c + 1],
                                             start=c == 0, stop=c == DC - 1)
                    last.then_inc(s.pe_ada_used.sem, 1)

                def sum_over_channels(dst, src, chunks):
                    for c in range(chunks):
                        last = mm(dst, ones, src[:, c, :], start=c == 0, stop=c == chunks - 1)
                    return last

                def index_unit(t):
                    n = (t + 1) * P
                    for h in range(IH):
                        last = mm(ps[:, 4 + h % 4, (h // 4) * n:(h // 4 + 1) * n],
                                  turned[:, IQT + h // 4, t * P:(t + 1) * P], index_kt[:, h % 4, 0:n],
                                  start=True, stop=True)
                    last.then_inc(s.index_done.sem, 1)

                def attention_unit(t, half):
                    n = (t + 1) * P
                    for h in (range(HEADS) if t == 0 else range(4 * half, 4 * half + 4)):
                        at = h // 2 if t == 0 else h // 2 % 2
                        last = mm(ps[:, 4 + h % 2, at * n:(at + 1) * n],
                                  turned[:, QT + h // 2, t * P:(t + 1) * P], turned[:, KT[h % 2], 0:n],
                                  start=True, stop=True)
                    last.then_inc(s.att_done.sem, 1)

                def sum_squares(n):
                    for c in range(DC):
                        if c % 2 == 0:
                            pe.wait_ge(*s.sq_ready.at(4 * (n - 1) + c // 2 + 1))
                        last = mm(ps[:, 7, 0:T], ones, square[:, c, :], start=c == 0, stop=c == DC - 1)
                    last.then_inc(s.ssq_ready.sem, 1)

                sum_squares(1)
                if l == 0:
                    whole_ada_item(2)
                    sum_modulation(2, partial_first, 3, [q for q in range(4) if q != PE_ADA[3]])
                else:
                    keep_warm(18)

                run_block()
                run_block()
                run_block()
                pe.wait_ge(*s.index_rotated.at(1))
                pe.wait_ge(*s.q_rotated.at(1))
                groups = ((("i", 0), ("i", 1)), (("i", 2), ("q", 4)), (("q", 0), ("q", 1)), (("q", 2), ("q", 3)))
                for g, group in enumerate(groups):
                    if g == 3:
                        pe.wait_ge(*s.turn_kept.at(1))
                    for half, (kind, n) in enumerate(group):
                        for t in range(TC):
                            src = ir[:, t, 4 * n:4 * n + 4, :] if kind == "i" else qr[:, t, 2 * n:2 * n + 2, :]
                            o = half * T + t * P
                            last = turn(ps[:, 4 + g % 3, o:o + P], src.rearrange("p h d -> p (h d)"))
                    last.then_inc(s.turn_done.sem, 1)
                pe.wait_ge(*s.turn_kept.at(4))
                index_unit(0)
                run_block()
                pe.wait_ge(*s.index_kept.at(1))
                index_unit(1)
                run_block()
                pe.wait_ge(*s.index_kept.at(2))
                sum_modulation(6, partial_early, n_ada + 4)
                attention_unit(0, 0)
                pe.wait_ge(*s.att_masked.at(1))
                attention_unit(1, 0)
                run_block()
                pe.wait_ge(*s.att_masked.at(2))
                attention_unit(1, 1)
                run_block()

                pe.wait_ge(*s.att_exp.at(8))
                for g in range(2):
                    for i in range(4):
                        last = turn(ps[:, 6 + g, i * P:(i + 1) * P], scores0[:, 4 * g + i, :])
                    last.then_inc(s.prob_turned.sem, 1)
                pe.wait_ge(*s.prob_kept.at(2))
                pe.wait_ge(*s.att_masked.at(3))
                for h in range(HEADS):
                    last = mm(ps[:, 4 + h // 4, (h % 4) * P:(h % 4 + 1) * P], probsT[:, h, 0:P],
                              kvi[:, 0, HD:HD + P], start=True, stop=True)
                last.then_inc(s.pv_done.sem, 1)
                pe.wait_ge(*s.att_exp.at(16))
                for g in range(4):
                    if g >= 2:
                        pe.wait_ge(*s.prob_kept.at(2 + g - 1))
                    for i in range(2):
                        for sc in range(TC):
                            last = turn(ps[:, 6 + g % 2, (2 * i + sc) * P:(2 * i + sc + 1) * P],
                                        scores[:, 2 * g + i, sc * P:(sc + 1) * P])
                    last.then_inc(s.prob_turned.sem, 1)
                pe.wait_ge(*s.prob_kept.at(6))
                for h in range(HEADS):
                    for sc in range(TC):
                        last = mm(ps[:, 6 + h // 4, (h % 4) * P:(h % 4 + 1) * P], probsT[:, h, sc * P:(sc + 1) * P],
                                  kvi[:, sc, HD:HD + P], start=sc == 0, stop=sc == TC - 1)
                last.then_inc(s.pv_done.sem, 1)
                run_block()

                pe.wait_ge(*s.attn_ready.at(2))
                for c in range(4):
                    for t in range(TC):
                        last = turn(ps[:, 6 + c // 2, (c % 2) * T + t * P:(c % 2) * T + (t + 1) * P],
                                    attn[:, t, 2 * c:2 * c + 2, :].rearrange("p h d -> p (h d)"))
                last.then_inc(s.attn_turned.sem, 1)
                pe.wait_ge(*s.attn_kept.at(1))
                pe.wait_ge(*s.block_kept.at(len(BLOCKS)))
                wt = item(4)
                for n in range(DC):
                    if n == 2:
                        pe.wait_ge(*s.conv_ready.at(1))
                        sum_over_channels(ps[:, 7, 0:T], ca, CC).then_inc(s.mean_ready.sem, 1)
                    if n == 4:
                        pe.wait_ge(*s.ln_sq_ready.at(1))
                        sum_over_channels(ps[:, 7, T:2 * T], ca, CC).then_inc(s.var_ready.sem, 1)
                    for c in range(4):
                        last = mm(ps[:, n // 2, (n % 2) * T:(n % 2 + 1) * T], wt[:, c, n * P:(n + 1) * P],
                                  attnT[:, c, :], start=c == 0, stop=c == 3)
                    if n % 2 and n < DC - 1:
                        last.then_inc(s.ya_done.sem, 1)
                last.then_inc(s.item_used.sem, 1)

                pe.wait_ge(*s.conv_act_ready.at(CC))
                wt = item(4)
                for n in range(DC):
                    for c in range(4):
                        last = mm(ps[:, 4 + n // 2, (n % 2) * T:(n % 2 + 1) * T], wt[:, c, n * P:(n + 1) * P],
                                  ca[:, c, :], start=c == 0, stop=c == 3)
                    if n % 2 and n < DC - 1:
                        last.then_inc(s.yc_done.sem, 1)
                last.then_inc(s.item_used.sem, 1)

                pe.wait_ge(*s.ya_used.at(4))
                for n in range(DC):
                    if n == 4:
                        sum_modulation(4, partial_late, n_ada + 8)
                    if n % 4 == 0:
                        wt = item(DC)
                    for c in range(DC):
                        if n == 0:
                            pe.wait_ge(*s.merged_ready.at(c // 2 + 1))
                        last = mm(ps[:, n // 2, (n % 2) * T:(n % 2 + 1) * T],
                                  wt[:, c, (n % 4) * P:(n % 4 + 1) * P], merged[:, c, :],
                                  start=c == 0, stop=c == DC - 1)
                    if n % 4 == 3:
                        last.then_inc(s.item_used.sem, 1)
                    elif n % 2:
                        last.then_inc(s.out_done.sem, 1)

                keep_warm(10)
                sum_squares(2)
                if l + 1 < DEPTH:
                    sum_modulation(5, partial_next, n_ada + 12)
                else:
                    keep_warm(8)
                for c in range(DC):
                    wait_h(2, c)
                    for t in range(TC):
                        last = mm_halves(ps[:, 4 + 2 * t, 0:GROUPS + NE], hT[:, c, t * P:(t + 1) * P],
                                  w_route[:, l, c, :], start=c == 0, stop=c == DC - 1)
                last.then_inc(s.logits_done.sem, 1)
                for g in range(4):
                    t, half = g // 2, g % 2
                    for i in range(4):
                        last = turn(ps[:, g, i * P:(i + 1) * P], hT[:, 4 * half + i, t * P:(t + 1) * P])
                    last.then_inc(s.hn_turned.sem, 1)
                pe.wait_ge(*s.member_ready.at(1))
                mm_halves(ps[:, 5, 0:NE], before, member[:, 0, :], start=True, stop=True)
                mm_halves(ps[:, 5, NE:2 * NE], ones, member[:, 0, :], start=True, stop=False)
                mm_halves(ps[:, 5, NE:2 * NE], before, member[:, 1, :], start=False, stop=True)
                mm_halves(ps[:, 5, 2 * NE:3 * NE], ones, member[:, 0, :], start=True, stop=False)
                mm_halves(ps[:, 5, 2 * NE:3 * NE], ones, member[:, 1, :], start=False, stop=True).then_inc(
                    s.rank_done.sem, 1)
                keep_warm(14)
                pe.wait_ge(*s.hn_rest_ready.at(4))
                pe.wait_ge(*s.onehot_ready.at(TC))
                for c in range(DC):
                    if c >= 4:
                        pe.wait_ge(*s.sorted_kept.at(c - 3))
                    for part in (hn_rounded, hn_rest):
                        for t in range(TC):
                            last = mm(ps[:, c % 4, :], part[:, t, c:D:DC], sorter[:, t, :],
                                      start=part is hn_rounded and t == 0, stop=part is hn_rest and t == TC - 1)
                    last.then_inc(s.sorted_done.sem, 1)
                pe.wait_ge(*s.weighted_ready.at(TC))
                for j in range(4):
                    for t in range(TC):
                        last = turn(ps[:, 6 + j // 2, (j % 2) * T + t * P:(j % 2) * T + (t + 1) * P],
                                    weighted[:, t, j * P:(j + 1) * P])
                last.then_inc(s.spread_turned.sem, 1)

                def gate_up(slot, b, x_block, e):
                    rest = [gate_up_rest(slot)[:, :, 4 * h:4 * h + 4, :] for h in range(2)]
                    n = 0
                    for weights, ready in ((rounded[b], s.rounded_ready), (rest, s.rest_ready)):
                        for half in range(2):
                            pe.wait_ge(*ready.at(e * 2 + half + 1))
                            for c in range(4):
                                last = mm(ps[:, 0, :].rearrange("p (g n) -> p g n", g=2),
                                          x_block[:, 4 * half + c].rearrange("p h s -> p (h s)"),
                                          weights[half][:, :, c, :], start=n == 0, stop=n == 15)
                                n += 1
                    return last

                def fold_products(used=None):
                    for f in range(2 * FC):
                        last = mm(ps[:, 1, f * P:(f + 1) * P], products[:, f * P:(f + 1) * P], fold, start=True, stop=True)
                        if f == 0 and used is not None:
                            last.then_inc(used.sem, 1)
                    return last

                def down(slot, bank):
                    wt = expert_down(slot)
                    for c in range(DC):
                        for f in range(FC):
                            last = mm(ps[:, bank + c // 4, c % 4 * P:(c % 4 + 1) * P], wt[:, f, c * P:(c + 1) * P],
                                      hid[:, f, :], start=f == 0, stop=f == FC - 1)
                    return last

                pe.wait_ge(*s.sorted_kept.at(DC))
                pe.wait_ge(*s.offs_ready.at(1))
                big = pe.value_load(flag[0:1, l:l + 1], min_val=0, max_val=1)
                with pe.If(big == 0):
                    def step_up(e, j):
                        pe.wait_ge(*s.xe_ready.at(e + 1))
                        gate_up(j, j % 2, xe[:, j % 2], e).then_inc(s.gu_done.sem, 1)

                    def step_fold(e):
                        pe.wait_ge(*s.products_kept.at(e + 1))
                        fold_products(s.gate_up_used).then_inc(s.folded.sem, 1)

                    def step_down(e, r, j):
                        pe.wait_ge(down_in[l][j], r * 16 + 16)
                        pe.wait_ge(*s.hid_ready.at(e + 1))
                        if not isinstance(e, int) or e >= 2:
                            pe.wait_ge(*s.y_stored.at(e - 1))
                        down(j, 2 + 2 * (j % 2)).then_inc(s.expert_used.sem, 1)

                    for j in range(NEXP):
                        step_up(j, j)
                        if j > 0:
                            step_down(j - 1, 0, j - 1)
                        step_fold(j)
                    with pe.Fori(1, NE // NEXP) as r:
                        for j in range(NEXP):
                            step_up(r * NEXP + j, j)
                            step_down(r * NEXP + j - 1, r - (j == 0), (j - 1) % NEXP)
                            step_fold(r * NEXP + j)
                    step_down(NE - 1, NE // NEXP - 1, NEXP - 1)
                with pe.Else():
                    pe.sem_inc(s.gu_done.sem, 1)
                    with pe.Fori(0, NE // NEXP) as r:
                        for j in range(NEXP):
                            def run_slow(n, used, gate_up_used=None):
                                pe.wait_ge(*s.xe_ready.at(n + 1))
                                gate_up(j, 0, xe[:, 0], r * NEXP + j).then_inc(s.gu_done.sem, 1)
                                pe.wait_ge(*s.products_kept.at(n + 1))
                                fold_products(gate_up_used).then_inc(s.folded.sem, 1)
                                pe.wait_ge(down_in[l][j], r * 16 + 16)
                                pe.wait_ge(*s.hid_ready.at(n + 1))
                                pe.wait_ge(*s.y_stored.at(n + 1))
                                down(j, 2).then_inc(used.sem, 1)

                            with pe.Fori(0, NBLK - 1) as b:
                                run_slow((r * NEXP + j) * NBLK + b, s.down_slow)
                            run_slow((r * NEXP + j) * NBLK + NBLK - 1, s.expert_used, s.gate_up_used)

                pe.wait_ge(*s.experts_done.at(1))
                pe.wait_ge(*s.spread_kept.at(1))
                for g in range(8):
                    j, half = g // 2, g % 2
                    if g >= 4:
                        kept = s.made_kept_too if half else s.made_kept
                        pe.wait_ge(*kept.at(j - 1))
                    for i in range(4):
                        last = turn(ps[:, 4 + g % 4, i * P:(i + 1) * P], made[:, 4 * half + i, j * P:(j + 1) * P])
                    last.then_inc(s.made_turned.sem, 1)
                for c in range(DC):
                    for j in range(4):
                        if c == 0:
                            pe.wait_ge(*s.made_kept.at(j + 1))
                            pe.wait_ge(*s.made_kept_too.at(j + 1))
                        last = mm(ps[:, c // 2, (c % 2) * T:(c % 2 + 1) * T], made_n[:, j, c * P:(c + 1) * P],
                                  spread[:, j, :], start=j == 0, stop=j == 3)
                    if c % 2:
                        last.then_inc(s.final_done.sem, 1)

            for g in range(4):
                half, t = g // 2, g % 2
                pe.wait_ge(*sig[DEPTH - 1].x_ready.at(10 + 2 * half))
                for i in range(4):
                    last = turn(ps[:, 4 + g, i * P:(i + 1) * P], xT[:, 4 * half + i, t * P:(t + 1) * P])
                last.then_inc(y_turned, 1)

        @block.gpsimd
        def _(pool):
            for l in range(DEPTH):
                pool.dma_start(qk_gain[:, l, 0:HEADS, :],
                               w["q_norm_g"][l:l + 1, :].unsqueeze(1).to_broadcast([P, HEADS, HD])).then_inc(small_in, 16)
                pool.dma_start(qk_gain[:, l, HEADS, :], w["k_norm_g"][l:l + 1, :].to_broadcast([P, HD])).then_inc(small_in, 16)
                pool.dma_start(w_route[:, l, :, 0:GROUPS],
                               w["w_group"][l].rearrange("(c p) n -> p c n", p=P)).then_inc(small_in, 16)
                pool.dma_start(w_route[:, l, :, GROUPS:],
                               w["w_router"][l].rearrange("(c p) n -> p c n", p=P)).then_inc(small_in, 16)
                pool.dma_start(b_route[:, l, 0:GROUPS], w["b_group"][l:l + 1, :].to_broadcast([P, GROUPS])).then_inc(small_in, 16)
                pool.dma_start(b_route[:, l, GROUPS:], w["b_router"][l:l + 1, :].to_broadcast([P, NE])).then_inc(small_in, 16)
            for l in range(DEPTH):
                s = sig[l]
                pool.wait_ge(*s.x_ready.at(4))
                pool.memset(turned[:, KT[0], :], 0.0)
                pool.memset(turned[:, KT[1], :], 0.0)
                pool.memset(index_kt, 0.0)
                pool.memset(pad[:, :, 0:TAPS - 1], 0.0).then_inc(s.pad_zero.sem, 1)
                pool.wait_ge(*s.ssq_ready.at(2))
                pool.wait_ge(*s.mod_summed.at(2 + (l == 0) + (l + 1 < DEPTH)))
                pool.memset(sorted_x[:, :, PAIRS:PADDED], 0.0).then_inc(s.tail_zero.sem, 1)
                for g in range(4):
                    pool.wait_ge(*s.hn_kept.at(g + 1))
                    part = slice((g % 2) * 512, (g % 2 + 1) * 512)
                    pool.tensor_tensor(hn_rest[:, g // 2, part], hn[:, g // 2, part], hn_rounded[:, g // 2, part],
                                       ALU.subtract).then_inc(s.hn_rest_ready.sem, 1)

        @block.scalar
        def _(act):
            activate = nc.scalar.activation
            act.wait_ge(vec_kept, 2)
            activate(silu_c[:, :], row(0, "c"), ACT.Silu).then_inc(silu_c_ready, 1)
            for p in range(4):
                act.wait_ge(x_turned, p + 1)
                nc.scalar.copy(xT[:, 2 * p:2 * p + 2, :].rearrange("p c t -> p (c t)"),
                               ps[:, 3 + p, :]).then_inc(sig[0].x_ready.sem, 1)

            for l in range(DEPTH):
                s = sig[l]
                at = Place()

                def keep_block():
                    j = at.block
                    at.block += 1
                    b, bank = BLOCKS[j], 2 * (j % 2)
                    act.wait_ge(*s.item_used.at(j + 1))
                    pair = ps[:, bank:bank + 2, :].rearrange("p b (n t) -> p (b n) t", t=T)
                    if b == "KVI":
                        nc.scalar.copy(qk[:, :, HEADS, :], ps[:, bank:bank + 2, 0:HD])
                        last = nc.scalar.copy(kvi, ps[:, bank:bank + 2, 0:N_KVI])
                    elif b == "Q":
                        last = nc.scalar.copy(qk[:, :, 0:HEADS, :].rearrange("p t h d -> p t (h d)"),
                                              ps[:, bank:bank + 2, :])
                    elif b == "CA":
                        last = nc.scalar.copy(ca, pair)
                    elif b == "CB":
                        last = activate(cb, pair, ACT.Sigmoid)
                    else:
                        g = j - 4
                        last = activate(gates[:, g // 2, 4 * (g % 2):4 * (g % 2) + 4, :], pair, ACT.Sigmoid)
                    last.then_inc(s.block_kept.sem, 1)

                def norm(n, shift):
                    act.preload_act_table(ACT.Sqrt)
                    for p in range(4):
                        act.wait_ge(*s.x_ready.at(4 * (n - 1) + p + 1))
                        activate(square[:, 2 * p:2 * p + 2, :], xT[:, 2 * p:2 * p + 2, :],
                                 ACT.Square).then_inc(s.sq_ready.sem, 1)
                    act.wait_ge(*s.ssq_ready.at(n))
                    activate(std[:, :], ps[:, 7, 0:T], ACT.Sqrt, bias=eps, scale=1.0 / D).then_inc(s.std_ready.sem, 1)
                    act.wait_ge(*s.gain_ready.at(n))
                    for c in range(DC // 2):
                        if c % 2 == 0:
                            act.wait_ge(*s.scaled.at(2 * (n - 1) + c // 2 + 1))
                        activate(hT[:, c, :], hT[:, c, :], ACT.Identity, bias=modulation(l, shift)[:, c:c + 1],
                                 scale=gain[:, l, n - 1, c:c + 1]).then_inc(s.h_ready.sem, 1)

                act.wait_ge(const_in, 16)
                norm(1, SHIFT1)
                keep_block()
                keep_block()
                act.wait_ge(*s.q_rms_ready.at(1))
                activate(rms, sumsq, ACT.Sqrt, bias=eps, scale=1.0 / HD).then_inc(s.q_std_ready.sem, 1)
                keep_block()
                for g in range(4):
                    act.wait_ge(*s.turn_done.at(g + 1))
                    both = ps[:, 4 + g % 3, :].rearrange("p (n t) -> p n t", t=T)
                    if g == 1:
                        act.wait_ge(*s.pad_zero.at(1))
                        for q in range(4):
                            rows = slice(ID * q, ID * (q + 1))
                            nc.scalar.copy(index_kt[rows, q, :], both[rows, 0, :])
                        nc.scalar.copy(turned[0:HD, KT[0], :], both[0:HD, 1, :])
                        last = nc.scalar.copy(turned[HD:P, KT[1], :], both[HD:P, 1, :])
                    else:
                        last = nc.scalar.copy(turned[:, 2 * g:2 * g + 2, :], both)
                    last.then_inc(s.turn_kept.sem, 1)

                def keep_index(u):
                    act.wait_ge(*s.index_done.at(u + 1))
                    n = (u + 1) * P
                    if u == 1:
                        act.wait_ge(*s.index_read.at(1))
                    activate(scores[:, :, 0:n].rearrange("p (b g) s -> p b g s", g=2),
                             ps[:, 4:8, 0:2 * n].rearrange("p b (g s) -> p b g s", s=n),
                             ACT.Relu).then_inc(s.index_kept.sem, 1)

                def exponentials(u):
                    act.wait_ge(*s.att_max.at(u + 1))
                    for h in (range(HEADS) if u == 0 else range(4 * (u - 1), 4 * u)):
                        tile = scores0[:, h, :] if u == 0 else scores[:, h, :]
                        i = (HEADS if u else 0) + h
                        activate(tile, tile, ACT.Exp, bias=rowmax[:, i:i + 1],
                                 accum_out=rowsum[:, i:i + 1]).then_inc(s.att_exp.sem, 1)

                keep_index(0)
                keep_block()
                keep_index(1)
                keep_block()
                exponentials(0)
                keep_block()
                exponentials(1)
                exponentials(2)
                keep_block()
                for g in range(2):
                    act.wait_ge(*s.prob_turned.at(g + 1))
                    nc.scalar.copy(probsT[:, 4 * g:4 * g + 4, 0:P],
                                   ps[:, 6 + g, :].rearrange("p (h t) -> p h t", t=P)).then_inc(s.prob_kept.sem, 1)
                act.wait_ge(*s.pv_done.at(1))
                for g in range(4):
                    act.wait_ge(*s.prob_turned.at(2 + g + 1))
                    nc.scalar.copy(probsT[:, 2 * g:2 * g + 2, :],
                                   ps[:, 6 + g % 2, :].rearrange("p (h t) -> p h t", t=T)).then_inc(s.prob_kept.sem, 1)
                keep_block()
                act.wait_ge(*s.attn_turned.at(1))
                nc.scalar.copy(attnT, ps[:, 6:8, :].rearrange("p b (n t) -> p (b n) t", t=T)).then_inc(s.attn_kept.sem, 1)

                act.preload_act_table(ACT.Sqrt)
                act.wait_ge(*s.centred.at(1))
                activate(ca, cb, ACT.Square).then_inc(s.ln_sq_ready.sem, 1)
                act.wait_ge(*s.var_ready.at(1))
                activate(std[:, :], ps[:, 7, T:2 * T], ACT.Sqrt, bias=eps, scale=1.0 / CH).then_inc(s.ln_std_ready.sem, 1)
                act.wait_ge(*s.ln_ready.at(1))
                for c in range(CC):
                    activate(ca[:, c, :], cb[:, c, :], ACT.Silu, bias=row(l, "conv_ln_b")[:, c:c + 1],
                             scale=row(l, "conv_ln_g")[:, c:c + 1]).then_inc(s.conv_act_ready.sem, 1)

                norm(2, SHIFT2)
                for g in range(4):
                    act.wait_ge(*s.hn_turned.at(g + 1))
                    part = slice((g % 2) * 512, (g % 2 + 1) * 512)
                    nc.scalar.copy(hn_rounded[:, g // 2, part], ps[:, g, :])
                    nc.scalar.copy(hn[:, g // 2, part], ps[:, g, :]).then_inc(s.hn_kept.sem, 1)
                act.wait_ge(*s.group_shifted.at(1))
                activate(g_exp, g_shift, ACT.Exp).then_inc(s.group_exp.sem, 1)
                act.wait_ge(*s.gap_ready.at(1))
                activate(gap_exp, gap, ACT.Exp).then_inc(s.gap_exp.sem, 1)

                def round_half(slot, b, half):
                    nc.scalar.copy(rounded[b][half],
                                   gate_up_of(slot)[:, :, 4 * half:4 * half + 4, :]).then_inc(s.rounded_ready.sem, 1)

                act.preload_act_table(ACT.Silu)
                act.wait_ge(gate_up_in[l][0], 32)
                round_half(0, 0, 0)
                round_half(0, 0, 1)
                for c in range(DC):
                    act.wait_ge(*s.sorted_done.at(c + 1))
                    nc.scalar.copy(sorted_x[:, c, 0:PAIRS], ps[:, c % 4, :]).then_inc(s.sorted_kept.sem, 1)
                act.wait_ge(*s.offs_ready.at(1))
                act.wait_ge(*s.weighted_ready.at(TC))
                big = act.value_load(flag[0:1, l:l + 1], min_val=0, max_val=1)
                starts = offs[0:1, l].rearrange("q b e -> q (b e)")

                def store(n, bank):
                    at = act.value_load(starts[0:1, bass.ds(n, 1)], min_val=0, max_val=PAIRS)
                    return nc.scalar.copy(made[:, :, bass.ds(at, BLK)],
                                          ps[:, bank:bank + 2, :].rearrange("p b (c s) -> p (b c) s", s=P)[:, :, 0:BLK])

                def start_next(slot, count):
                    act.wait_ge(gate_up_in[l][slot], count)
                    round_half(slot, 0, 0)
                    round_half(slot, 0, 1)

                def silu_gate():
                    return activate(act_g, ps[:, 1, 0:FC * P], ACT.Silu)

                with act.If(big == 0):

                    def step_round(e, r, j, half):
                        if half == 0:
                            act.wait_ge(gate_up_in[l][j], r * 32 + 32)
                            if not isinstance(e, int) or e >= 2:
                                act.wait_ge(*s.gu_done.at(e - 1))
                        round_half(j, j % 2, half)

                    def step(e, r, j, store_last=True, round_next=True):
                        act.wait_ge(*s.gu_done.at(e + 1))
                        nc.scalar.copy(products, ps[:, 0, :]).then_inc(s.products_kept.sem, 1)
                        if store_last:
                            act.wait_ge(*s.expert_used.at(e))
                            if not isinstance(e, int) or e >= 2:
                                act.wait_ge(*s.y_stored.at(e - 1))
                            store(e - 1, 2 + 2 * ((j - 1) % 2)).then_inc(s.y_stored.sem, 1)
                        act.wait_ge(*s.folded.at(e + 1))
                        silu_gate().then_inc(s.act_ready.sem, 1)
                        if round_next:
                            for half in range(2):
                                step_round(e + 2, r + (j + 2) // NEXP, (j + 2) % NEXP, half)

                    act.wait_ge(*s.spread_turned.at(1))
                    for half in range(2):
                        step_round(1, 0, 1, half)
                    for j in range(NEXP):
                        step(j, 0, j, store_last=j > 0)
                    with act.Fori(1, NE // NEXP - 1) as r:
                        for j in range(NEXP):
                            step(r * NEXP + j, r, j)
                    for j in range(NEXP):
                        step(NE - NEXP + j, NE // NEXP - 1, j, round_next=j < NEXP - 2)
                    act.wait_ge(*s.expert_used.at(NE))
                    act.wait_ge(*s.y_stored.at(NE - 1))
                    store(NE - 1, 2 + 2 * ((NE - 1) % 2)).then_inc(s.experts_done.sem, 1)
                with act.Else():
                    act.sem_inc(s.y_stored.sem, 1)

                    def step_slow(e, b, stored):
                        n = e * NBLK + b
                        act.wait_ge(*s.gu_done.at(n + 2))
                        nc.scalar.copy(products, ps[:, 0, :]).then_inc(s.products_kept.sem, 1)
                        act.wait_ge(*s.folded.at(n + 1))
                        silu_gate().then_inc(s.act_ready.sem, 1)
                        if b < NBLK - 1:
                            act.wait_ge(*s.down_slow.at(e * (NBLK - 1) + b + 1))
                        else:
                            act.wait_ge(*s.expert_used.at(e + 1))
                        act.wait_ge(*s.y_stored.at(n + 1))
                        store(e + b * NE, 2).then_inc(stored.sem, 1)

                    with act.Fori(0, NE // NEXP - 1) as r:
                        for j in range(NEXP):
                            for b in range(NBLK):
                                step_slow(r * NEXP + j, b, s.y_stored)
                            start_next((j + 1) % NEXP, (r + (j + 1) // NEXP) * 32 + 32)
                    for j in range(NEXP):
                        for b in range(NBLK):
                            last = j == NEXP - 1 and b == NBLK - 1
                            step_slow(NE - NEXP + j, b, s.experts_done if last else s.y_stored)
                        if j < NEXP - 1:
                            start_next(j + 1, NE // NEXP * 32)

                for j in range(4):
                    act.wait_ge(*s.made_turned.at(2 * j + 1))
                    nc.scalar.copy(made_n[:, j, 0:512], ps[:, 4 + 2 * j % 4, :]).then_inc(s.made_kept.sem, 1)

            for g in range(4):
                act.wait_ge(y_turned, g + 1)
                half, t = g // 2, g % 2
                nc.scalar.copy(y_nat[:, t, half * 512:(half + 1) * 512], ps[:, 4 + g, :]).then_inc(y_kept, 1)

        @block.vector
        def _(dve):
            v = nc.vector
            n_step = Place()

            def mark(ins):
                n_step.n += 1
                ins.then_inc(dve_step, 1)
                return n_step.n

            def sync():
                dve.wait_ge(dve_step, n_step.n)

            def do(ins):
                mark(ins)
                sync()

            tt, ts, stt, red = v.tensor_tensor, v.tensor_scalar, v.scalar_tensor_tensor, v.tensor_reduce

            dve.wait_ge(const_in, 16)
            dve.wait_ge(vec_turned, 1)
            v.tensor_copy(vec[:, :, :], ps[:, 0, 0:256].rearrange("p (l r) -> p l r", l=DEPTH)[:, :, 0:N_ROWS]).then_inc(vec_kept, 1)
            v.tensor_copy(taps[:, :, :, :].rearrange("p l k c -> p l (k c)"),
                          ps[:, 0, 256:512].rearrange("p (l r) -> p l r", l=DEPTH)[:, :, 0:N_TAPROWS]).then_inc(vec_kept, 1)
            dve.wait_ge(vec_kept, 2)

            for l in range(DEPTH):
                s = sig[l]
                users = used_by(mixer_items(l))
                own = [i for i, (who, _) in enumerate(users) if who == "DVE"]
                at = Place()

                def ada_item(partial):
                    i = own[at.item]
                    at.item += 1
                    dve.wait_ge(item_in[l][i % NITEM], 16 * (i // NITEM + 1))
                    wt = item_slot(i).rearrange("p (c n) -> p c n", c=DC)
                    acc = partial[:, mixer_items(l)[i][3], :]
                    do(ts(acc, wt[:, 0, :], silu_c[:, 0:1], None, ALU.mult))
                    for c in range(1, DC - 1):
                        do(stt(out=acc, in0=wt[:, c, :], scalar=silu_c[:, c:c + 1], in1=acc,
                               op0=ALU.mult, op1=ALU.add))
                    stt(out=acc, in0=wt[:, DC - 1, :], scalar=silu_c[:, DC - 1:DC], in1=acc,
                        op0=ALU.mult, op1=ALU.add).then_inc(s.ada_used.sem, 1)

                def keep_modulation(ml, third, bank, nth):
                    dve.wait_ge(*s.mod_summed.at(nth))
                    a, b = 16 * third, 16 * third + 16
                    do(tt(mod[:, ml, a:b], ps[:, bank, 0:16], row(ml, "b_ada")[:, a:b], ALU.add))

                def gains(n, scale, g):
                    return stt(out=gain[:, l, n, :], in0=modulation(l, scale), scalar=1.0, in1=row(l, g),
                               op0=ALU.add, op1=ALU.mult)

                def norm():
                    do(v.reciprocal(rstd[:, :], std[:, :]))
                    for p in range(4):
                        ins = tt(hT[:, 2 * p:2 * p + 2, :], xT[:, 2 * p:2 * p + 2, :],
                                 rstd[:, :].unsqueeze(1).to_broadcast([P, 2, T]), ALU.mult)
                        if p < 2:
                            ins.then_inc(s.scaled.sem, 1)
                        else:
                            mark(ins)

                def gain_and_shift(n, shift):
                    dve.wait_ge(*s.gain_ready.at(n))
                    sync()
                    for c in range(DC // 2, DC):
                        ts(hT[:, c, :], hT[:, c, :], gain[:, l, n - 1, c:c + 1], modulation(l, shift)[:, c:c + 1],
                           ALU.mult, ALU.add).then_inc(s.h_late_ready.sem, 1)

                summed = 0
                if l == 0:
                    dve.wait_ge(silu_c_ready, 1)
                    ada_item(partial_first)
                    ada_item(partial_first)
                dve.wait_ge(*s.x_ready.at(4))
                dve.wait_ge(*s.std_ready.at(1))
                norm()
                if l == 0:
                    ada_item(partial_first)
                    summed = 1
                    keep_modulation(0, 0, 2, summed)
                gains(0, SCALE1, "g_norm1").then_inc(s.gain_ready.sem, 1)
                gain_and_shift(1, SHIFT1)
                ada_item(partial_early)
                ada_item(partial_early)

                def rotate(dst, src, cos, sin, heads, half):
                    shape = [P, TC, heads, half]
                    cs, sn = cos.unsqueeze(2).to_broadcast(shape), sin.unsqueeze(2).to_broadcast(shape)
                    x1, x2 = src[:, :, :, 0:half], src[:, :, :, half:2 * half]
                    o1, o2 = dst[:, :, 0:heads, 0:half], dst[:, :, 0:heads, half:2 * half]
                    t1, t2 = tmp[:, :, 0:heads, 0:half], tmp[:, :, 0:heads, half:2 * half]
                    mark(tt(o1, x1, cs, ALU.mult))
                    mark(tt(o2, x2, cs, ALU.mult))
                    mark(tt(t1, x2, sn, ALU.mult))
                    mark(tt(t2, x1, sn, ALU.mult))
                    sync()
                    mark(tt(o1, o1, t1, ALU.subtract))
                    mark(tt(o2, o2, t2, ALU.add))
                    sync()

                dve.wait_ge(*s.block_kept.at(1))
                index = kvi[:, :, 2 * HD:2 * HD + (IH + 1) * ID].rearrange("p t (h d) -> p t h d", d=ID)
                iweight = kvi[:, :, N_KVI - IH:N_KVI]
                rotate(ir, index, cos_i, sin_i, IH + 1, ID // 2)
                v.tensor_copy(ir[:, :, IH + 1:IH + 4, :],
                              ir[:, :, IH:IH + 1, :].to_broadcast([P, TC, 3, ID])).then_inc(s.index_rotated.sem, 1)
                ada_item(partial_early)
                if l == 0:
                    dve.wait_ge(small_in, 16 * N_SMALL)
                dve.wait_ge(*s.block_kept.at(2))
                do(tt(tmp, qk, qk, ALU.mult))
                red(sumsq.rearrange("p (t h) -> p t h", t=TC), tmp, AX.X, ALU.add).then_inc(s.q_rms_ready.sem, 1)
                dve.wait_ge(*s.q_std_ready.at(1))
                do(v.reciprocal(rms, rms))
                do(tt(qk, qk, rms.rearrange("p (t h) -> p t h", t=TC).unsqueeze(3).to_broadcast(
                    [P, TC, HEADS + 1, HD]), ALU.mult))
                do(tt(qk, qk, qk_gain[:, l].unsqueeze(1).to_broadcast([P, TC, HEADS + 1, HD]), ALU.mult))
                rotate(qr, qk, cos_h, sin_h, HEADS + 1, HD // 2)
                v.tensor_copy(qr[:, :, HEADS + 1, :], qr[:, :, HEADS, :]).then_inc(s.q_rotated.sem, 1)
                ada_item(partial_early)

                def add_index(t, heads):
                    n = (t + 1) * P
                    acc = iscore[:, t, 0:n]
                    for h in heads:
                        at = (h % 4) * 2 + h // 4
                        if h == 0:
                            ins = ts(acc, scores[:, at, 0:n], iweight[:, t, h:h + 1], None, ALU.mult)
                        else:
                            ins = stt(out=acc, in0=scores[:, at, 0:n], scalar=iweight[:, t, h:h + 1], in1=acc,
                                      op0=ALU.mult, op1=ALU.add)
                        if h < IH - 1 or t > 0:
                            do(ins)
                        else:
                            ins.then_inc(s.index_read.sem, 1)
                            dve.wait_ge(*s.index_read.at(1))

                def select(t):
                    n = (t + 1) * P
                    work = iscore[:, t, 0:n]
                    do(stt(out=work, in0=work, scalar=ISCALE, in1=causal[:, t, 0:n], op0=ALU.mult, op1=ALU.add))
                    for _ in range(TOPK // 8):
                        do(v.max(out=top8, in_=work))
                        do(v.match_replace(out=work, in_to_replace=top8, in_values=work, imm_value=TAKEN))
                    do(ts(drop[:, t, 0:n], work, 0.5 * TAKEN, NEG, ALU.is_gt, ALU.mult))
                    do(tt(drop[:, t, 0:n], drop[:, t, 0:n], causal[:, t, 0:n], ALU.add))

                def mask(u):
                    t = 0 if u == 0 else 1
                    dve.wait_ge(*s.att_done.at(u + 1))
                    if u == 0:
                        dst, heads, n, i = scores0, HEADS, P, 0
                    else:
                        dst, heads, n, i = scores[:, 4 * (u - 1):4 * u, :], 4, T, HEADS + 4 * (u - 1)
                    stt(out=dst, in0=ps[:, 4:6, :].rearrange("p b (h s) -> p (b h) s", s=n), scalar=HD ** -0.5,
                        in1=drop[:, t, 0:n].unsqueeze(1).to_broadcast([P, heads, n]),
                        op0=ALU.mult, op1=ALU.add).then_inc(s.att_masked.sem, 1)
                    dve.wait_ge(*s.att_masked.at(u + 1))
                    red(rowmax[:, i:i + heads], dst, AX.X, ALU.max, negate=True).then_inc(s.att_max.sem, 1)

                at_tap = {}

                def convolve(a, b):
                    for tap in range(a, b):
                        for c in range(CC):
                            src, wt = pad[:, c, tap:tap + T], taps[:, l, tap, c:c + 1]
                            if tap == 0:
                                ins = ts(ca[:, c, :], src, wt, row(l, "conv_b")[:, c:c + 1], ALU.mult, ALU.add)
                            else:
                                dve.wait_ge(dve_step, at_tap[c])
                                ins = stt(out=ca[:, c, :], in0=src, scalar=wt, in1=ca[:, c, :],
                                          op0=ALU.mult, op1=ALU.add)
                            at_tap[c] = mark(ins)

                def normalise(t):
                    dve.wait_ge(*s.pv_done.at(t + 1))
                    do(v.reciprocal(rowinv[:, 8 * t:8 * t + 8], rowsum[:, 8 * t:8 * t + 8]))
                    units = 1 if t == 0 else 2
                    n = HEADS // units
                    for u in range(units):
                        out_v = ps[:, 4:6, :] if t == 0 else ps[:, 6 + u, :].rearrange("p (q s) -> p q s", q=2)
                        last = tt(attn[:, t, u * n:(u + 1) * n, :].rearrange("p (c q) d -> p q c d", q=2),
                                  out_v.rearrange("p q (c d) -> p q c d", d=P)[:, :, :, 0:HD],
                                  rowinv[:, 8 * t + u * n:8 * t + (u + 1) * n].rearrange("p (q c) -> p q c", q=2)
                                  .unsqueeze(3).to_broadcast([P, 2, n // 2, HD]), ALU.mult)
                        if u < units - 1:
                            mark(last)
                    last.then_inc(s.attn_ready.sem, 1)

                dve.wait_ge(*s.index_kept.at(1))
                add_index(0, range(IH))
                select(0)
                dve.wait_ge(*s.block_kept.at(4))
                dve.wait_ge(*s.pad_zero.at(1))
                mark(tt(pad[:, :, TAPS - 1:], ca, cb, ALU.mult))
                dve.wait_ge(*s.index_kept.at(2))
                add_index(1, range(IH))
                select(1)
                keep_modulation(l, 1, 6, summed + 1)
                mask(0)
                mask(1)
                convolve(0, 12)
                mask(2)
                convolve(12, 22)
                normalise(0)
                normalise(1)
                convolve(22, TAPS - 1)
                for c in range(CC):
                    dve.wait_ge(dve_step, at_tap[c])
                    src, wt = pad[:, c, TAPS - 1:], taps[:, l, TAPS - 1, c:c + 1]
                    ins = stt(out=ca[:, c, :], in0=src, scalar=wt, in1=ca[:, c, :], op0=ALU.mult, op1=ALU.add)
                    if c < CC - 1:
                        mark(ins)
                    else:
                        ins.then_inc(s.conv_ready.sem, 1)
                sync()

                ada_item(partial_late)
                dve.wait_ge(*s.mean_ready.at(1))
                dve.wait_ge(*s.conv_ready.at(1))
                stt(out=cb, in0=ps[:, 7, 0:T].unsqueeze(1).to_broadcast([P, CC, T]), scalar=-1.0 / CH, in1=ca,
                    op0=ALU.mult, op1=ALU.add).then_inc(s.centred.sem, 1)
                dve.wait_ge(*s.ln_std_ready.at(1))
                do(v.reciprocal(rstd[:, :], std[:, :]))
                tt(cb, cb, rstd[:, :].unsqueeze(1).to_broadcast([P, CC, T]), ALU.mult).then_inc(s.ln_ready.sem, 1)

                dve.wait_ge(*s.block_kept.at(len(BLOCKS)))
                for p in range(4):
                    if p < 3:
                        dve.wait_ge(*s.ya_done.at(p + 1))
                    else:
                        dve.wait_ge(*s.item_used.at(N_OUT - 1))
                    g = gates[:, 1, 2 * p:2 * p + 2, :]
                    tt(g, ps[:, p, :].rearrange("p (n t) -> p n t", t=T), g, ALU.mult).then_inc(s.ya_used.sem, 1)
                for p in range(4):
                    if p < 2:
                        ada_item(partial_late)
                    if p < 3:
                        dve.wait_ge(*s.yc_done.at(p + 1))
                    else:
                        dve.wait_ge(*s.item_used.at(N_OUT))
                    for n in range(2):
                        c = 2 * p + n
                        mark(stt(out=gates[:, 0, c, :], in0=ps[:, 4 + p, n * T:(n + 1) * T],
                                 scalar=row(l, "b_conv_out")[:, c:c + 1], in1=gates[:, 0, c, :],
                                 op0=ALU.add, op1=ALU.mult))
                    sync()
                    dve.wait_ge(*s.ya_used.at(p + 1))
                    tt(merged[:, 2 * p:2 * p + 2, :], gates[:, 0, 2 * p:2 * p + 2, :],
                       gates[:, 1, 2 * p:2 * p + 2, :], ALU.add).then_inc(s.merged_ready.sem, 1)
                ada_item(partial_late)
                if l + 1 < DEPTH:
                    ada_item(partial_next)
                    ada_item(partial_next)
                keep_modulation(l, 2, 4, summed + 2)
                gains(1, SCALE2, "g_norm2").then_inc(s.gain_ready.sem, 1)
                if l + 1 < DEPTH:
                    ada_item(partial_next)
                    ada_item(partial_next)
                for c in range(DC):
                    if c % 4 == 1 or c % 4 == 0:
                        dve.wait_ge(*s.out_done.at(c // 4 + 1))
                    else:
                        dve.wait_ge(*s.item_used.at(N_OUT + 1 + c // 4))
                    ins = stt(out=xT[:, c, :], in0=ps[:, c // 2, (c % 2) * T:(c % 2 + 1) * T],
                              scalar=modulation(l, GATE1)[:, c:c + 1], in1=xT[:, c, :], op0=ALU.mult, op1=ALU.add)
                    if c % 2:
                        ins.then_inc(s.x_ready.sem, 1)

                dve.wait_ge(*s.x_ready.at(8))
                dve.wait_ge(*s.std_ready.at(2))
                norm()
                gain_and_shift(2, SHIFT2)
                if l + 1 < DEPTH:
                    keep_modulation(l + 1, 0, 5, summed + 3)
                dve.wait_ge(*s.logits_done.at(1))
                W = GROUPS + NE
                do(tt(logits, ps[:, 4:7:2, 0:W],
                      b_route[:, l].unsqueeze(1).to_broadcast([P, TC, W]), ALU.add))
                g_log = logits[:, :, 0:GROUPS]

                def over(x, n):
                    return x.unsqueeze(2).to_broadcast([P, TC, n])

                def first_of(dst, eq, n, best):
                    do(tt(eq, eq, falling[:, 0:n].unsqueeze(1).to_broadcast([P, TC, n]), ALU.mult))
                    do(red(best, eq, AX.X, ALU.max))
                    return tt(dst, eq, over(best, n), ALU.is_equal)

                do(red(g_max, g_log, AX.X, ALU.max))
                tt(g_shift3, g_log, over(g_max, GROUPS), ALU.subtract).then_inc(s.group_shifted.sem, 1)
                do(tt(g_one, g_log, over(g_max, GROUPS), ALU.is_equal))
                do(first_of(g_one, g_one, GROUPS, best))
                do(ts(g_one, g_one, -1.0, -NEG, ALU.add, ALU.mult))
                do(tt(e_in.rearrange("p t (g e) -> p t g e", g=GROUPS),
                      logits[:, :, GROUPS:].rearrange("p t (g e) -> p t g e", g=GROUPS),
                      g_one.unsqueeze(3).to_broadcast([P, TC, GROUPS, EPG]), ALU.add))
                do(red(top_a, e_in, AX.X, ALU.max))
                do(tt(hot_a, e_in, over(top_a, NE), ALU.is_equal))
                do(first_of(hot_a, hot_a, NE, best))
                do(stt(out=e_in, in0=hot_a, scalar=2 * NEG, in1=e_in, op0=ALU.mult, op1=ALU.add))
                do(red(top_b, e_in, AX.X, ALU.max))
                do(tt(hot_b, e_in, over(top_b, NE), ALU.is_equal))
                do(first_of(hot_b, hot_b, NE, best))
                tt(member, hot_a, hot_b, ALU.add).then_inc(s.member_ready.sem, 1)
                tt(gap, top_b, top_a, ALU.subtract).then_inc(s.gap_ready.sem, 1)
                dve.wait_ge(*s.rank_done.at(1))
                counts = ps[:, 5, 2 * NE:3 * NE]
                do(v.tensor_copy(count_sb, counts))
                do(v.tensor_tensor_scan(start, ones[:, 0:NE], count_sb, 0.0, ALU.mult, ALU.add))
                do(tt(start, start, count_sb, ALU.subtract))
                do(tt(place, ps[:, 5, 0:2 * NE].rearrange("p (t e) -> p t e", t=TC),
                      start.unsqueeze(1).to_broadcast([P, TC, NE]), ALU.add))
                mark(tt(hot_a, hot_a, place, ALU.mult))
                mark(tt(hot_b, hot_b, place, ALU.mult))
                sync()
                mark(red(slot_a, hot_a, AX.X, ALU.add))
                mark(red(slot_b, hot_b, AX.X, ALU.add))
                sync()
                for t in range(TC):
                    do(ts(onehot[:, t, :], iota, slot_a[:, t:t + 1], None, ALU.is_equal))
                    stt(out=sorter[:, t, :], in0=iota, scalar=slot_b[:, t:t + 1], in1=onehot[:, t, :],
                        op0=ALU.is_equal, op1=ALU.add).then_inc(s.onehot_ready.sem, 1)
                for b in range(NBLK):
                    mark(ts(offs[0:1, l, b, :], start[0:1, :], float(b * BLK), float(PAIRS), ALU.add, ALU.min))
                do(red(best[0:1, 0:1], count_sb[0:1, :], AX.X, ALU.max))
                ts(flag[0:1, l:l + 1], best[0:1, 0:1], float(BLK), None, ALU.is_gt).then_inc(s.offs_ready.sem, 1)
                dve.wait_ge(*s.group_exp.at(1))
                dve.wait_ge(*s.offs_ready.at(1))
                do(red(best, g_exp3, AX.X, ALU.add))
                do(v.reciprocal(best, best))
                dve.wait_ge(*s.gap_exp.at(1))
                do(ts(weight_b, gap_exp, 1.0, None, ALU.add))
                do(v.reciprocal(weight_b, weight_b))
                do(tt(weight_a, best, weight_b, ALU.mult))
                do(tt(weight_b, weight_a, gap_exp, ALU.mult))
                for t in range(TC):
                    mark(ts(weighted[:, t, :], iota, slot_a[:, t:t + 1], weight_a[:, t:t + 1], ALU.is_equal, ALU.mult))
                    mark(ts(scratch[:, t, :], iota, slot_b[:, t:t + 1], weight_b[:, t:t + 1], ALU.is_equal, ALU.mult))
                    sync()
                    tt(weighted[:, t, :], weighted[:, t, :], scratch[:, t, :], ALU.add).then_inc(s.weighted_ready.sem, 1)

                def keep_spread():
                    dve.wait_ge(*s.spread_turned.at(1))
                    v.tensor_copy(spread.rearrange("p j t -> p (j t)"),
                                  ps[:, 6:8, :].rearrange("p b n -> p (b n)")).then_inc(s.spread_kept.sem, 1)

                def keep_rest(e, slot, b, half):
                    chunks = slice(4 * half, 4 * half + 4)
                    dve.wait_ge(*s.rounded_ready.at(e * 2 + half + 1))
                    for g in range(2):
                        ins = tt(gate_up_rest(slot)[:, g, chunks], gate_up_of(slot)[:, g, chunks], rounded[b][half][:, g],
                                 ALU.subtract)
                    ins.then_inc(s.rest_ready.sem, 1)

                keep_rest(0, 0, 0, 0)
                keep_rest(0, 0, 0, 1)

                dve.wait_ge(*s.offs_ready.at(1))
                big = dve.value_load(flag[0:1, l:l + 1], min_val=0, max_val=1)

                starts = offs[0:1, l].rearrange("q b e -> q (b e)")

                def gather(n, buffer, nth):
                    at = dve.value_load(starts[0:1, bass.ds(n, 1)], min_val=0, max_val=PAIRS)
                    block, x_block = sorted_x[:, :, bass.ds(at, BLK)], xe[:, buffer]
                    v.tensor_copy(x_block[:, :, 0, :], block).then_inc(s.xe_rounded.sem, 1)
                    dve.wait_ge(*s.xe_rounded.at(nth))
                    tt(x_block[:, :, 1, :], block, x_block[:, :, 0, :], ALU.subtract).then_inc(s.xe_ready.sem, 1)

                def product(n):
                    dve.wait_ge(*s.act_ready.at(n + 1))
                    tt(hid.rearrange("p f s -> p (f s)"), ps[:, 1, FC * P:2 * FC * P], act_g,
                       ALU.mult).then_inc(s.hid_ready.sem, 1)

                dve.wait_ge(*s.tail_zero.at(1))
                dve.wait_ge(*s.sorted_kept.at(DC))
                with dve.If(big == 0):
                    def step(e, j, ahead=True):
                        product(e)
                        if ahead:
                            dve.wait_ge(*s.gu_done.at(e + 1))
                            gather(e + 2, j % 2, e + 3)
                            keep_rest(e + 2, (j + 2) % NEXP, j % 2, 0)
                            keep_rest(e + 2, (j + 2) % NEXP, j % 2, 1)

                    for e in range(2):
                        gather(e, e, e + 1)
                    keep_rest(1, 1, 1, 0)
                    keep_rest(1, 1, 1, 1)
                    with dve.Fori(0, NE // NEXP - 1) as r:
                        for j in range(NEXP):
                            step(r * NEXP + j, j)
                    keep_spread()
                    for j in range(NEXP):
                        step(NE - NEXP + j, j, ahead=j < NEXP - 2)
                with dve.Else():
                    keep_spread()

                    def expert_slow(e, j, ahead=True):
                        for b in range(NBLK):
                            dve.wait_ge(*s.gu_done.at(e * NBLK + b + 1))
                            gather(e + b * NE, 0, e * NBLK + b + 1)
                            product(e * NBLK + b)
                        if ahead:
                            keep_rest(e + 1, (j + 1) % NEXP, 0, 0)
                            keep_rest(e + 1, (j + 1) % NEXP, 0, 1)

                    with dve.Fori(0, NE // NEXP - 1) as r:
                        for j in range(NEXP):
                            expert_slow(r * NEXP + j, j)
                    for j in range(NEXP):
                        expert_slow(NE - NEXP + j, j, ahead=j < NEXP - 1)

                for j in range(4):
                    dve.wait_ge(*s.made_turned.at(2 * j + 2))
                    v.tensor_copy(made_n[:, j, 512:D], ps[:, 5 + 2 * j % 4, :]).then_inc(s.made_kept_too.sem, 1)

                done = sig[l + 1].x_ready if l + 1 < DEPTH else s.x_ready
                for c in range(DC):
                    dve.wait_ge(*s.final_done.at(c // 2 + 1))
                    ins = stt(out=xT[:, c, :], in0=ps[:, c // 2, (c % 2) * T:(c % 2 + 1) * T],
                              scalar=modulation(l, GATE2)[:, c:c + 1], in1=xT[:, c, :], op0=ALU.mult, op1=ALU.add)
                    if c % 2:
                        ins.then_inc(done.sem, 1)


NAMES = ["x", "c", "w_ada", "b_ada", "g_norm1", "w_in", "q_norm_g", "k_norm_g", "conv_w", "conv_b", "conv_ln_g",
         "conv_ln_b", "w_conv_out", "b_conv_out", "w_attn_out", "w_out", "g_norm2", "w_group", "b_group",
         "w_router", "b_router", "w_gate", "w_up", "w_down"]


def shape_constants():
    import numpy as np

    f = np.float32
    table = np.zeros((P, N_CONST), f)
    i = np.arange(P)

    def put(name, value):
        table[:, CONST[name][0]:CONST[name][1]] = value

    put("ident", np.eye(P))
    put("ones", 1.0)
    put("before", i[:, None] < i[None, :])
    put("fold", i[:, None] % BLK == i[None, :] % BLK)
    token = np.arange(T).reshape(TC, P)
    later = np.arange(T)[None, None, :] > token.T[:, :, None]
    put("causal", np.where(later, f(NEG), f(0)).reshape(P, TC * T))
    put("iota", np.arange(PAIRS)[None, :])
    for tag, dim in (("h", HD), ("i", ID)):
        inv = f(10000.0) ** (-np.arange(0, dim, 2, dtype=f) / f(dim))
        ang = np.arange(T, dtype=f)[:, None] * inv.astype(f)[None, :]
        for name, fn in (("cos_", np.cos), ("sin_", np.sin)):
            put(name + tag, fn(ang).astype(f).reshape(TC, P, dim // 2).transpose(1, 0, 2).reshape(P, -1))
    put("falling", np.arange(NE, 0, -1)[None, :])
    put("eps", EPS)
    return table


def kernel(**inputs):
    import numpy as np
    import concourse.bacc as bacc
    from concourse.bass_utils import run_bass_kernel_spmd as run

    nc = bacc.Bacc("TRN2", target_bir_lowering=False, num_devices=1)
    arrays, w = {}, {}
    for name in NAMES:
        a = np.ascontiguousarray(inputs[name])
        arrays[f"in_{name}"] = a
        w[name] = nc.dram_tensor(f"in_{name}", a.shape, mybir.dt.from_np(a.dtype), kind="ExternalInput").ap()
    arrays["constants"] = shape_constants()
    constants = nc.dram_tensor("constants", (P, N_CONST), F32, kind="ExternalInput").ap()
    out = nc.dram_tensor("out", (1, T, D), F32, kind="ExternalOutput").ap()
    trunk_kernel(nc, w, constants, out)
    r = run(nc, [arrays], core_ids=[0])
    return r.results[0]["out"]
```
